# Optimizing a Trainium2 kernel written in Bass

```python
import math
import jax, jax.numpy as jnp
from jax import lax
import numpy as np

D_MODEL = 1024
BATCH = 1
SEQ = 256
DEPTH = 2

MOBA_HEADS = 8
HEAD_DIM = 64
MOBA_BLOCK = 256
MOBA_TOPK = 3
MOBA_Q_CHUNK = 16
MLA_HEADS = 8
MLA_Q_LORA = 384
MLA_KV_LORA = 256
MLA_NOPE = 64
MLA_ROPE = 32
MLA_V = 64
ROPE_THETA = 10000.0
DIFF_HEADS = 4
DIFF_QK = 64
DIFF_V = 2 * DIFF_QK
PLE_DIM = 256
Q_BLOCK = 128
NORM_EPS = 1e-5
NEG = -1e30

MOBA_W = MOBA_HEADS * HEAD_DIM
MLA_W = MLA_HEADS * MLA_V
DIFF_W = DIFF_HEADS * DIFF_V
DIFF_QK_W = DIFF_HEADS * 2 * DIFF_QK
IN_SIZES = (MOBA_W, MOBA_W, MOBA_W, MOBA_W,
            MLA_Q_LORA, MLA_KV_LORA, MLA_ROPE, MLA_W,
            DIFF_QK_W, DIFF_QK_W, DIFF_W, DIFF_W)
IN_WIDTH = sum(IN_SIZES)
N_BRANCH = 3
ALPHA = (2 * DEPTH) ** 0.25
BETA = (8 * DEPTH) ** -0.25


def _split_points():
    return [int(v) for v in np.cumsum(np.array(IN_SIZES))[:-1]]

def _alibi_slopes():
    n = MOBA_HEADS + DIFF_HEADS
    s = 2.0 ** (-8.0 * (np.arange(n) + 1) / n)
    diff_idx = np.arange(DIFF_HEADS) * (n // DIFF_HEADS)
    moba_idx = np.setdiff1d(np.arange(n), diff_idx)
    return (jnp.asarray(s[moba_idx], dtype=jnp.float32),
            jnp.asarray(s[diff_idx], dtype=jnp.float32))

def _rmsnorm(x, g, eps=1e-6):
    xf = x.astype(jnp.float32)
    y = xf * lax.rsqrt(jnp.mean(xf * xf, axis=-1, keepdims=True) + eps)
    return (y * g.astype(jnp.float32)).astype(x.dtype)

def _layernorm(x, g, b):
    xf = x.astype(jnp.float32)
    mu = jnp.mean(xf, axis=-1, keepdims=True)
    var = jnp.mean(jnp.square(xf - mu), axis=-1, keepdims=True)
    y = (xf - mu) * lax.rsqrt(var + NORM_EPS)
    return (y * g.astype(jnp.float32) + b.astype(jnp.float32)).astype(x.dtype)

def _rope(t, pos):
    d = t.shape[-1]
    freqs = ROPE_THETA ** (-jnp.arange(0, d, 2, dtype=jnp.float32) / d)
    ang = pos.astype(jnp.float32)[:, None] * freqs[None, :]
    cos, sin = jnp.cos(ang), jnp.sin(ang)
    tf = t.astype(jnp.float32)
    t1, t2 = tf[..., : d // 2], tf[..., d // 2:]
    return jnp.concatenate([t1 * cos - t2 * sin, t1 * sin + t2 * cos], axis=-1).astype(t.dtype)

def _split_heads(t, n):
    B, S, _ = t.shape
    return t.reshape(B, S, n, -1).transpose(0, 2, 1, 3)

def _merge_heads(t):
    B, H, S, d = t.shape
    return t.transpose(0, 2, 1, 3).reshape(B, S, H * d)

def moba_attention(q, k, v, slopes):
    B, H, S, dh = q.shape
    blk = MOBA_BLOCK
    nb = -(-S // blk)
    s_pad = nb * blk
    padw = ((0, 0), (0, 0), (0, s_pad - S), (0, 0))
    kp = jnp.pad(k, padw)
    vp = jnp.pad(v, padw)
    kb = kp.reshape(B, H, nb, blk, dh)
    vb = vp.reshape(B, H, nb, blk, dh)
    kmean = jnp.mean(kb.astype(jnp.float32), axis=3)
    pos = jnp.arange(S)
    gate = jnp.einsum('bhsd,bhnd->bhsn', q.astype(jnp.float32), kmean)
    past = jnp.arange(nb)[None, :] < (pos // blk)[:, None]
    gate = jnp.where(past, gate, -jnp.inf)
    kk = min(MOBA_TOPK, nb)
    _, sel = lax.top_k(gate, kk)

    C = MOBA_Q_CHUNK
    nc = S // C
    qc = q.reshape(B, H, nc, C, dh).transpose(2, 0, 1, 3, 4)
    selc = sel.reshape(B, H, nc, C, kk).transpose(2, 0, 1, 3, 4)
    bi = jnp.arange(B)[:, None, None, None]
    hi = jnp.arange(H)[None, :, None, None]
    scale = dh ** -0.5
    offs = jnp.arange(blk)

    def one(args):
        qi, si, c = args
        qpos = c * C + jnp.arange(C)
        ob = (c * C) // blk
        kg = kb[bi, hi, si]
        vg = vb[bi, hi, si]
        s_sel = jnp.einsum('bhqd,bhqjkd->bhqjk', qi, kg).astype(jnp.float32) * scale
        kpos_sel = si[..., None] * blk + offs
        dist_sel = (qpos[None, None, :, None, None] - kpos_sel).astype(jnp.float32)
        s_sel = s_sel - slopes[None, :, None, None, None] * dist_sel
        valid = jnp.arange(kk)[None, :] < (qpos // blk)[:, None]
        s_sel = jnp.where(valid[None, None, :, :, None], s_sel, NEG)
        ko = lax.dynamic_slice_in_dim(kp, ob * blk, blk, axis=2)
        vo = lax.dynamic_slice_in_dim(vp, ob * blk, blk, axis=2)
        dist_own = (qpos[:, None] - (ob * blk + offs)[None, :]).astype(jnp.float32)
        s_own = jnp.einsum('bhqd,bhkd->bhqk', qi, ko).astype(jnp.float32) * scale
        s_own = s_own - slopes[None, :, None, None] * dist_own
        s_own = jnp.where(dist_own >= 0, s_own, NEG)
        s_all = jnp.concatenate([s_sel.reshape(B, H, C, kk * blk), s_own], axis=-1)
        pr = jax.nn.softmax(s_all, axis=-1).astype(v.dtype)
        p_sel = pr[..., : kk * blk].reshape(B, H, C, kk, blk)
        p_own = pr[..., kk * blk:]
        return (jnp.einsum('bhqjk,bhqjkd->bhqd', p_sel, vg)
                + jnp.einsum('bhqk,bhkd->bhqd', p_own, vo))

    out = lax.map(one, (qc, selc, jnp.arange(nc)))
    return out.transpose(1, 2, 0, 3, 4).reshape(B, H, S, dh)

def mla_attention(q, k, v):
    B, H, S, dq = q.shape
    nq = S // Q_BLOCK
    scale = dq ** -0.5
    qb = q.reshape(B, H, nq, Q_BLOCK, dq).transpose(2, 0, 1, 3, 4)
    kpos = jnp.arange(S)

    def one(args):
        qi, i = args
        qpos = i * Q_BLOCK + jnp.arange(Q_BLOCK)
        s = jnp.einsum('bhqd,bhkd->bhqk', qi, k).astype(jnp.float32) * scale
        s = jnp.where(kpos[None, :] <= qpos[:, None], s, NEG)
        pr = jax.nn.softmax(s, axis=-1).astype(v.dtype)
        return jnp.einsum('bhqk,bhkd->bhqd', pr, v)

    out = lax.map(one, (qb, jnp.arange(nq)))
    return out.transpose(1, 2, 0, 3, 4).reshape(B, H, S, -1)

def diff_attention(q, k, v, slopes, lam):
    B, H, S = q.shape[:3]
    nq = S // Q_BLOCK
    scale = DIFF_QK ** -0.5
    qb = q.reshape(B, H, nq, Q_BLOCK, 2, DIFF_QK).transpose(2, 0, 1, 3, 4, 5)
    kpos = jnp.arange(S)

    def one(args):
        qi, i = args
        qpos = i * Q_BLOCK + jnp.arange(Q_BLOCK)
        dist = (qpos[:, None] - kpos[None, :]).astype(jnp.float32)
        s = jnp.einsum('bhqcd,bhkcd->bhcqk', qi, k).astype(jnp.float32) * scale
        s = s - slopes[None, :, None, None, None] * dist
        s = jnp.where(dist >= 0, s, NEG)
        pr = jax.nn.softmax(s, axis=-1)
        a = (pr[:, :, 0] - lam * pr[:, :, 1]).astype(v.dtype)
        return jnp.einsum('bhqk,bhkd->bhqd', a, v)

    out = lax.map(one, (qb, jnp.arange(nq)))
    return out.transpose(1, 2, 0, 3, 4).reshape(B, H, S, -1)

def _layer(x, p_i, li, w_in, gq, gkv, w_uq, w_ukv, lam_p, subln_g, w_a, w_b, w_c,
           w_m, b_m, w_o, ln_g, ln_b, w_pg, w_p, slopes_a, slopes_c):
    B, S, D = x.shape
    pos = jnp.arange(S)
    h = x @ w_in
    (a_q, a_k, a_v, a_z, b_cq, b_ckv, b_kr, b_z,
     c_q, c_k, c_v, c_z) = jnp.split(h, _split_points(), axis=-1)

    ya = moba_attention(_split_heads(a_q, MOBA_HEADS), _split_heads(a_k, MOBA_HEADS),
                        _split_heads(a_v, MOBA_HEADS), slopes_a)
    ya = _merge_heads(ya) * jax.nn.silu(a_z)

    cq = _rmsnorm(b_cq, gq)
    ckv = _rmsnorm(b_ckv, gkv)
    qh = _split_heads(cq @ w_uq, MLA_HEADS)
    q_b = jnp.concatenate([qh[..., :MLA_NOPE], _rope(qh[..., MLA_NOPE:], pos)], axis=-1)
    kvh = _split_heads(ckv @ w_ukv, MLA_HEADS)
    k_rope = _rope(b_kr[:, None], pos)
    k_b = jnp.concatenate([kvh[..., :MLA_NOPE],
                           jnp.broadcast_to(k_rope, (B, MLA_HEADS, S, MLA_ROPE))], axis=-1)
    yb = mla_attention(q_b, k_b, kvh[..., MLA_NOPE:])
    yb = _merge_heads(yb) * jax.nn.silu(b_z)

    lam_init = 0.8 - 0.6 * math.exp(-0.3 * li)
    lf = lam_p.astype(jnp.float32)
    lam = (jnp.exp(jnp.sum(lf[0] * lf[1])) - jnp.exp(jnp.sum(lf[2] * lf[3])) + lam_init)
    qc = c_q.reshape(B, S, DIFF_HEADS, 2, DIFF_QK).transpose(0, 2, 1, 3, 4)
    kc = c_k.reshape(B, S, DIFF_HEADS, 2, DIFF_QK).transpose(0, 2, 1, 3, 4)
    yc = diff_attention(qc, kc, _split_heads(c_v, DIFF_HEADS), slopes_c, lam)
    yc = _rmsnorm(yc, subln_g, eps=1e-5) * (1.0 - lam_init)
    yc = _merge_heads(yc) * jax.nn.silu(c_z)

    g = jax.nn.sigmoid(x @ w_m + b_m)
    ga, gb, gc = jnp.split(g, N_BRANCH, axis=-1)
    merged = ga * (ya @ w_a) + gb * (yb @ w_b) + gc * (yc @ w_c)
    out = merged @ w_o

    r = ALPHA * x + out
    r = r + jax.nn.sigmoid(r @ w_pg) * (p_i @ w_p)
    return _layernorm(r, ln_g, ln_b)

def first_inputs(seed: int = 0) -> dict:
    key = jax.random.key(seed)
    ks = jax.random.split(key, 20)
    f32 = jnp.float32

    def nrm(k, shape, scale):
        return jax.random.normal(k, shape, f32) * scale

    L, D = DEPTH, D_MODEL
    return {
        'x': nrm(ks[0], (BATCH, SEQ, D), 1.0),
        'p': nrm(ks[1], (L, BATCH, SEQ, PLE_DIM), 1.0),
        'w_in': nrm(ks[2], (L, D, IN_WIDTH), D ** -0.5),
        'mla_q_norm_g': 1.0 + nrm(ks[3], (L, MLA_Q_LORA), 0.01),
        'mla_kv_norm_g': 1.0 + nrm(ks[4], (L, MLA_KV_LORA), 0.01),
        'mla_w_uq': nrm(ks[5], (L, MLA_Q_LORA, MLA_HEADS * (MLA_NOPE + MLA_ROPE)), MLA_Q_LORA ** -0.5),
        'mla_w_ukv': nrm(ks[6], (L, MLA_KV_LORA, MLA_HEADS * (MLA_NOPE + MLA_V)), MLA_KV_LORA ** -0.5),
        'diff_lambda': nrm(ks[7], (L, 4, DIFF_QK), 0.1),
        'diff_subln_g': 1.0 + nrm(ks[8], (L, DIFF_V), 0.01),
        'w_branch_a': nrm(ks[9], (L, MOBA_W, D), BETA * MOBA_W ** -0.5),
        'w_branch_b': nrm(ks[10], (L, MLA_W, D), BETA * MLA_W ** -0.5),
        'w_branch_c': nrm(ks[11], (L, DIFF_W, D), BETA * DIFF_W ** -0.5),
        'w_merge': nrm(ks[12], (L, D, N_BRANCH * D), D ** -0.5),
        'b_merge': nrm(ks[13], (L, N_BRANCH * D), 0.01),
        'w_out': nrm(ks[14], (L, D, D), BETA * D ** -0.5),
        'ln_g': 1.0 + nrm(ks[15], (L, D), 0.01),
        'ln_b': nrm(ks[16], (L, D), 0.01),
        'w_ple_gate': nrm(ks[17], (L, D, D), D ** -0.5),
        'w_ple': nrm(ks[18], (L, PLE_DIM, D), BETA * PLE_DIM ** -0.5),
    }

def first_block(x, p, w_in, mla_q_norm_g, mla_kv_norm_g, mla_w_uq, mla_w_ukv, diff_lambda,
              diff_subln_g, w_branch_a, w_branch_b, w_branch_c, w_merge, b_merge, w_out,
              ln_g, ln_b, w_ple_gate, w_ple):
    slopes_a, slopes_c = _alibi_slopes()
    h = x
    for i in range(DEPTH):
        h = _layer(h, p[i], i, w_in[i], mla_q_norm_g[i], mla_kv_norm_g[i], mla_w_uq[i],
                   mla_w_ukv[i], diff_lambda[i], diff_subln_g[i], w_branch_a[i], w_branch_b[i],
                   w_branch_c[i], w_merge[i], b_merge[i], w_out[i], ln_g[i], ln_b[i],
                   w_ple_gate[i], w_ple[i], slopes_a, slopes_c)
    return h


CHUNK = 64
SB_BLOCK = 128
RET_HEADS = 4
RET_DIM = 128
SB_HEADS = 4
SB_DIM = 128
SSM_HEADS = 8
SSM_HEAD_DIM = 64
SSM_STATE = 128
SSM_GROUPS = 2
SSM_CONV = 4
D_FF = 2816
ROPE_BASE = 10000.0
NORM_EPS_2 = 1e-6
N_SUB = 3

RET_W = RET_HEADS * RET_DIM
SB_W = SB_HEADS * SB_DIM
SSM_W = SSM_HEADS * SSM_HEAD_DIM
MIX_W = RET_W + SB_W + SSM_W
SSM_XBC = SSM_W + 2 * SSM_GROUPS * SSM_STATE
IN_W = 4 * RET_W + 3 * SB_W + SSM_W + SSM_XBC + SSM_HEADS


def rmsnorm(x, gain):
    xf = x.astype(jnp.float32)
    y = xf * lax.rsqrt(jnp.mean(xf * xf, axis=-1, keepdims=True) + NORM_EPS_2)
    return (y * gain.astype(jnp.float32)).astype(x.dtype)

def modulate(h, shift, scale):
    return h * (1.0 + scale) + shift

def swiglu(u, wg, wu, wd):
    return (jax.nn.silu(u @ wg) * (u @ wu)) @ wd

def rope(x, pos):
    half = x.shape[-1] // 2
    inv_freq = ROPE_BASE ** (-jnp.arange(half, dtype=jnp.float32) / half)
    ang = pos[:, None] * inv_freq[None, :]
    cos = jnp.cos(ang)[None, :, None, :]
    sin = jnp.sin(ang)[None, :, None, :]
    x1 = x[..., :half].astype(jnp.float32)
    x2 = x[..., half:].astype(jnp.float32)
    return jnp.concatenate([x1 * cos - x2 * sin, x1 * sin + x2 * cos], axis=-1)

def retention(q, k, v, g, gn_gain):
    B, S, _ = q.shape
    nc = S // CHUNK
    H, Dh = RET_HEADS, RET_DIM
    pos = jnp.arange(S, dtype=jnp.float32)
    q = rope(q.reshape(B, S, H, Dh), pos)
    k = rope(k.reshape(B, S, H, Dh), pos) * (Dh ** -0.5)
    v = v.reshape(B, S, H, Dh).astype(jnp.float32)
    log_gamma = jnp.log1p(-(2.0 ** (-5.0 - jnp.arange(H, dtype=jnp.float32))))
    idx = jnp.arange(CHUNK, dtype=jnp.float32)
    dmat = jnp.exp(log_gamma[:, None, None] * jnp.abs(idx[:, None] - idx[None, :]))
    qc = q.reshape(B, nc, CHUNK, H, Dh)
    kc = k.reshape(B, nc, CHUNK, H, Dh)
    vc = v.reshape(B, nc, CHUNK, H, Dh)
    scores = jnp.einsum('bclhd,bcshd->bchls', qc, kc) * dmat[None, None]
    y_intra = jnp.einsum('bchls,bcshe->bclhe', scores, vc)
    k_decay = jnp.exp(log_gamma[:, None] * (CHUNK - 1 - idx)[None, :])
    kv = jnp.einsum('bcshd,hs,bcshe->bchde', kc, k_decay, vc).astype(jnp.float32)
    chunk_decay = jnp.exp(log_gamma * CHUNK)[None, :, None, None]

    def step(state, kv_c):
        return state * chunk_decay + kv_c, state

    _, s_prev = lax.scan(step, jnp.zeros((B, H, Dh, Dh), jnp.float32), jnp.moveaxis(kv, 1, 0))
    s_prev = jnp.moveaxis(s_prev, 0, 1)
    q_decay = jnp.exp(log_gamma[:, None] * (idx + 1.0)[None, :])
    y_cross = jnp.einsum('bclhd,hl,bchde->bclhe', qc, q_decay, s_prev)
    y = (y_intra + y_cross).reshape(B, S, H, Dh)
    y = rmsnorm(y, gn_gain.reshape(H, Dh)).reshape(B, S, RET_W)
    return y * jax.nn.silu(g.astype(jnp.float32))

def stick_breaking(q, k, v):
    B, S, _ = q.shape
    H, Dh = SB_HEADS, SB_DIM
    q = q.reshape(B, S, H, Dh).transpose(0, 2, 1, 3)
    k = k.reshape(B, S, H, Dh).transpose(0, 2, 1, 3)
    v = v.reshape(B, S, H, Dh).transpose(0, 2, 1, 3)
    scale = Dh ** -0.5
    outs = []
    for i in range(S // SB_BLOCK):
        q0 = i * SB_BLOCK
        kend = q0 + SB_BLOCK
        qb = q[:, :, q0:kend]
        kb = k[:, :, :kend]
        vb = v[:, :, :kend]
        z = jnp.einsum('bhtd,bhsd->bhts', qb, kb).astype(jnp.float32) * scale
        t_pos = q0 + jnp.arange(SB_BLOCK)
        s_pos = jnp.arange(kend)
        visible = s_pos[None, :] < t_pos[:, None]
        log_beta = jax.nn.log_sigmoid(z)
        log_keep = jnp.where(visible, jax.nn.log_sigmoid(-z), 0.0)
        tail = lax.cumsum(log_keep, axis=3, reverse=True) - log_keep
        w = jnp.where(visible, jnp.exp(log_beta + tail), 0.0)
        outs.append(jnp.einsum('bhts,bhsd->bhtd', w, vb.astype(jnp.float32)))
    y = jnp.concatenate(outs, axis=2)
    return y.transpose(0, 2, 1, 3).reshape(B, S, SB_W)

def mamba2(z, xbc, dt_raw, conv_w, conv_b, dt_bias, a_log, d_skip, norm_gain):
    B, S, _ = xbc.shape
    G, Hg, P, N = SSM_GROUPS, SSM_HEADS // SSM_GROUPS, SSM_HEAD_DIM, SSM_STATE
    nc = S // CHUNK
    xbc = lax.conv_general_dilated(
        xbc, conv_w[:, None, :], window_strides=(1,), padding=[(SSM_CONV - 1, 0)],
        dimension_numbers=('NWC', 'WIO', 'NWC'), feature_group_count=SSM_XBC) + conv_b
    xbc = jax.nn.silu(xbc).astype(jnp.float32)
    xs = xbc[..., :SSM_W].reshape(B, nc, CHUNK, G, Hg, P)
    bm = xbc[..., SSM_W:SSM_W + G * N].reshape(B, nc, CHUNK, G, N)
    cm = xbc[..., SSM_W + G * N:].reshape(B, nc, CHUNK, G, N)
    dt = jax.nn.softplus(dt_raw.astype(jnp.float32) + dt_bias).reshape(B, nc, CHUNK, G, Hg)
    a = -jnp.exp(a_log.astype(jnp.float32)).reshape(G, Hg)
    acum = jnp.cumsum(dt * a, axis=2)
    xdt = xs * dt[..., None]
    causal = jnp.tril(jnp.ones((CHUNK, CHUNK), dtype=bool))[None, None, :, :, None, None]
    seg = acum[:, :, :, None] - acum[:, :, None, :]
    decay = jnp.exp(jnp.where(causal, seg, -jnp.inf))
    cb = jnp.einsum('bclgn,bcsgn->bcgls', cm, bm)
    y_intra = jnp.einsum('bcgls,bclsgh,bcsghp->bclghp', cb, decay, xdt)
    decay_end = jnp.exp(acum[:, :, -1:] - acum)
    states = jnp.einsum('bcsgn,bcsgh,bcsghp->bcghpn', bm, decay_end, xdt)
    chunk_decay = jnp.exp(acum[:, :, -1])

    def step(h, inp):
        st, dec = inp
        return h * dec[..., None, None] + st, h

    _, h_prev = lax.scan(step, jnp.zeros((B, G, Hg, P, N), jnp.float32),
                         (jnp.moveaxis(states, 1, 0), jnp.moveaxis(chunk_decay, 1, 0)))
    h_prev = jnp.moveaxis(h_prev, 0, 1)
    y_inter = jnp.einsum('bclgn,bcghpn,bclgh->bclghp', cm, h_prev, jnp.exp(acum))
    y = y_intra + y_inter + xs * d_skip.astype(jnp.float32).reshape(G, Hg)[..., None]
    y = y.reshape(B, S, SSM_W)
    return rmsnorm(y * jax.nn.silu(z.astype(jnp.float32)), norm_gain)

def second_inputs(seed: int = 0) -> dict:
    key = jax.random.key(seed)
    ks = jax.random.split(key, 32)
    f32 = jnp.float32
    nrm = lambda k, shape, s: jax.random.normal(k, shape, f32) * s
    gain = lambda k, shape: 1.0 + 0.01 * jax.random.normal(k, shape, f32)
    dt0 = jnp.exp(jax.random.uniform(ks[11], (DEPTH, SSM_HEADS), f32, math.log(1e-3), math.log(1e-1)))
    return {
        "x": nrm(ks[0], (BATCH, SEQ, D_MODEL), 1.0),
        "c": nrm(ks[1], (BATCH, D_MODEL), 1.0),
        "ada_w": nrm(ks[2], (DEPTH, D_MODEL, 3 * N_SUB * D_MODEL), 0.1 * D_MODEL ** -0.5),
        "ada_b": nrm(ks[3], (DEPTH, 3 * N_SUB * D_MODEL), 0.01),
        "norm_ffn1": gain(ks[4], (DEPTH, D_MODEL)),
        "ffn1_wg": nrm(ks[5], (DEPTH, D_MODEL, D_FF), D_MODEL ** -0.5),
        "ffn1_wu": nrm(ks[6], (DEPTH, D_MODEL, D_FF), D_MODEL ** -0.5),
        "ffn1_wd": nrm(ks[7], (DEPTH, D_FF, D_MODEL), D_FF ** -0.5),
        "norm_mix": gain(ks[8], (DEPTH, D_MODEL)),
        "w_in": nrm(ks[9], (DEPTH, D_MODEL, IN_W), D_MODEL ** -0.5),
        "conv_w": nrm(ks[10], (DEPTH, SSM_CONV, SSM_XBC), SSM_CONV ** -0.5),
        "conv_b": nrm(ks[12], (DEPTH, SSM_XBC), 0.01),
        "dt_bias": dt0 + jnp.log(-jnp.expm1(-dt0)),
        "a_log": jnp.log(jax.random.uniform(ks[13], (DEPTH, SSM_HEADS), f32, 1.0, 16.0)),
        "d_skip": gain(ks[14], (DEPTH, SSM_HEADS)),
        "ret_gn": gain(ks[15], (DEPTH, RET_W)),
        "ssm_norm": gain(ks[16], (DEPTH, SSM_W)),
        "w_out": nrm(ks[17], (DEPTH, MIX_W, D_MODEL), MIX_W ** -0.5),
        "norm_ffn2": gain(ks[18], (DEPTH, D_MODEL)),
        "ffn2_wg": nrm(ks[19], (DEPTH, D_MODEL, D_FF), D_MODEL ** -0.5),
        "ffn2_wu": nrm(ks[20], (DEPTH, D_MODEL, D_FF), D_MODEL ** -0.5),
        "ffn2_wd": nrm(ks[21], (DEPTH, D_FF, D_MODEL), D_FF ** -0.5),
        "final_ada_w": nrm(ks[22], (D_MODEL, 2 * D_MODEL), 0.1 * D_MODEL ** -0.5),
        "final_ada_b": nrm(ks[23], (2 * D_MODEL,), 0.01),
        "final_norm": gain(ks[24], (D_MODEL,)),
    }

def second_block(x, c, ada_w, ada_b, norm_ffn1, ffn1_wg, ffn1_wu, ffn1_wd, norm_mix, w_in,
              conv_w, conv_b, dt_bias, a_log, d_skip, ret_gn, ssm_norm, w_out,
              norm_ffn2, ffn2_wg, ffn2_wu, ffn2_wd, final_ada_w, final_ada_b, final_norm):
    B, S, _ = x.shape
    cond = jax.nn.silu(c)
    splits = [RET_W, 2 * RET_W, 3 * RET_W, 4 * RET_W,
              4 * RET_W + SB_W, 4 * RET_W + 2 * SB_W, 4 * RET_W + 3 * SB_W,
              4 * RET_W + 3 * SB_W + SSM_W, 4 * RET_W + 3 * SB_W + SSM_W + SSM_XBC]
    h = x
    for l in range(DEPTH):
        mod = (cond @ ada_w[l] + ada_b[l]).reshape(B, 3 * N_SUB, D_MODEL)[:, None]
        u = modulate(rmsnorm(h, norm_ffn1[l]), mod[:, :, 0], mod[:, :, 1])
        h = h + 0.5 * (1.0 + mod[:, :, 2]) * swiglu(u, ffn1_wg[l], ffn1_wu[l], ffn1_wd[l])
        u = modulate(rmsnorm(h, norm_mix[l]), mod[:, :, 3], mod[:, :, 4])
        proj = u @ w_in[l]
        rq, rk, rv, rg, sq, sk, sv, mz, mxbc, mdt = jnp.split(proj, splits, axis=-1)
        y_ret = retention(rq, rk, rv, rg, ret_gn[l]).astype(x.dtype)
        y_sb = stick_breaking(sq, sk, sv).astype(x.dtype)
        y_ssm = mamba2(mz, mxbc, mdt, conv_w[l], conv_b[l], dt_bias[l], a_log[l],
                       d_skip[l], ssm_norm[l]).astype(x.dtype)
        mixed = jnp.concatenate([y_ret, y_sb, y_ssm], axis=-1) @ w_out[l]
        h = h + (1.0 + mod[:, :, 5]) * mixed
        u = modulate(rmsnorm(h, norm_ffn2[l]), mod[:, :, 6], mod[:, :, 7])
        h = h + 0.5 * (1.0 + mod[:, :, 8]) * swiglu(u, ffn2_wg[l], ffn2_wu[l], ffn2_wd[l])
    fmod = (cond @ final_ada_w + final_ada_b).reshape(B, 2, D_MODEL)[:, None]
    return modulate(rmsnorm(h, final_norm), fmod[:, :, 0], fmod[:, :, 1])


_first_inputs = second_inputs


def second_inputs(seed=0):
    import zlib

    import numpy as np

    out = dict(_first_inputs(seed))
    spreads = {}
    factors = {'norm_ffn1': 7.71,
     'norm_mix': 4.029,
     'conv_b': 50.656,
     'd_skip': 64.0,
     'ret_gn': 47.138,
     'ssm_norm': 64.0,
     'norm_ffn2': 30.16,
     'final_ada_b': 4.079,
     'final_norm': 32.273}
    for name, (base, spread) in spreads.items():
        noise = np.random.default_rng([zlib.crc32(name.encode()), seed]).standard_normal(out[name].shape)
        drawn = base * np.exp(spread * noise) if base else spread * noise
        out[name] = __import__('jax').numpy.asarray(drawn.astype(out[name].dtype))
    for name, factor in factors.items():
        out[name] = (out[name] * factor).astype(out[name].dtype)
    return out


_narrow_inputs = second_inputs


def second_inputs(seed=0):
    out = dict(_narrow_inputs(seed))
    wider = {'d_skip': 12.0, 'ret_gn': 3.94, 'ssm_norm': 7.75, 'norm_ffn2': 3.19, 'final_norm': 6.36}
    for name, times in wider.items():
        mean = out[name].mean()
        out[name] = (mean + times * (out[name] - mean)).astype(out[name].dtype)
    return out


def setup_inputs(seed=0):
    out = dict(first_inputs(seed))
    for name, value in second_inputs(seed + 1).items():
        if name != "x":
            out[name + "_2"] = value
    return out


def reference(
    x, p, w_in, mla_q_norm_g, mla_kv_norm_g, mla_w_uq, mla_w_ukv, diff_lambda, diff_subln_g,
    w_branch_a, w_branch_b, w_branch_c, w_merge, b_merge, w_out, ln_g, ln_b, w_ple_gate, w_ple,
    c_2, ada_w_2, ada_b_2, norm_ffn1_2, ffn1_wg_2, ffn1_wu_2, ffn1_wd_2, norm_mix_2, w_in_2,
    conv_w_2, conv_b_2, dt_bias_2, a_log_2, d_skip_2, ret_gn_2, ssm_norm_2, w_out_2,
    norm_ffn2_2, ffn2_wg_2, ffn2_wu_2, ffn2_wd_2, final_ada_w_2, final_ada_b_2, final_norm_2,
):
    x = first_block(
        x, p, w_in, mla_q_norm_g, mla_kv_norm_g, mla_w_uq, mla_w_ukv, diff_lambda, diff_subln_g,
        w_branch_a, w_branch_b, w_branch_c, w_merge, b_merge, w_out, ln_g, ln_b, w_ple_gate,
        w_ple,
    )
    return second_block(
        x, c_2, ada_w_2, ada_b_2, norm_ffn1_2, ffn1_wg_2, ffn1_wu_2, ffn1_wd_2, norm_mix_2,
        w_in_2, conv_w_2, conv_b_2, dt_bias_2, a_log_2, d_skip_2, ret_gn_2, ssm_norm_2, w_out_2,
        norm_ffn2_2, ffn2_wg_2, ffn2_wu_2, ffn2_wd_2, final_ada_w_2, final_ada_b_2,
        final_norm_2,
    )


_drawn_inputs = setup_inputs


def setup_inputs(seed=0):
    import zlib

    import numpy as np

    out = dict(_drawn_inputs(seed))
    spreads = {}
    factors = {'mla_q_norm_g': 8.0, 'mla_kv_norm_g': 8.0, 'diff_subln_g': 8.0, 'b_merge': 8.0}
    for name, (base, spread) in spreads.items():
        noise = np.random.default_rng([zlib.crc32(name.encode()), seed]).standard_normal(out[name].shape)
        drawn = base * np.exp(spread * noise) if base else spread * noise
        out[name] = __import__('jax').numpy.asarray(drawn.astype(out[name].dtype))
    for name, factor in factors.items():
        out[name] = (out[name] * factor).astype(out[name].dtype)
    return out
```

```python
from contextlib import ExitStack
import math

import numpy as np
import concourse.bass as bass
from concourse import mybir

F32 = mybir.dt.float32
ALU = mybir.AluOpType
ACT = mybir.ActivationFunctionType
AX = mybir.AxisListType

P = 128
T = 256
TB = T // P
D = 1024
DC = D // P
DEPTH = 2
TRI = 3 * P

HEADS, HD = 8, 64
Q_LORA, KV_LORA, NOPE, ROPE = 384, 256, 64, 32
DIFF_HEADS, DIFF_QK = 4, 64
PLE = 256
W = HEADS * HD
IN1 = dict(a_q=(0, 512), a_k=(512, 512), a_v=(1024, 512), a_z=(1536, 512), b_cq=(2048, 384),
           b_ckvr=(2432, 288), b_z=(2720, 512), c_q=(3232, 512), c_k=(3744, 512),
           c_v=(4256, 512), c_z=(4768, 512))
ALPHA = (2 * DEPTH) ** 0.25
NSLOPE = HEADS + DIFF_HEADS
SLOPES = 2.0 ** (-8.0 * (np.arange(NSLOPE) + 1) / NSLOPE)
DIFF_IDX = np.arange(DIFF_HEADS) * (NSLOPE // DIFF_HEADS)
DIFF_SLOPES = SLOPES[DIFF_IDX].astype(np.float32)
MOBA_SLOPES = SLOPES[np.setdiff1d(np.arange(NSLOPE), DIFF_IDX)].astype(np.float32)

RH, RD = 4, 128
SBH, SBD = 4, 128
MH, MP, MN, MG = 8, 64, 128, 2
TAPS = 4
FF = 2816
FC = FF // P
IN2 = dict(r_q=(0, 512), r_k=(512, 512), r_v=(1024, 512), r_g=(1536, 512), s_q=(2048, 512),
           s_k=(2560, 512), s_v=(3072, 512), m_z=(3584, 512), m_x=(4096, 512),
           m_bc=(4608, 512), m_dt=(5120, 8))
XBC = 1024
MIX = 1536
NMOD = 9

NEG = -1e30
SLOT = 4096
SLOTS = 3


def columns(sizes):
    at, out = 0, {}
    for name, n in sizes:
        out[name] = at
        at += n
    return out, at


CONST_SIZES = [("ident", P), ("ones", P), ("swap64", P), ("swap16", 32), ("dist", TRI), ("causal", TRI),
               ("cos32", 2 * T), ("sin32", 2 * T), ("cos128", 2 * T), ("sin128", 2 * T),
               ("decay", RH * TRI), ("before", TRI), ("before_neg", TRI), ("upto_min", P),
               ("le", P), ("gt", P), ("neg_ge", P), ("neg_ones", P)]
CONST_AT, CONST_N = columns(CONST_SIZES)

PER_LAYER = [("gq", 3), ("gkv", 2), ("subln", 1), ("b_merge", 24), ("ln_g", 8), ("ln_b", 8),
             ("ada_b", 72), ("norm_ffn1", 8), ("norm_mix", 8), ("norm_ffn2", 8), ("conv_w", 32),
             ("conv_b", 8), ("ret_gn", 4), ("ssm_norm", 4), ("d_skip", 4), ("dt_bias", 8),
             ("a_log", 8), ("lambda", 256)]
SMALL_SIZES = [(f"{n}{l}", s) for l in range(DEPTH) for n, s in PER_LAYER]
SMALL_SIZES += [("c", 8), ("final_ada_b", 16), ("final_norm", 8)]
SMALL_AT, SMALL_N = columns(SMALL_SIZES)


class Engine:

    def __init__(self, queue, semaphore):
        self.queue, self.semaphore, self.count, self.waited = queue, semaphore, 0, {}

    def done(self, instruction):
        instruction.then_inc(self.semaphore, 1)
        self.count += 1
        return (self.semaphore, self.count)

    def settle(self):
        if self.count:
            self.wait((self.semaphore, self.count))

    def wait(self, *marks):
        for mark in marks:
            if mark is None:
                continue
            if isinstance(mark, list):
                self.wait(*mark)
                continue
            semaphore, value = mark
            if self.waited.get(semaphore.name, 0) < value:
                self.queue.wait_ge(semaphore, value)
                self.waited[semaphore.name] = value


class Buffer:

    def __init__(self, tile):
        self.tile, self.free = tile, None


class Filler:

    def __init__(self, steps):
        self.steps, self.passed = steps, set()

    def step(self):
        for point in self.steps:
            if point is None:
                return True
            self.passed.add(point)
        return False

    def until(self, point):
        while point not in self.passed:
            if not self.step():
                assert point in self.passed


class Turn:

    def __init__(self, tiles):
        self.buffers, self.at = [Buffer(t) for t in tiles], 0

    def take(self):
        self.at += 1
        return self.buffers[(self.at - 1) % len(self.buffers)]


def build(nc, a, out):
    with ExitStack() as whole:
        Program(nc, a, out, whole)


class Program:
    def __init__(self, nc, a, out, whole):
        self.nc, self.a = nc, a
        sb = lambda name, shape: whole.enter_context(nc.sbuf_tensor(name, shape, F32))
        sem = lambda name: whole.enter_context(nc.semaphore(name))
        self.pe = Engine(nc.tensor, sem("pe_marks"))
        self.dve = Engine(nc.vector, sem("dve_marks"))
        self.act = Engine(nc.scalar, sem("act_marks"))
        self.pool = Engine(nc.gpsimd, sem("pool_marks"))
        self.sp = Engine(nc.sync, sem("sp_marks"))
        banks = [whole.enter_context(nc.psum_tensor(f"bank{i}", [P, 512], F32)) for i in range(8)]
        self.products = Turn(banks[0:3])
        self.scores = Turn(banks[3:5])
        self.turned = Turn(banks[5:7])
        self.values = Turn(banks[7:8])
        self.slots = Turn([sb(f"weights{i}", [P, SLOT]) for i in range(SLOTS)])
        for i, s in enumerate(self.slots.buffers):
            s.semaphore, s.loads = sem(f"weights{i}_loaded"), 0

        self.const = sb("constants", [P, CONST_N])
        self.small = sb("small_parameters", [P, SMALL_N])
        self.h = sb("h", [P, DC, T])
        loaded = sem("loaded_once")
        nc.sync.dma_start(self.h[:, :, :], a["x"].rearrange("(c p) t -> p c t", p=P)).then_inc(loaded, 16)
        nc.sync.dma_start(self.small[:, :], a["small"]).then_inc(loaded, 16)
        nc.sync.dma_start(self.const[:, :], a["constants"]).then_inc(loaded, 16)
        self.loaded = (loaded, 48)
        for e in (self.pe, self.dve, self.act, self.pool):
            e.wait(self.loaded)
        self.h_ready = None

        self.stats = Turn([sb(f"statistics{i}", [P, 3, 8]) for i in range(2)])
        self.zero = self.k("ident", 0)

        self.mods = sb("modulations", [P, DEPTH * 72 + 16])
        self.mod_sum = Turn([sb(f"mod_sum{i}", [P, 512]) for i in range(1)])
        self.cond = sb("cond", [P, DC])
        self.cond_ready = self.act.done(nc.scalar.activation(self.cond[:, :], self.s("c", 8), ACT.Silu))
        self.mod_ready = {}
        self.mod_todo = [("ada_w", l, j) for l in range(DEPTH) for j in range(18)]
        self.mod_todo += [("final_ada_w", DEPTH, j) for j in range(4)]
        self.since_mod = 0

        with ExitStack() as stack:
            self.first_stack(stack)
        with ExitStack() as stack:
            self.second_stack(stack, out)

    def k(self, name, i=None, n=None):
        at = CONST_AT[name] + (i or 0)
        size = n if n is not None else (1 if i is not None else dict(CONST_SIZES)[name])
        return self.const[:, at:at + size]

    def s(self, name, n=1, i=0):
        at = SMALL_AT[name] + i
        return self.small[:, at:at + n]

    def load(self, source, rows, cols):
        slot = self.slots.take()
        kc = rows // P
        self.sp.wait(slot.free)
        view = slot.tile[:, 0:kc * cols].rearrange("p (k n) -> p k n", k=kc)
        self.nc.sync.dma_start(view, source.rearrange("(k p) n -> p k n", p=P)).then_inc(slot.semaphore, 16)
        slot.loads += 1
        slot.view, slot.loaded = view, (slot.semaphore, 16 * slot.loads)
        return slot

    def product(self, out, pairs, start=True, stop=True, **more):
        for i, (lhsT, rhs) in enumerate(pairs):
            last = self.nc.tensor.matmul(out, lhsT, rhs, start=start and i == 0,
                                         stop=stop and i == len(pairs) - 1, **more)
        return last

    def dense(self, source, rows, cols, x, x_ready, evacuate, width=P):
        kc = rows // P
        slot = self.load(source, rows, cols)
        blocks = -(-cols // width)
        self.pe.wait(slot.loaded)
        for b in range(0, blocks, 2):
            bank = self.products.take()
            self.pe.wait(bank.free)
            n = min(2, blocks - b)
            for j in range(n):
                for k in range(kc):
                    if b == 0 and j == 0 and x_ready is not None:
                        self.pe.wait(x_ready[k] if isinstance(x_ready, list) else x_ready)
                    last = self.nc.tensor.matmul(
                        bank.tile[:, j * T:(j + 1) * T],
                        slot.view[:, k, (b + j) * width:(b + j + 1) * width], x[:, k, :],
                        start=k == 0, stop=k == kc - 1)
            mark = self.pe.done(last)
            slot.free = mark
            bank.free = evacuate(bank.tile, b, n, mark)
            yield
        self.count_panel()

    def token_major(self, source, rows, cols, x, x_ready, evacuate):
        kc = rows // P
        slot = self.load(source, rows, cols)
        self.pe.wait(slot.loaded, x_ready)
        for b in range(TB):
            bank = self.products.take()
            self.pe.wait(bank.free)
            last = self.product(bank.tile[:, 0:cols],
                                [(x[:, k, b * P:(b + 1) * P], slot.view[:, k, :]) for k in range(kc)])
            mark = self.pe.done(last)
            slot.free = mark
            bank.free = evacuate(bank.tile, b, mark)
            yield
        self.count_panel()

    def count_panel(self):
        self.since_mod += 1
        if self.since_mod >= self.mod_every:
            self.since_mod = 0
            self.mod_step()

    def mod_step(self):
        if not self.mod_todo:
            return
        name, l, j = self.mod_todo.pop(0)
        nc = self.nc
        source = self.a[name][l] if l < DEPTH else self.a[name]
        slot = self.load(source[:, j * 512:(j + 1) * 512], D, 512)
        total = self.mod_sum.take()
        self.dve.wait(slot.loaded, self.cond_ready, total.free)
        mark = self.dve.done(nc.vector.tensor_scalar(
            total.tile[:, :], slot.view[:, 0, :], self.cond[:, 0:1], None, ALU.mult))
        for k in range(1, DC):
            self.dve.wait(mark)
            mark = self.dve.done(nc.vector.scalar_tensor_tensor(
                total.tile[:, :], slot.view[:, k, :], self.cond[:, k:k + 1], total.tile[:, :],
                ALU.mult, ALU.add))
        slot.free = mark
        bank = self.turned.take()
        self.pe.wait(mark, bank.free)
        for i in range(4):
            last = nc.tensor.matmul(bank.tile[:, i:i + 1], total.tile[:, i * P:(i + 1) * P],
                                    self.k("ones", 0), start=True, stop=True)
        mark = self.pe.done(last)
        total.free = mark
        at = l * 72 + 4 * j
        bias = self.s(f"ada_b{l}", 4, 4 * j) if l < DEPTH else self.s("final_ada_b", 4, 4 * j)
        self.dve.wait(mark)
        bank.free = self.mod_last = self.dve.done(nc.vector.tensor_tensor(
            self.mods[:, at:at + 4], bank.tile[:, 0:4], bias, ALU.add))

    def finish_mods(self, left):
        while len(self.mod_todo) > left:
            self.mod_step()

    def inverse_rms(self, squares, groups, per_group, count, eps, ready):
        nc, pe, dve, act = self.nc, self.pe, self.dve, self.act
        n = groups * TB
        sums = self.turned.take()
        pe.wait(sums.free, ready)
        for g in range(groups):
            for b in range(TB):
                last = self.product(
                    sums.tile[:, g * TB + b:g * TB + b + 1],
                    [(squares[:, g * per_group + k, b * P:(b + 1) * P], self.k("ones", 0))
                     for k in range(per_group)])
        mark = pe.done(last)
        st = self.stats.take()
        mean, inv, tmp = st.tile[:, 0, 0:n], st.tile[:, 1, 0:n], st.tile[:, 2, 0:n]
        dve.wait(mark, st.free)
        sums.free = mark = dve.done(nc.vector.tensor_scalar(mean, sums.tile[:, 0:n], 1.0 / count, eps,
                                                            ALU.mult, ALU.add))
        act.wait(mark)
        mark = act.done(nc.scalar.activation(tmp, mean, ACT.Sqrt))
        dve.wait(mark)
        dve.wait(dve.done(nc.vector.reciprocal(inv, tmp)))
        dve.wait(dve.done(nc.vector.tensor_tensor(tmp, mean, inv, ALU.mult)))
        dve.wait(dve.done(nc.vector.tensor_tensor(tmp, tmp, inv, ALU.mult)))
        dve.wait(dve.done(nc.vector.tensor_scalar(tmp, tmp, -0.5, 1.5, ALU.mult, ALU.add)))
        mark = dve.done(nc.vector.tensor_tensor(inv, inv, tmp, ALU.mult))
        pe.wait(mark)
        return self.broadcast(st, inv, groups)

    def broadcast(self, st, columns_, groups):
        banks = []
        for g in range(groups):
            if g % 2 == 0:
                bank = self.scores.take()
                self.pe.wait(bank.free)
                banks.append(bank)
            for b in range(TB):
                i = g * TB + b
                last = self.nc.tensor.matmul(
                    bank.tile[:, (g % 2) * T + b * P:(g % 2) * T + (b + 1) * P],
                    columns_[:, i:i + 1].to_broadcast([P, P]), self.k("ident"), start=True, stop=True)
            bank.ready = self.pe.done(last)
        st.free = bank.ready
        return banks

    def square(self, out, in_, ready):
        self.pool.wait(ready)
        self.pool.settle()
        return self.pool.done(self.nc.gpsimd.tensor_tensor(out, in_, in_, ALU.mult))

    def pipeline(self, units, filler):
        active, units = [], list(units)
        while active or units:
            if units:
                active.append(units.pop(0))
            active = [u for u in active if next(u, "ended") != "ended"]
            filler.step()

    def softmax(self, raw, raw_ready, buf, bias_op):
        nc, dve, act = self.nc, self.dve, self.act
        st = buf.stat
        dve.wait(raw_ready, buf.free)
        mark = dve.done(bias_op(buf.tile))
        raw.free = mark
        dve.wait(mark)
        parts = ((0, P), (P, TRI))
        for i, (lo, hi) in enumerate(parts):
            mark = dve.done(nc.vector.tensor_reduce(st[:, i:i + 1], buf.tile[:, lo:hi], AX.X, ALU.max,
                                                    negate=True))
        act.wait(mark)
        for i, (lo, hi) in enumerate(parts):
            mark = act.done(nc.scalar.activation(buf.tile[:, lo:hi], buf.tile[:, lo:hi], ACT.Exp,
                                                 bias=st[:, i:i + 1], accum_out=st[:, 2 + i:3 + i]))
        dve.wait(mark)
        mark = dve.done(nc.vector.reciprocal(st[:, 4:6], st[:, 2:4]))
        dve.wait(mark)
        return parts

    def transpose_map(self, probs, ready):
        nc = self.nc
        bank = self.turned.take()
        self.pe.wait(ready, bank.free)
        for i in range(3):
            last = nc.tensor.transpose(bank.tile[:, i * P:(i + 1) * P],
                                       probs.tile[:, i * P:(i + 1) * P], self.k("ident"))
        probs.free = mark = self.pe.done(last)
        pt = self.maps_t.take()
        self.act.wait(mark, pt.free)
        bank.free = pt.ready = self.act.done(nc.scalar.copy(pt.tile[:, :], bank.tile[:, 0:TRI]))
        return pt

    def weigh_values(self, out, v, cols, pt):
        nc = self.nc
        self.pe.wait(pt.ready)
        nc.tensor.matmul(out, v[:, 0, cols], pt.tile[:, 0:T], start=True, stop=False)
        pt.free = mark = self.pe.done(nc.tensor.matmul(
            out[:, P:T], v[:, 1, cols], pt.tile[:, T:TRI], start=False, stop=True))
        return mark

    def rows_of(self, name, l):
        return self.a[name][l]

    def copy_to(self, dst, name, scale=1.0):
        def evacuate(tile, b, n, mark):
            self.act.wait(mark, self.reuse.get(name))
            if n == 2:
                got = self.act.done(self.nc.scalar.activation(
                    dst[:, b:b + 2, :], tile[:, :].rearrange("p (j t) -> p j t", j=2), ACT.Copy, scale=scale))
            else:
                got = self.act.done(self.nc.scalar.activation(dst[:, b, :], tile[:, 0:T], ACT.Copy, scale=scale))
            self.ready[name] = got
            return got
        return evacuate

    def function_to(self, dst, name, func, bias=None):
        def evacuate(tile, b, n, mark):
            self.act.wait(mark, self.reuse.get(name))
            if bias is None:
                got = self.act.done(self.nc.scalar.activation(
                    dst[:, b:b + 2, :], tile[:, :].rearrange("p (j t) -> p j t", j=2), func))
            else:
                for j in range(n):
                    got = self.act.done(self.nc.scalar.activation(
                        dst[:, b + j, :], tile[:, j * T:(j + 1) * T], func, bias=bias(b + j)))
            self.ready[name] = got
            return got
        return evacuate

    def tokens_to(self, dst, name):
        def evacuate(tile, b, mark):
            self.act.wait(mark, self.reuse.get(name))
            self.ready[name] = self.act.done(self.nc.scalar.copy(dst[:, b, :], tile[:, :]))
            return self.ready[name]
        return evacuate

    def first_stack(self, stack):
        nc = self.nc
        sb = lambda name, shape: stack.enter_context(nc.sbuf_tensor(name, shape, F32))
        self.ready, self.reuse = {}, {}
        self.mod_every = 3
        b = self.b = {}
        for n in ("a_q", "a_k", "c_q", "c_k", "a_z", "b_z", "c_z"):
            b[n] = sb(n, [P, 4, T])
        for n in ("a_v", "b_v", "c_v"):
            b[n] = sb(n, [P, TB, W])
        b["cq"], b["ckv"] = sb("cq", [P, 3, T]), sb("ckv", [P, 2, T])
        b["kr"] = sb("kr", [P, T])
        b["b_q"], b["b_k"] = sb("b_q", [P, HEADS, T]), sb("b_k", [P, HEADS, T])
        b["gates"] = sb("gates", [P, 3 * DC, T])
        b["pT"] = sb("pT", [P, PLE // P, T])
        b["tmp"] = sb("tmp", [P, 2 * T])
        maps = [sb(f"map{i}", [P, TRI]) for i in range(4)]
        self.maps = Turn(maps)
        for i, m in enumerate(self.maps.buffers):
            m.stat = sb(f"map_stat{i}", [P, 8])
        self.maps_t = Turn([sb(f"map_t{i}", [P, TRI]) for i in range(2)])
        b["lam"] = sb("lam", [P, 8])
        b["lam_prod"] = sb("lam_prod", [P, 2, DIFF_QK])
        self.p_sem = stack.enter_context(nc.semaphore("p_loaded"))
        for l in range(DEPTH):
            self.first_layer(l)
        self.finish_mods(22)

    def first_layer(self, l):
        nc, b, pe, dve, act, pool = self.nc, self.b, self.pe, self.dve, self.act, self.pool
        ready, x = self.ready, self.h
        w_in = self.a["w_in"][l]
        part = lambda n: w_in[:, IN1[n][0]:IN1[n][0] + IN1[n][1]]

        self.sp.wait(self.reuse.get("pT"))
        nc.sync.dma_start(b["pT"][:, :, :], self.a["p"][l].rearrange("(c p) t -> p c t", p=P)).then_inc(self.p_sem, 16)
        p_loaded = (self.p_sem, 16 * (l + 1))

        lam_init = 0.8 - 0.6 * math.exp(-0.3 * l)
        lam, prod = b["lam"], b["lam_prod"]
        lf = self.s(f"lambda{l}", 256).rearrange("p (a b d) -> p a b d", a=2, b=2)
        dve.wait(dve.done(nc.vector.tensor_tensor(prod[:, :, :], lf[:, :, 0, :], lf[:, :, 1, :], ALU.mult)))
        mark = dve.done(nc.vector.tensor_reduce(lam[:, 0:2], prod[:, :, :], AX.X, ALU.add))
        act.wait(mark)
        mark = act.done(nc.scalar.activation(lam[:, 2:4], lam[:, 0:2], ACT.Exp))
        dve.wait(mark)
        dve.wait(dve.done(nc.vector.scalar_tensor_tensor(lam[:, 4:5], lam[:, 3:4], -lam_init, lam[:, 2:3],
                                                         ALU.add, ALU.subtract)))
        mark = dve.done(nc.vector.tensor_scalar(lam[:, 5:6], self.s(f"subln{l}"), 1.0 - lam_init, None, ALU.mult))
        dve.wait(mark)
        neg_lam, subln = lam[:, 4:5], lam[:, 5:6]

        def run(g):
            for _ in g:
                pass
        run(self.dense(part("b_cq"), D, Q_LORA, x, self.h_ready, self.copy_to(b["cq"], "cq")))

        def ckvr(tile, blk, n, mark):
            return self.copy_to(b["ckv"], "ckv")(tile, blk, n, mark)
        slot = self.load(part("b_ckvr"), D, 288)
        pe.wait(slot.loaded)
        bank = self.products.take()
        pe.wait(bank.free)
        for j in range(2):
            last = self.product(bank.tile[:, j * T:(j + 1) * T],
                                [(slot.view[:, k, j * P:(j + 1) * P], x[:, k, :]) for k in range(DC)])
        bank.free = ckvr(bank.tile, 0, 2, pe.done(last))
        bank = self.products.take()
        pe.wait(bank.free)
        last = self.product(bank.tile[64:96, 0:T],
                            [(slot.view[:, k, 256:288], x[:, k, :]) for k in range(DC)])
        slot.free = mark = pe.done(last)
        act.wait(mark)
        bank.free = ready["kr"] = act.done(nc.scalar.copy(b["kr"][64:96, :], bank.tile[64:96, 0:T]))
        self.count_panel()

        run(self.dense(part("a_q"), D, W, x, None, self.copy_to(b["a_q"], "a_q", HD ** -0.5)))
        run(self.dense(part("a_k"), D, W, x, None, self.copy_to(b["a_k"], "a_k")))
        sq_q = self.square(b["b_q"][:, 0:3, :], b["cq"][:, :, :], [ready["cq"], self.reuse.get("b_q")])
        sq_kv = self.square(b["b_k"][:, 0:2, :], b["ckv"][:, :, :], [ready["ckv"], self.reuse.get("b_k")])
        run(self.token_major(part("a_v"), D, W, x, None, self.tokens_to(b["a_v"], "a_v")))

        def latent_norm(buf, chunks, gain, squares, sq_mark):
            (bank,) = self.inverse_rms(squares, 1, chunks, chunks * P, 1e-6, sq_mark)
            dve.wait(bank.ready)
            for c in range(chunks):
                mark = dve.done(nc.vector.scalar_tensor_tensor(
                    buf[:, c, :], buf[:, c, :], self.s(f"{gain}{l}", 1, c), bank.tile[:, 0:T], ALU.mult, ALU.mult))
            bank.free = mark
            return mark
        ready["cqn"] = latent_norm(b["cq"], 3, "gq", b["b_q"], sq_q)
        ready["ckvn"] = latent_norm(b["ckv"], 2, "gkv", b["b_k"], sq_kv)

        def rope32(raw, heads, mark):
            bank = self.products.take()
            pe.wait(mark, bank.free)
            rows = slice(64, 96)
            n = heads * T
            mark = pe.done(nc.tensor.matmul(bank.tile[rows, 0:n], self.k("swap16")[rows, :], raw,
                                            start=True, stop=True))
            dve.wait(mark, self.reuse.get("tmp"))
            tmp = b["tmp"][rows, 0:n]
            flat = raw.rearrange("p h t -> p (h t)") if heads == 2 else raw
            bank.free = m = dve.done(nc.vector.tensor_tensor(tmp, bank.tile[rows, 0:n], self.k("sin32")[rows, 0:n], ALU.mult))
            m2 = dve.done(nc.vector.tensor_tensor(flat, flat, self.k("cos32")[rows, 0:n], ALU.mult))
            dve.wait(m2)
            return dve.done(nc.vector.tensor_tensor(flat, flat, tmp, ALU.add))

        def mla_q():
            slot = self.load(self.a["mla_w_uq"][l], Q_LORA, 768)
            pe.wait(slot.loaded, ready["cqn"])
            for h in range(0, HEADS, 2):
                bank = self.products.take()
                pe.wait(bank.free)
                for j in range(2):
                    last = self.product(bank.tile[0:96, j * T:(j + 1) * T],
                                        [(slot.view[:, k, (h + j) * 96:(h + j + 1) * 96], b["cq"][:, k, :])
                                         for k in range(3)])
                slot.free = mark = pe.done(last)
                act.wait(mark)
                bank.free = mark = act.done(nc.scalar.copy(
                    b["b_q"][0:96, h:h + 2, :], bank.tile[0:96, :].rearrange("p (j t) -> p j t", j=2)))
                ready["b_q"] = rope32(b["b_q"][64:96, h:h + 2, :], 2, mark)
                yield
            self.count_panel()

        def mla_kv():
            mark = rope32(b["kr"][64:96, :], 1, ready["kr"])
            slot = self.load(self.a["mla_w_ukv"][l], KV_LORA, 1024)
            by_head = slot.view.rearrange("p k (h c) -> p k h c", h=HEADS)
            pool.wait(mark, ready["ckvn"])
            for h in range(HEADS):
                pool.settle()
                ready["b_k_rope"] = pool.done(nc.gpsimd.tensor_copy(b["b_k"][64:96, h, :], b["kr"][64:96, :]))
            pe.wait(slot.loaded, ready["ckvn"])
            for h in range(0, HEADS, 2):
                bank = self.products.take()
                pe.wait(bank.free)
                for j in range(2):
                    last = self.product(bank.tile[0:64, j * T:(j + 1) * T],
                                        [(by_head[:, k, h + j, 0:NOPE], b["ckv"][:, k, :]) for k in range(2)])
                mark = pe.done(last)
                act.wait(mark)
                bank.free = ready["b_k"] = act.done(nc.scalar.copy(
                    b["b_k"][0:64, h:h + 2, :], bank.tile[0:64, :].rearrange("p (j t) -> p j t", j=2)))
                if h % 4 == 2:
                    yield
            for t in range(TB):
                bank = self.products.take()
                pe.wait(bank.free)
                last = self.product(bank.tile[:, :].rearrange("p (h c) -> p h c", h=HEADS),
                                    [(b["ckv"][:, k, t * P:(t + 1) * P], by_head[:, k, :, NOPE:128])
                                     for k in range(2)])
                slot.free = mark = pe.done(last)
                act.wait(mark, self.reuse.get("b_v"))
                bank.free = ready["b_v"] = act.done(nc.scalar.copy(b["b_v"][:, t, :], bank.tile[:, :]))
            self.count_panel()
            yield

        def fill():
            yield from self.dense(part("a_z"), D, W, x, None, self.function_to(b["a_z"], "a_z", ACT.Silu))
            yield from self.dense(part("c_q"), D, W, x, None, self.copy_to(b["c_q"], "c_q", DIFF_QK ** -0.5))
            yield from self.dense(part("c_k"), D, W, x, None, self.copy_to(b["c_k"], "c_k"))
            yield from self.token_major(part("c_v"), D, W, x, None, self.tokens_to(b["c_v"], "c_v"))
            yield from self.dense(part("c_z"), D, W, x, None, self.function_to(b["c_z"], "c_z", ACT.Silu))
            yield "differential attention can start"
            yield from mla_q()
            yield from mla_kv()
            yield from self.dense(part("b_z"), D, W, x, None, self.function_to(b["b_z"], "b_z", ACT.Silu))
            yield "MLA can start"
            w_m = self.a["w_merge"][l]
            for j in range(6):
                bias = lambda blk, j=j: self.s(f"b_merge{l}", 1, 4 * j + blk)
                yield from self.dense(w_m[:, 512 * j:512 * (j + 1)], D, 512, x, None,
                                      self.function_to(b["gates"][:, 4 * j:4 * j + 4, :], "gates", ACT.Sigmoid, bias))
        filler = Filler(fill())

        state = {}

        def moba(h):
            rows, c = slice(64 * (h % 2), 64 * (h % 2) + 64), h // 2
            raw, probs = self.scores.take(), self.maps.take()
            pe.wait(ready["a_q"], ready["a_k"], raw.free)
            q, k_ = b["a_q"], b["a_k"]
            nc.tensor.matmul(raw.tile[:, 0:P], q[rows, c, 0:P], k_[rows, c, 0:P], start=True, stop=True)
            mark = pe.done(nc.tensor.matmul(raw.tile[:, P:TRI], q[rows, c, P:T], k_[rows, c, :], start=True, stop=True))
            parts = self.softmax(raw, mark, probs, lambda o: nc.vector.scalar_tensor_tensor(
                o[:, :], self.k("dist"), -float(MOBA_SLOPES[h]), raw.tile[:, 0:TRI], ALU.mult, ALU.add))
            mark = self.normalise(probs, parts)
            yield
            pt = self.transpose_map(probs, mark)
            yield
            if h % 2 == 0:
                state["bank"] = self.values.take()
                pe.wait(state["bank"].free)
            bank = state["bank"]
            mark = self.weigh_values(bank.tile[rows, 0:T], b["a_v"], slice(h * HD, (h + 1) * HD), pt)
            if h % 2 == 1:
                dve.wait(mark, ready["a_z"])
                bank.free = ready["ya"] = dve.done(nc.vector.tensor_tensor(
                    b["a_z"][:, c, :], bank.tile[:, 0:T], b["a_z"][:, c, :], ALU.mult))
        self.pipeline([moba(h) for h in range(HEADS)], filler)
        self.reuse["a_v"] = self.reuse["a_q"] = self.reuse["a_k"] = ready["ya"]

        filler.until("differential attention can start")
        yc = b["a_q"]
        yc_sq = b["a_k"]

        def diff(h):
            p_maps = []
            for m in range(2):
                rows = slice(64 * m, 64 * m + 64)
                raw, probs = self.scores.take(), self.maps.take()
                pe.wait(ready["c_q"], ready["c_k"], raw.free)
                q, k_ = b["c_q"], b["c_k"]
                nc.tensor.matmul(raw.tile[:, 0:P], q[rows, h, 0:P], k_[rows, h, 0:P], start=True, stop=True)
                mark = pe.done(nc.tensor.matmul(raw.tile[:, P:TRI], q[rows, h, P:T], k_[rows, h, :], start=True, stop=True))
                parts = self.softmax(raw, mark, probs, lambda o: nc.vector.scalar_tensor_tensor(
                    o[:, :], self.k("dist"), -float(DIFF_SLOPES[h]), raw.tile[:, 0:TRI], ALU.mult, ALU.add))
                p_maps.append(probs)
                if m == 0:
                    self.normalise(probs, parts)
            st = p_maps[1].stat
            dve.wait(dve.done(nc.vector.tensor_scalar(st[:, 6:8], st[:, 4:6], neg_lam, None, ALU.mult)))
            first, second = p_maps
            for i, (lo, hi) in enumerate(parts):
                mark = dve.done(nc.vector.scalar_tensor_tensor(
                    first.tile[:, lo:hi], second.tile[:, lo:hi], st[:, 6 + i:7 + i], first.tile[:, lo:hi],
                    ALU.mult, ALU.add))
            second.free = mark
            yield
            pt = self.transpose_map(first, mark)
            yield
            bank = self.values.take()
            pe.wait(bank.free)
            mark = self.weigh_values(bank.tile[:, 0:T], b["c_v"], slice(h * P, (h + 1) * P), pt)
            act.wait(mark)
            bank.free = ready["yc"] = mark = act.done(nc.scalar.copy(yc[:, h, :], bank.tile[:, 0:T]))
            ready["yc_sq"] = self.square(yc_sq[:, h, :], yc[:, h, :], mark)
        self.pipeline([diff(h) for h in range(DIFF_HEADS)], filler)
        self.reuse["c_v"] = self.reuse["c_q"] = self.reuse["c_k"] = ready["yc"]

        filler.until("MLA can start")

        def mla(h):
            raw, probs = self.scores.take(), self.maps.take()
            pe.wait(ready["b_q"], ready["b_k"], ready["b_k_rope"], raw.free)
            q, k_ = b["b_q"], b["b_k"]
            nc.tensor.matmul(raw.tile[:, 0:P], q[0:96, h, 0:P], k_[0:96, h, 0:P], start=True, stop=True)
            mark = pe.done(nc.tensor.matmul(raw.tile[:, P:TRI], q[0:96, h, P:T], k_[0:96, h, :], start=True, stop=True))
            parts = self.softmax(raw, mark, probs, lambda o: nc.vector.scalar_tensor_tensor(
                o[:, :], raw.tile[:, 0:TRI], (NOPE + ROPE) ** -0.5, self.k("causal"), ALU.mult, ALU.add))
            mark = self.normalise(probs, parts)
            yield
            pt = self.transpose_map(probs, mark)
            yield
            rows, c = slice(64 * (h % 2), 64 * (h % 2) + 64), h // 2
            if h % 2 == 0:
                state["bank"] = self.values.take()
                pe.wait(state["bank"].free)
            bank = state["bank"]
            mark = self.weigh_values(bank.tile[rows, 0:T], b["b_v"], slice(h * HD, (h + 1) * HD), pt)
            if h % 2 == 1:
                dve.wait(mark, ready["b_z"])
                bank.free = ready["yb"] = dve.done(nc.vector.tensor_tensor(
                    b["b_z"][:, c, :], bank.tile[:, 0:T], b["b_z"][:, c, :], ALU.mult))
        self.pipeline([mla(h) for h in range(HEADS)], filler)
        self.reuse["b_v"] = ready["yb"]

        banks = self.inverse_rms(yc_sq, 4, 1, P, 1e-5, ready["yc_sq"])
        for g in range(0, 4, 2):
            bank = banks[g // 2]
            both = yc[:, g:g + 2, :].rearrange("p j t -> p (j t)")
            z = b["c_z"][:, g:g + 2, :].rearrange("p j t -> p (j t)")
            dve.wait(bank.ready, ready["yc"], ready["c_z"])
            bank.free = mark = dve.done(nc.vector.tensor_tensor(both, both, bank.tile[:, :], ALU.mult))
            dve.wait(mark)
            ready["ycn"] = dve.done(nc.vector.scalar_tensor_tensor(z, both, subln, z, ALU.mult, ALU.mult))
        while filler.step():
            pass

        merged, tmp = b["b_q"], b["tmp"]
        for i, (name, y, y_ready) in enumerate((("w_branch_a", "a_z", "ya"), ("w_branch_b", "b_z", "yb"),
                                                ("w_branch_c", "c_z", "ycn"))):
            def gate(tile, blk, n, mark, i=i):
                m = merged[:, blk:blk + 2, :].rearrange("p j t -> p (j t)")
                g = b["gates"][:, i * DC + blk:i * DC + blk + 2, :].rearrange("p j t -> p (j t)")
                dve.wait(mark, ready["gates"], ready["yb"])
                if i == 0:
                    ready["merged"] = got = dve.done(nc.vector.tensor_tensor(m, tile[:, :], g, ALU.mult))
                    return got
                dve.wait(ready["merged"])
                got = dve.done(nc.vector.tensor_tensor(g, tile[:, :], g, ALU.mult))
                dve.wait(got)
                ready["merged"] = dve.done(nc.vector.tensor_tensor(m, m, g, ALU.add))
                return got
            run(self.dense(self.a[name][l], W, D, b[y], ready[y_ready], gate))
        for n in ("a_z", "b_z", "c_z", "gates"):
            self.reuse[n] = ready["merged"]

        pp = b["b_k"]
        run(self.dense(self.a["w_ple"][l], PLE, D, b["pT"], p_loaded, self.copy_to(pp, "pp")))
        self.reuse["pT"] = ready["pp"]

        def residual(tile, blk, n, mark, base=0):
            r = x[:, base + blk:base + blk + 2, :].rearrange("p j t -> p (j t)")
            dve.wait(mark)
            ready["r"] = dve.done(nc.vector.scalar_tensor_tensor(r, r, ALPHA, tile[:, :], ALU.mult, ALU.add))
            return ready["r"]
        for j in range(2):
            run(self.dense(self.a["w_out"][l][:, 512 * j:512 * (j + 1)], D, 512, merged, ready["merged"],
                           lambda t_, blk, n, m, j=j: residual(t_, blk, n, m, 4 * j)))
        r2, sg = b["b_q"], b["gates"]
        def ple(tile, blk, n, mark, base=0):
            c = base + blk
            act.wait(mark, ready["merged"], ready["r"])
            s_ = sg[:, c:c + 2, :].rearrange("p j t -> p (j t)")
            q_ = pp[:, c:c + 2, :].rearrange("p j t -> p (j t)")
            r_ = x[:, c:c + 2, :].rearrange("p j t -> p (j t)")
            o_ = r2[:, c:c + 2, :].rearrange("p j t -> p (j t)")
            got = act.done(nc.scalar.activation(s_, tile[:, :], ACT.Sigmoid))
            dve.wait(got, ready["pp"])
            dve.wait(dve.done(nc.vector.tensor_tensor(s_, s_, q_, ALU.mult)))
            ready["r2"] = dve.done(nc.vector.tensor_tensor(o_, s_, r_, ALU.add))
            return got
        for j in range(2):
            run(self.dense(self.a["w_ple_gate"][l][:, 512 * j:512 * (j + 1)], D, 512, x, ready["r"],
                           lambda t_, blk, n, m, j=j: ple(t_, blk, n, m, 4 * j)))

        sums = self.turned.take()
        pe.wait(ready["r2"], sums.free)
        for t in range(TB):
            last = self.product(sums.tile[:, t:t + 1],
                                [(r2[:, k, t * P:(t + 1) * P], self.k("ones", 0)) for k in range(DC)])
        mark = pe.done(last)
        st = self.stats.take()
        dve.wait(mark, st.free)
        sums.free = mark = dve.done(nc.vector.tensor_scalar(st.tile[:, 0, 0:TB], sums.tile[:, 0:TB], -1.0 / D, None, ALU.mult))
        pe.wait(mark)
        (bank,) = self.broadcast(st, st.tile[:, 0, 0:TB], 1)
        dve.wait(bank.ready)
        sq = b["gates"]
        for c in range(DC):
            mark = dve.done(nc.vector.tensor_tensor(r2[:, c, :], r2[:, c, :], bank.tile[:, 0:T], ALU.add))
            act.wait(mark)
            sq_mark = act.done(nc.scalar.activation(sq[:, 8 + c, :], r2[:, c, :], ACT.Square))
        bank.free = mark
        (bank,) = self.inverse_rms(sq[:, 8:16, :], 1, DC, D, 1e-5, sq_mark)
        self.h_ready = []
        dve.wait(bank.ready)
        for c in range(DC):
            mark = dve.done(nc.vector.scalar_tensor_tensor(
                r2[:, c, :], r2[:, c, :], self.s(f"ln_g{l}", 1, c), bank.tile[:, 0:T], ALU.mult, ALU.mult))
            bank.free = mark
            act.wait(mark)
            self.h_ready.append(act.done(nc.scalar.activation(
                x[:, c, :], r2[:, c, :], ACT.Identity, bias=self.s(f"ln_b{l}", 1, c))))
        self.reuse["b_q"] = self.reuse["b_k"] = self.reuse["gates"] = self.h_ready[-1]
        for n in ("a_q", "a_k"):
            self.reuse[n] = ready["ycn"]

    def normalise(self, probs, parts):
        for i, (lo, hi) in enumerate(parts):
            mark = self.dve.done(self.nc.vector.tensor_scalar(
                probs.tile[:, lo:hi], probs.tile[:, lo:hi], probs.stat[:, 4 + i:5 + i], None, ALU.mult))
        return mark

    def second_stack(self, stack, out):
        nc = self.nc
        sb = lambda name, shape: stack.enter_context(nc.sbuf_tensor(name, shape, F32))
        self.ready, self.reuse = {}, {}
        self.mod_every = 3
        b = self.b = {}
        b["u"] = sb("u", [P, DC, T])
        b["squares"] = sb("squares", [P, DC, T])
        b["ff"] = sb("ff", [P, FC, T])
        for n in ("s_q", "s_k", "m_z"):
            b[n] = sb(n, [P, 4, T])
        for n in ("s_v", "m_v"):
            b[n] = sb(n, [P, TB, 512])
        for i, n in enumerate(("r_q", "r_k", "r_g")):
            b[n] = b["ff"][:, 4 * i:4 * i + 4, :]
        b["r_v"] = b["ff"][:, 12:16, :].rearrange("p (b j) t -> p b (j t)", b=TB)
        b["xbc_in"] = sb("xbc_in", [P, XBC // P, T + TAPS - 1])
        b["xbc"] = sb("xbc", [P, XBC // P, T])
        b["dt"] = sb("dt", [P, 6, 2 * MH])
        b["cum"] = sb("cum", [P, 4, MH])
        b["neg_a"] = sb("neg_a", [P, MH])
        b["y"] = sb("y", [P, MIX // P, T])
        b["tmp"] = sb("tmp2", [P, 2 * T])
        b["cb"] = sb("cb", [P, MG, TRI])
        b["coef"] = sb("coef", [P, 4, DC])
        self.maps = Turn([sb(f"work{i}", [P, TRI]) for i in range(3)])
        self.keep = Turn([sb(f"keep{i}", [P, TRI]) for i in range(3)])
        self.maps_t = Turn([sb(f"weights_t{i}", [P, TRI]) for i in range(3)])
        self.dve.wait(self.h_ready)
        self.pool.wait(self.h_ready)
        self.act.wait(self.h_ready)
        self.sp.wait(self.h_ready)
        self.pad_ready = self.dve.done(nc.vector.memset(b["xbc_in"][:, :, 0:TAPS - 1], 0.0))
        for l in range(DEPTH):
            self.second_layer(l)
        self.finish_mods(0)
        marks = self.modulated_norm("final_norm", DEPTH * 72, DEPTH * 72 + 8, self.b["xbc"])
        written = stack.enter_context(nc.semaphore("written"))
        for c in range(0, DC, 2):
            self.sp.wait(marks[c + 1])
            nc.sync.dma_start(out.rearrange("(c p) t -> p c t", p=P)[:, c:c + 2, :],
                              self.b["xbc"][:, c:c + 2, :]).then_inc(written, 16)
        nc.sync.wait_ge(written, 16 * (DC // 2))

    def modulated_norm(self, gain, shift_at, scale_at, dst):
        nc, b, dve, act = self.nc, self.b, self.dve, self.act
        h, coef = self.h, b["coef"]
        for c in range(DC):
            act.wait(self.h_ready[c], self.reuse.get("squares"))
            sq = act.done(nc.scalar.activation(b["squares"][:, c, :], h[:, c, :], ACT.Square))
        dve.wait(self.mod_last, self.reuse.get("coef"))
        dve.wait(dve.done(nc.vector.scalar_tensor_tensor(
            coef[:, 0, :], self.mods[:, scale_at:scale_at + DC], 1.0, self.s(gain, DC), ALU.add, ALU.mult)))
        (bank,) = self.inverse_rms(b["squares"], 1, DC, D, 1e-6, sq)
        self.reuse["squares"] = bank.ready
        marks = []
        dve.wait(bank.ready, self.reuse.get("u"))
        for c in range(DC):
            mark = dve.done(nc.vector.scalar_tensor_tensor(
                dst[:, c, :], h[:, c, :], coef[:, 0, c:c + 1], bank.tile[:, 0:T], ALU.mult, ALU.mult))
            bank.free = mark
            act.wait(mark)
            marks.append(act.done(nc.scalar.activation(
                dst[:, c, :], dst[:, c, :], ACT.Identity, bias=self.mods[:, shift_at + c:shift_at + c + 1])))
        return marks

    def run(self, g):
        for _ in g:
            pass

    def feed_forward(self, l, n, gain, at):
        nc, b, pe, dve, act = self.nc, self.b, self.pe, self.dve, self.act
        ready, h, u, ff = self.ready, self.h, b["u"], b["ff"]
        marks = self.modulated_norm(gain, at, at + DC, u)
        dve.wait(dve.done(nc.vector.tensor_scalar(b["coef"][:, 1, :], self.mods[:, at + 2 * DC:at + 3 * DC],
                                                  0.5, 0.5, ALU.mult, ALU.add)))
        wg, wu, wd = (self.a[f"ffn{n}_{w}_2"][l] for w in ("wg", "wu", "wd"))
        for c0 in range(0, FF, 512):
            cols = min(512, FF - c0)
            base = c0 // P

            def gate(tile, blk, m, mark):
                act.wait(mark, self.reuse.get("ff"))
                ready["gate"] = act.done(nc.scalar.activation(
                    ff[:, base + blk:base + blk + 2, :].rearrange("p j t -> p (j t)"), tile[:, :], ACT.Silu))
                return ready["gate"]

            def up(tile, blk, m, mark):
                f = ff[:, base + blk:base + blk + 2, :].rearrange("p j t -> p (j t)")
                dve.wait(mark, ready["gate"])
                ready["ff"] = dve.done(nc.vector.tensor_tensor(f, tile[:, :], f, ALU.mult))
                return ready["ff"]
            self.run(self.dense(wg[:, c0:c0 + cols], D, cols, u, marks if c0 == 0 else None, gate))
            self.run(self.dense(wu[:, c0:c0 + cols], D, cols, u, None, up))
        half = FC // 2
        new = []
        for j in range(0, DC, 2):
            banks = [self.products.take() for _ in range(2)]
            for part in range(2):
                rows = slice(part * half * P, (part + 1) * half * P)
                slot = self.load(wd[rows, j * P:(j + 2) * P], half * P, 2 * P)
                pe.wait(slot.loaded, ready["ff"])
                for i in range(2):
                    if part == 0:
                        pe.wait(banks[i].free)
                    last = self.product(banks[i].tile[:, 0:T],
                                        [(slot.view[:, k, i * P:(i + 1) * P], ff[:, part * half + k, :])
                                         for k in range(half)], start=part == 0, stop=part == 1)
                    if part == 1:
                        mark = pe.done(last)
                        dve.wait(mark)
                        c = j + i
                        banks[i].free = got = dve.done(nc.vector.scalar_tensor_tensor(
                            h[:, c, :], banks[i].tile[:, 0:T], b["coef"][:, 1, c:c + 1], h[:, c, :],
                            ALU.mult, ALU.add))
                        new.append(got)
                    elif i == 1:
                        mark = pe.done(last)
                slot.free = mark
                self.count_panel()
        self.reuse["ff"] = self.reuse["u"] = mark
        self.h_ready = new

    def second_layer(self, l):
        self.finish_mods(22 if l == 0 else 4)
        at = 72 * l
        self.feed_forward(l, 1, f"norm_ffn1{l}", at)
        self.mixers(l, at + 3 * DC)
        self.feed_forward(l, 2, f"norm_ffn2{l}", at + 6 * DC)

    def mixers(self, l, at):
        nc, b, pe, dve, act, pool = self.nc, self.b, self.pe, self.dve, self.act, self.pool
        ready, u, h, y = self.ready, b["u"], self.h, b["y"]
        marks = self.modulated_norm(f"norm_mix{l}", at, at + DC, u)
        dve.wait(dve.done(nc.vector.tensor_scalar(b["coef"][:, 1, :], self.mods[:, at + 2 * DC:at + 3 * DC],
                                                  1.0, None, ALU.add)))
        w_in = self.a["w_in_2"][l]
        part = lambda n: w_in[:, IN2[n][0]:IN2[n][0] + IN2[n][1]]

        def conv_in(base):
            def evacuate(tile, blk, n, mark):
                act.wait(mark, self.pad_ready, self.reuse.get("xbc_in"))
                got = act.done(nc.scalar.copy(b["xbc_in"][:, base + blk:base + blk + 2, TAPS - 1:],
                                              tile[:, :].rearrange("p (j t) -> p j t", j=2)))
                dve.wait(got)
                for c in (base + blk, base + blk + 1):
                    src, dst = b["xbc_in"], b["xbc"]
                    tap = lambda i: self.s(f"conv_w{l}", 1, 8 * i + c)
                    m = dve.done(nc.vector.tensor_scalar(dst[:, c, :], src[:, c, 0:T], tap(0), None, ALU.mult))
                    for i in range(1, TAPS):
                        dve.wait(m)
                        m = dve.done(nc.vector.scalar_tensor_tensor(
                            dst[:, c, :], src[:, c, i:i + T], tap(i), dst[:, c, :], ALU.mult, ALU.add))
                    act.wait(m)
                    ready["xbc"] = act.done(nc.scalar.activation(dst[:, c, :], dst[:, c, :], ACT.Silu,
                                                                 bias=self.s(f"conv_b{l}", 1, c)))
                return got
            return evacuate
        self.run(self.dense(part("m_x"), D, 512, u, marks, conv_in(0)))
        self.run(self.dense(part("m_bc"), D, 512, u, None, conv_in(4)))

        slot = self.load(part("m_dt"), D, MH)
        bank = self.products.take()
        pe.wait(slot.loaded, bank.free)
        for t in range(TB):
            last = self.product(bank.tile[:, t * MH:(t + 1) * MH],
                                [(u[:, k, t * P:(t + 1) * P], slot.view[:, k, :]) for k in range(DC)])
        slot.free = mark = pe.done(last)
        z, az, ez, lz, dt, da = (b["dt"][:, i, :] for i in range(6))
        dve.wait(mark)
        for t in range(TB):
            bank.free = m = dve.done(nc.vector.tensor_tensor(
                z[:, t * MH:(t + 1) * MH], bank.tile[:, t * MH:(t + 1) * MH], self.s(f"dt_bias{l}", MH), ALU.add))
        act.wait(m)
        act.wait(act.done(nc.scalar.activation(az, z, ACT.Abs)))
        act.wait(act.done(nc.scalar.activation(ez, az, ACT.Exp, scale=-1.0)))
        act.done(nc.scalar.activation(b["neg_a"][:, :], self.s(f"a_log{l}", MH), ACT.Exp))
        m = act.done(nc.scalar.activation(lz, ez, ACT.Ln, bias=1.0))
        dve.wait(m)
        dve.wait(dve.done(nc.vector.scalar_tensor_tensor(dt, z, 0.0, lz, ALU.max, ALU.add)))
        for t in range(TB):
            cols = slice(t * MH, (t + 1) * MH)
            da_ready = dve.done(nc.vector.scalar_tensor_tensor(da[:, cols], dt[:, cols], -1.0, b["neg_a"][:, :],
                                                               ALU.mult, ALU.mult))

        def fill():
            yield from self.dense(part("s_q"), D, 512, u, None, self.copy_to(b["s_q"], "s_q", SBD ** -0.5))
            yield from self.dense(part("s_k"), D, 512, u, None, self.copy_to(b["s_k"], "s_k"))
            yield from self.token_major(part("s_v"), D, 512, u, None, self.tokens_to(b["s_v"], "s_v"))
            yield from self.dense(part("m_z"), D, 512, u, None, self.function_to(b["m_z"], "m_z", ACT.Silu))
            yield "stick-breaking and Mamba can start"
            yield from self.dense(part("r_q"), D, 512, u, None, self.copy_to(b["r_q"], "r_q"))
            yield from self.dense(part("r_k"), D, 512, u, None, self.copy_to(b["r_k"], "r_k"))
            yield from self.token_major(part("r_v"), D, 512, u, None, self.tokens_to(b["r_v"], "r_v"))
            yield from self.dense(part("r_g"), D, 512, u, None, self.function_to(b["r_g"], "r_g", ACT.Silu))
            yield "retention can start"
        filler = Filler(fill())
        filler.until("stick-breaking and Mamba can start")

        def stick(i):
            q, k_ = b["s_q"], b["s_k"]
            bank, work, keep = self.scores.take(), self.maps.take(), self.keep.take()
            pe.wait(ready["s_q"], ready["s_k"], bank.free)
            nc.tensor.matmul(bank.tile[:, 0:T], k_[:, i, 0:P], q[:, i, :], start=True, stop=False, skip_group_check=True)
            mark = pe.done(nc.tensor.matmul(bank.tile[:, T:TRI], k_[:, i, P:T], q[:, i, P:T], start=False, stop=False,
                                            skip_group_check=True))
            raw = bank.tile[:, 0:TRI]
            act.wait(mark, work.free, keep.free)
            act.wait(act.done(nc.scalar.activation(work.tile[:, :], raw, ACT.Abs)))
            act.wait(act.done(nc.scalar.activation(work.tile[:, :], work.tile[:, :], ACT.Exp, scale=-1.0)))
            m = act.done(nc.scalar.activation(work.tile[:, :], work.tile[:, :], ACT.Ln, bias=1.0))
            dve.wait(m)
            m = dve.done(nc.vector.scalar_tensor_tensor(work.tile[:, :], raw, 0.0, work.tile[:, :], ALU.max, ALU.add))
            dve.wait(m)
            m = dve.done(nc.vector.tensor_tensor(keep.tile[:, :], work.tile[:, :], self.k("before"), ALU.mult))
            yield
            pe.wait(m)
            nc.tensor.matmul(bank.tile[:, 0:T], self.k("neg_ge"), keep.tile[:, 0:T], start=False, stop=False, skip_group_check=True)
            nc.tensor.matmul(bank.tile[:, P:T], self.k("neg_ones"), keep.tile[:, T:TRI], start=False, stop=False, skip_group_check=True)
            keep.free = m = pe.done(nc.tensor.matmul(bank.tile[:, T:TRI], self.k("neg_ge"), keep.tile[:, T:TRI],
                                                     start=False, stop=True, skip_group_check=True))
            wt = self.maps_t.take()
            dve.wait(m, wt.free)
            bank.free = m = dve.done(nc.vector.tensor_tensor(work.tile[:, :], raw, self.k("before_neg"), ALU.add))
            act.wait(m)
            work.free = wt.ready = act.done(nc.scalar.activation(wt.tile[:, :], work.tile[:, :], ACT.Exp))
            yield
            vbank = self.values.take()
            pe.wait(vbank.free, ready["s_v"])
            m = self.weigh_values(vbank.tile[:, 0:T], b["s_v"], slice(i * P, (i + 1) * P), wt)
            act.wait(m, self.reuse.get("y"))
            vbank.free = ready["y_s"] = act.done(nc.scalar.copy(y[:, 4 + i, :], vbank.tile[:, 0:T]))
        self.pipeline([stick(i) for i in range(SBH)], filler)

        bank = self.scores.take()
        pe.wait(da_ready, bank.free)
        for t in range(TB):
            nc.tensor.matmul(bank.tile[:, t * MH:(t + 1) * MH], self.k("le"), da[:, t * MH:(t + 1) * MH], start=True, stop=True)
        m = pe.done(nc.tensor.matmul(bank.tile[:, 2 * MH:3 * MH], self.k("gt"), da[:, 0:MH], start=True, stop=True))
        dve.wait(m, self.reuse.get("cum"))
        bank.free = cum_ready = dve.done(nc.vector.tensor_copy(
            b["cum"][:, 0:3, :].rearrange("p i h -> p (i h)"), bank.tile[:, 0:3 * MH]))
        for t in range(TB):
            bank = self.turned.take()
            pe.wait(ready["xbc"], bank.free)
            for c in range(4):
                last = nc.tensor.transpose(bank.tile[:, c * P:(c + 1) * P], b["xbc"][:, c, t * P:(t + 1) * P], self.k("ident"))
            m = pe.done(last)
            act.wait(m)
            bank.free = ready["m_v"] = act.done(nc.scalar.copy(b["m_v"][:, t, :], bank.tile[:, :]))
        for g in range(MG):
            bank = self.scores.take()
            pe.wait(bank.free)
            B_, C_ = b["xbc"][:, 4 + g, :], b["xbc"][:, 6 + g, :]
            nc.tensor.matmul(bank.tile[:, 0:T], B_[:, 0:P], C_, start=True, stop=True)
            m = pe.done(nc.tensor.matmul(bank.tile[:, T:TRI], B_[:, P:T], C_[:, P:T], start=True, stop=True))
            act.wait(m)
            bank.free = cb_ready = act.done(nc.scalar.copy(b["cb"][:, g, :], bank.tile[:, 0:TRI]))
        state = {}

        def mamba(i):
            bank, work = self.scores.take(), self.maps.take()
            pe.wait(bank.free)
            for t in range(TB):
                last = nc.tensor.matmul(bank.tile[:, t * P:(t + 1) * P],
                                        da[:, t * MH + i:t * MH + i + 1].to_broadcast([P, P]), self.k("le"),
                                        start=True, stop=True)
            m = pe.done(last)
            cum = lambda j: b["cum"][:, j, i:i + 1]
            dve.wait(m, cum_ready, work.free)
            w_ = work.tile
            nc.vector.scalar_tensor_tensor(w_[:, 0:P], bank.tile[:, 0:P], cum(0), self.k("upto_min"), ALU.subtract, ALU.min)
            nc.vector.tensor_scalar(w_[:, P:T], bank.tile[:, P:T], cum(2), None, ALU.add)
            bank.free = m = dve.done(nc.vector.scalar_tensor_tensor(
                w_[:, T:TRI], bank.tile[:, P:T], cum(1), self.k("upto_min"), ALU.subtract, ALU.min))
            act.wait(m)
            m = act.done(nc.scalar.activation(w_[:, :], w_[:, :], ACT.Exp))
            wt = self.maps_t.take()
            dve.wait(m, cb_ready, wt.free)
            g = i // (MH // MG)
            nc.vector.scalar_tensor_tensor(wt.tile[:, 0:T], w_[:, 0:T], dt[:, i:i + 1], b["cb"][:, g, 0:T], ALU.mult, ALU.mult)
            wt.ready = work.free = dve.done(nc.vector.scalar_tensor_tensor(
                wt.tile[:, T:TRI], w_[:, T:TRI], dt[:, MH + i:MH + i + 1], b["cb"][:, g, T:TRI], ALU.mult, ALU.mult))
            yield
            rows, c = slice(64 * (i % 2), 64 * (i % 2) + 64), i // 2
            if i % 2 == 0:
                state["bank"] = self.values.take()
                pe.wait(state["bank"].free)
            vbank = state["bank"]
            pe.wait(ready["m_v"])
            m = self.weigh_values(vbank.tile[rows, 0:T], b["m_v"], slice(i * MP, (i + 1) * MP), wt)
            if i % 2 == 1:
                dve.wait(m, ready["m_z"], self.reuse.get("y"))
                vbank.free = m = dve.done(nc.vector.scalar_tensor_tensor(
                    y[:, 8 + c, :], b["xbc"][:, c, :], self.s(f"d_skip{l}", 1, c), vbank.tile[:, 0:T], ALU.mult, ALU.add))
                dve.wait(m)
                m = dve.done(nc.vector.tensor_tensor(y[:, 8 + c, :], y[:, 8 + c, :], b["m_z"][:, c, :], ALU.mult))
                ready["y_m_sq"] = self.square(b["squares"][:, c, :], y[:, 8 + c, :], [m, self.reuse["squares"]])
                ready["y_m"] = m
        self.pipeline([mamba(i) for i in range(MH)], filler)
        filler.until("retention can start")
        self.reuse["xbc_in"] = self.reuse["cum"] = self.reuse["m_z"] = ready["y_m"]

        (bank,) = self.inverse_rms(b["squares"], 1, 4, 512, 1e-6, ready["y_m_sq"])
        dve.wait(bank.ready)
        for c in range(4):
            m = dve.done(nc.vector.scalar_tensor_tensor(
                y[:, 8 + c, :], y[:, 8 + c, :], self.s(f"ssm_norm{l}", 1, c), bank.tile[:, 0:T], ALU.mult, ALU.mult))
        bank.free = ready["y_m"] = m

        for name in ("r_q", "r_k"):
            for c in range(0, 4, 2):
                both = b[name][:, c:c + 2, :].rearrange("p j t -> p (j t)")
                bank = self.products.take()
                pe.wait(ready[name], bank.free)
                m = pe.done(nc.tensor.matmul(bank.tile[:, :], self.k("swap64"), both, start=True, stop=True))
                dve.wait(m, self.reuse.get("tmp"))
                bank.free = dve.done(nc.vector.tensor_tensor(b["tmp"][:, :], bank.tile[:, :], self.k("sin128"), ALU.mult))
                dve.wait(dve.done(nc.vector.tensor_tensor(both, both, self.k("cos128"), ALU.mult)))
                self.reuse["tmp"] = ready[name + "_rot"] = dve.done(nc.vector.tensor_tensor(both, both, b["tmp"][:, :], ALU.add))

        def retain(i):
            q, k_ = b["r_q"], b["r_k"]
            bank, wt = self.scores.take(), self.maps_t.take()
            pe.wait(ready["r_q_rot"], ready["r_k_rot"], bank.free)
            nc.tensor.matmul(bank.tile[:, 0:T], k_[:, i, 0:P], q[:, i, :], start=True, stop=True)
            m = pe.done(nc.tensor.matmul(bank.tile[:, T:TRI], k_[:, i, P:T], q[:, i, P:T], start=True, stop=True))
            dve.wait(m, wt.free)
            bank.free = wt.ready = dve.done(nc.vector.tensor_tensor(
                wt.tile[:, :], bank.tile[:, 0:TRI], self.k("decay", i * TRI, TRI), ALU.mult))
            yield
            vbank = self.values.take()
            pe.wait(vbank.free, ready["r_v"])
            m = self.weigh_values(vbank.tile[:, 0:T], b["r_v"], slice(i * P, (i + 1) * P), wt)
            act.wait(m)
            vbank.free = m = act.done(nc.scalar.activation(y[:, i, :], vbank.tile[:, 0:T], ACT.Copy))
            ready["y_r"] = m
            ready["y_r_sq"] = self.square(b["squares"][:, 4 + i, :], y[:, i, :], m)
        self.pipeline([retain(i) for i in range(RH)], filler)
        banks = self.inverse_rms(b["squares"][:, 4:8, :], 4, 1, RD, 1e-6, ready["y_r_sq"])
        for i in range(RH):
            bank = banks[i // 2]
            dve.wait(bank.ready, ready["y_r"], ready["r_g"])
            bank.free = m = dve.done(nc.vector.scalar_tensor_tensor(
                y[:, i, :], y[:, i, :], self.s(f"ret_gn{l}", 1, i), bank.tile[:, (i % 2) * T:(i % 2 + 1) * T],
                ALU.mult, ALU.mult))
            dve.wait(m)
            ready["y_r"] = dve.done(nc.vector.tensor_tensor(y[:, i, :], y[:, i, :], b["r_g"][:, i, :], ALU.mult))
        self.reuse["squares"] = bank.ready
        for n in ("r_q", "r_k", "r_v", "r_g", "s_q", "s_k", "s_v"):
            self.reuse[n] = ready["y_r"]

        new = []
        y_ready = [ready["y_r"], ready["y_s"], ready["y_m"]]

        def residual(j):
            def evacuate(tile, blk, n, mark):
                dve.wait(mark)
                for i in range(2):
                    c = j + i
                    got = dve.done(nc.vector.scalar_tensor_tensor(
                        h[:, c, :], tile[:, i * T:(i + 1) * T], b["coef"][:, 1, c:c + 1], h[:, c, :], ALU.mult, ALU.add))
                    new.append(got)
                self.reuse["y"] = mark
                return got
            return evacuate
        pe.wait(*y_ready)
        for j in range(0, DC, 2):
            self.run(self.dense(self.a["w_out_2"][l][:, j * P:(j + 2) * P], MIX, 2 * P, y, None, residual(j)))
        self.reuse["u"] = self.reuse["y"]
        self.h_ready = new


def constants():
    f = np.float32
    c = {}
    i = np.arange(P)
    c["ident"] = np.eye(P, dtype=f)
    c["ones"] = np.ones((P, P), f)
    c["swap64"] = (i[:, None] == (i[None, :] + 64) % P).astype(f)
    s16 = np.zeros((P, 32), f)
    j = np.arange(32)
    s16[64 + (j + 16) % 32, j] = 1.0
    c["swap16"] = s16

    def tri(fn):
        k = np.arange(T)
        return np.concatenate([fn(i[:, None], k[None, :P]), fn(P + i[:, None], k[None, :])], 1).astype(f)

    def tri_t(fn):
        t = np.arange(T)
        return np.concatenate([fn(i[:, None], t[None, :]), fn(P + i[:, None], t[None, P:])], 1).astype(f)
    c["dist"] = tri(lambda q, k: np.where(k <= q, q - k, 1e33))
    c["causal"] = tri(lambda q, k: np.where(k <= q, 0.0, NEG))

    def rotary(half, base_row, rows, freqs):
        pos = np.arange(T, dtype=f)
        ang = (pos[:, None] * freqs[None, :]).astype(f)
        cos, sin = np.cos(ang).T, np.sin(ang).T
        cc, ss = np.zeros((P, T), f), np.zeros((P, T), f)
        cc[base_row:base_row + rows] = np.concatenate([cos, cos])
        ss[base_row:base_row + rows] = np.concatenate([-sin, sin])
        return np.concatenate([cc, cc], 1), np.concatenate([ss, ss], 1)
    fr = (f(10000.0) ** (-np.arange(0, ROPE, 2, dtype=f) / f(ROPE))).astype(f)
    c["cos32"], c["sin32"] = rotary(16, 64, 32, fr)
    fr = (f(10000.0) ** (-np.arange(64, dtype=f) / f(64))).astype(f)
    c["cos128"], c["sin128"] = rotary(64, 0, 128, fr)
    decay = []
    for h in range(RH):
        lg = math.log1p(-(2.0 ** (-5.0 - h)))
        decay.append(tri_t(lambda s, t: np.where(s // 64 <= t // 64, np.exp(lg * np.abs(t - s)), 0.0) * RD ** -0.5))
    c["decay"] = np.concatenate(decay, 1)
    c["before"] = tri_t(lambda s, t: s < t)
    c["before_neg"] = tri_t(lambda s, t: np.where(s < t, 0.0, NEG))
    c["upto_min"] = np.where(i[:, None] <= i[None, :], 0.0, NEG).astype(f)
    c["le"] = (i[:, None] <= i[None, :]).astype(f)
    c["gt"] = (i[:, None] > i[None, :]).astype(f)
    c["neg_ge"] = -(i[:, None] >= i[None, :]).astype(f)
    c["neg_ones"] = -np.ones((P, P), f)
    return np.ascontiguousarray(np.concatenate([c[n] for n, _ in CONST_SIZES], 1))


def small_parameters(a):
    col = lambda v: np.ascontiguousarray(v).reshape(-1, P).T
    every = lambda v: np.broadcast_to(np.asarray(v).reshape(1, -1), (P, np.asarray(v).size))
    parts = []
    for l in range(DEPTH):
        parts += [col(a["mla_q_norm_g"][l]), col(a["mla_kv_norm_g"][l]), col(a["diff_subln_g"][l]),
                  col(a["b_merge"][l]), col(a["ln_g"][l]), col(a["ln_b"][l]), col(a["ada_b_2"][l]),
                  col(a["norm_ffn1_2"][l]), col(a["norm_mix_2"][l]), col(a["norm_ffn2_2"][l]),
                  col(a["conv_w_2"][l].reshape(-1)), col(a["conv_b_2"][l]), col(a["ret_gn_2"][l]),
                  col(a["ssm_norm_2"][l]), col(np.repeat(a["d_skip_2"][l], MP)), every(a["dt_bias_2"][l]),
                  every(a["a_log_2"][l]), every(a["diff_lambda"][l])]
    parts += [col(a["c_2"]), col(a["final_ada_b_2"]), col(a["final_norm_2"])]
    return np.ascontiguousarray(np.concatenate(parts, 1))


DIRECT = {"w_in": "w_in", "mla_w_uq": "mla_w_uq", "mla_w_ukv": "mla_w_ukv", "w_branch_a": "w_branch_a",
          "w_branch_b": "w_branch_b", "w_branch_c": "w_branch_c", "w_merge": "w_merge", "w_out": "w_out",
          "w_ple_gate": "w_ple_gate", "w_ple": "w_ple", "ada_w": "ada_w_2", "final_ada_w": "final_ada_w_2",
          "ffn1_wg_2": "ffn1_wg_2", "ffn1_wu_2": "ffn1_wu_2", "ffn1_wd_2": "ffn1_wd_2", "w_in_2": "w_in_2",
          "w_out_2": "w_out_2", "ffn2_wg_2": "ffn2_wg_2", "ffn2_wu_2": "ffn2_wu_2", "ffn2_wd_2": "ffn2_wd_2"}


def kernel(**inputs):
    import concourse.bacc as bacc
    from concourse.bass_utils import run_bass_kernel_spmd

    given = {n: np.asarray(v) for n, v in inputs.items()}
    arrays = {n: np.ascontiguousarray(given[src]) for n, src in DIRECT.items()}
    arrays["x"] = np.ascontiguousarray(given["x"][0].T)
    arrays["p"] = np.ascontiguousarray(given["p"][:, 0].transpose(0, 2, 1))
    arrays["small"] = small_parameters(given)
    arrays["constants"] = constants()
    nc = bacc.Bacc("TRN2", target_bir_lowering=False, num_devices=1)
    handles = {n: nc.dram_tensor(f"in_{n}", v.shape, mybir.dt.from_np(v.dtype), kind="ExternalInput").ap()
               for n, v in arrays.items()}
    out = nc.dram_tensor("out", (D, T), F32, kind="ExternalOutput").ap()
    build(nc, handles, out)
    r = run_bass_kernel_spmd(nc, [{f"in_{n}": v for n, v in arrays.items()}], core_ids=[0])
    return np.ascontiguousarray(r.results[0]["out"].T)[None]
```

```python
from contextlib import ExitStack
import math

import numpy as np
import concourse.bass as bass
from concourse import mybir

F32 = mybir.dt.float32
F32R = mybir.dt.float32r
ALU = mybir.AluOpType
ACT = mybir.ActivationFunctionType
AX = mybir.AxisListType

P = 128
T = 256
TB = T // P
D = 1024
DC = D // P
DEPTH = 2
TRI = 3 * P

HEADS, HD = 8, 64
Q_LORA, KV_LORA, NOPE, ROPE = 384, 256, 64, 32
DIFF_HEADS, DIFF_QK = 4, 64
PLE = 256
W = HEADS * HD
IN1 = dict(a_q=(0, 512), a_k=(512, 512), a_v=(1024, 512), a_z=(1536, 512), b_cq=(2048, 384),
           b_ckvr=(2432, 288), b_z=(2720, 512), c_q=(3232, 512), c_k=(3744, 512),
           c_v=(4256, 512), c_z=(4768, 512))
ALPHA = (2 * DEPTH) ** 0.25
NSLOPE = HEADS + DIFF_HEADS
SLOPES = 2.0 ** (-8.0 * (np.arange(NSLOPE) + 1) / NSLOPE)
DIFF_IDX = np.arange(DIFF_HEADS) * (NSLOPE // DIFF_HEADS)
DIFF_SLOPES = SLOPES[DIFF_IDX].astype(np.float32)
MOBA_SLOPES = SLOPES[np.setdiff1d(np.arange(NSLOPE), DIFF_IDX)].astype(np.float32)

RH, RD = 4, 128
SBH, SBD = 4, 128
MH, MP, MN, MG = 8, 64, 128, 2
TAPS = 4
FF = 2816
FC = FF // P
IN2 = dict(r_q=(0, 512), r_k=(512, 512), r_v=(1024, 512), r_g=(1536, 512), s_q=(2048, 512),
           s_k=(2560, 512), s_v=(3072, 512), m_z=(3584, 512), m_x=(4096, 512),
           m_bc=(4608, 512), m_dt=(5120, 8))
XBC = 1024
MIX = 1536
OUT_ORDER = (4, 6, 8, 10, 0, 2)
HIDDEN_BLOCKS = 6
NMOD = 9

NEG = -1e30
SLOT = 2048
RAW_SLOTS = 4
SPLIT_SLOTS = 3
AHEAD = 2
MERGE_BLOCKS = 2


def columns(sizes):
    at, out = 0, {}
    for name, n in sizes:
        out[name] = at
        at += n
    return out, at


CONST_SIZES = {
    "both": [("ident", P), ("ones", P)],
    "first": [("swap16", 32), ("dist", TRI), ("causal", TRI), ("cos32", 2 * T), ("sin32", 2 * T)],
    "second": [("swap64", P), ("cos128", 2 * T), ("sin128", 2 * T), ("decay", RH * TRI), ("before", TRI),
               ("before_neg", TRI), ("upto_min", P), ("le", P), ("gt", P), ("neg_ge", P), ("neg_ones", P)]}
CONST_AT = {n: (group, at) for group, sizes in CONST_SIZES.items() for n, at in columns(sizes)[0].items()}
CONST_WIDTH = {n: w for sizes in CONST_SIZES.values() for n, w in sizes}

PER_LAYER = [("gq", 3), ("gkv", 2), ("subln", 1), ("b_merge", 24), ("ln_g", 8), ("ln_b", 8),
             ("ada_b", 72), ("norm_ffn1", 8), ("norm_mix", 8), ("norm_ffn2", 8), ("conv_w", 32),
             ("conv_b", 8), ("ret_gn", 4), ("ssm_norm", 4), ("d_skip", 4), ("dt_bias", 8),
             ("a_log", 8), ("lambda", 256)]
SMALL_SIZES = [(f"{n}{l}", s) for l in range(DEPTH) for n, s in PER_LAYER]
SMALL_SIZES += [("c", 8), ("final_ada_b", 16), ("final_norm", 8)]
SMALL_AT, SMALL_N = columns(SMALL_SIZES)


def plan(a):
    def panels(name, w, rows, start, total, width):
        for i, c in enumerate(range(0, total, width)):
            n = min(width, total - c)
            yield (name, i), w[:, start + c:start + c + n], rows, n

    def w_in(table, w, l, names):
        for n in names:
            yield from panels(f"{n}{l}", w[l], D, *table[n], 256)

    def merge(l, i, branch):
        width = MERGE_BLOCKS * P
        gates = panels(f"gate_{branch}{l}", a["w_merge"][l], D, i * D, D, width)
        products = panels(f"branch_{branch}{l}", a[f"w_branch_{branch}"][l], W, 0, D, width)
        for pair in zip(gates, products):
            yield from pair

    for l in range(DEPTH):
        yield from w_in(IN1, a["w_in"], l, ["b_cq"])
        start = IN1["b_ckvr"][0]
        yield (f"b_ckvr{l}", 0), a["w_in"][l][:, start:start + P], D, P
        yield (f"b_ckvr{l}", 1), a["w_in"][l][:, start + P:start + 288], D, 160
        yield from w_in(IN1, a["w_in"], l, ["a_q", "a_k", "a_v", "a_z", "c_q", "c_k", "c_v", "c_z"])
        yield from merge(l, 0, "a")
        yield from panels(f"uq{l}", a["mla_w_uq"][l], Q_LORA, 0, 768, 384)
        yield from panels(f"ukv{l}", a["mla_w_ukv"][l], KV_LORA, 0, 1024, 1024)
        yield from w_in(IN1, a["w_in"], l, ["b_z"])
        yield from merge(l, 2, "c")
        yield from merge(l, 1, "b")
        yield from panels(f"ple{l}", a["w_ple"][l], PLE, 0, D, D)
        yield from panels(f"w_out{l}", a["w_out"][l], D, 0, D, 256)
        yield from panels(f"ple_gate{l}", a["w_ple_gate"][l], D, 0, D, 256)
    for l in range(DEPTH):
        for ffn in (1, 2):
            wg, wu, wd = (a[f"ffn{ffn}_{w}_2"][l] for w in ("wg", "wu", "wd"))
            pairs = FC // 2
            for i in range(pairs + 1):
                if i < pairs:
                    yield (f"wg{ffn}{l}", i), wg[:, 256 * i:256 * (i + 1)], D, 256
                    yield (f"wu{ffn}{l}", i), wu[:, 256 * i:256 * (i + 1)], D, 256
                if i > 0:
                    yield (f"wd{ffn}{l}", i - 1), wd[256 * (i - 1):256 * i, :], 256, D
            if ffn == 1:
                yield from w_in(IN2, a["w_in_2"], l, ["m_x", "m_bc", "m_dt", "s_q", "s_k", "s_v", "m_z",
                                                      "r_q", "r_k", "r_v", "r_g"])
                for c in OUT_ORDER:
                    yield (f"mix_out{l}", c), a["w_out_2"][l][c * P:(c + 2) * P, :], 256, D


def keys(name, n):
    return [(name, i) for i in range(n)]


class Split:

    def __init__(self, hi, lo):
        self.hi, self.lo = hi, lo


class Engine:

    def __init__(self, queue, semaphore):
        self.queue, self.semaphore, self.count, self.waited = queue, semaphore, 0, {}

    def done(self, instruction):
        instruction.then_inc(self.semaphore, 1)
        self.count += 1
        return (self.semaphore, self.count)

    def settle(self):
        if self.count:
            self.wait((self.semaphore, self.count))

    def wait(self, *marks):
        for mark in marks:
            if mark is None:
                continue
            if isinstance(mark, list):
                self.wait(*mark)
                continue
            semaphore, value = mark
            if self.waited.get(semaphore.name, 0) < value:
                self.queue.wait_ge(semaphore, value)
                self.waited[semaphore.name] = value


class Buffer:

    def __init__(self, tile):
        self.tile, self.free = tile, None


class Filler:

    def __init__(self, steps):
        self.steps, self.passed = steps, set()

    def step(self):
        for point in self.steps:
            if point is None:
                return True
            self.passed.add(point)
        return False

    def until(self, point):
        while point not in self.passed:
            if not self.step():
                assert point in self.passed


class Turn:

    def __init__(self, tiles):
        self.buffers, self.at = [Buffer(t) for t in tiles], 0

    def take(self):
        self.at += 1
        return self.buffers[(self.at - 1) % len(self.buffers)]


def build(nc, a, out):
    with ExitStack() as whole:
        Program(nc, a, out, whole)


class Program:
    def __init__(self, nc, a, out, whole):
        self.nc, self.a = nc, a
        sb = lambda name, shape: whole.enter_context(nc.sbuf_tensor(name, shape, F32))
        sem = lambda name: whole.enter_context(nc.semaphore(name))
        self.pe = Engine(nc.tensor, sem("pe_marks"))
        self.dve = Engine(nc.vector, sem("dve_marks"))
        self.act = Engine(nc.scalar, sem("act_marks"))
        self.pool = Engine(nc.gpsimd, sem("pool_marks"))
        self.sp = Engine(nc.sync, sem("sp_marks"))
        banks = [whole.enter_context(nc.psum_tensor(f"bank{i}", [P, 512], F32)) for i in range(8)]
        self.products = Turn(banks[0:2])
        self.mod_banks = Turn(banks[2:3])
        self.scores = Turn(banks[3:5])
        self.turned = Turn(banks[5:7])
        self.values = Turn(banks[7:8])
        self.raw = Turn([sb(f"weights{i}", [P, SLOT]) for i in range(RAW_SLOTS)])
        for i, s in enumerate(self.raw.buffers):
            s.semaphore, s.loads = sem(f"weights{i}_loaded"), 0
        sb_r = lambda name, shape: whole.enter_context(nc.sbuf_tensor(name, shape, F32R))
        self.split = Turn([(sb_r(f"weights_hi{i}", [P, SLOT]), sb_r(f"weights_lo{i}", [P, SLOT]))
                           for i in range(SPLIT_SLOTS)])

        self.const = {"both": sb("constants", [P, columns(CONST_SIZES["both"])[1]])}
        self.small = sb("small_parameters", [P, SMALL_N])
        self.h = sb("h", [P, DC, T])
        self.diagonal = sb("diagonal", [P, P])
        self.loaded, self.x_loaded = sem("parameters_loaded"), sem("x_loaded")

        self.stats = Turn([sb(f"statistics{i}", [P, 3, 8]) for i in range(2)])

        self.mods = sb("modulations", [P, DEPTH * 72 + 16])
        self.mod_sum = Turn([sb(f"mod_sum{i}", [P, 256]) for i in range(2)])
        self.cond = sb("cond", [P, DC])
        self.mod_ready = {}
        self.mod_todo = [("ada_w", l, j) for l in range(DEPTH) for j in range(36)]
        self.mod_todo += [("final_ada_w", DEPTH, j) for j in range(8)]
        self.diagonal_free, self.mods_pause = None, False
        self.since_mod, self.mod_scaled, self.mod_summed = 0, [], []
        self.planned, self.prepared = list(plan(a)), []

        with ExitStack() as stack:
            self.first_stack(stack)
        with ExitStack() as stack:
            self.second_stack(stack, out)

    def k(self, name, i=None, n=None):
        group, at = CONST_AT[name]
        at += i or 0
        size = n if n is not None else (1 if i is not None else CONST_WIDTH[name])
        return self.const[group][:, at:at + size]

    def load_constants(self, stack, group):
        nc = self.nc
        self.const[group] = stack.enter_context(
            nc.sbuf_tensor(f"constants_{group}", [P, columns(CONST_SIZES[group])[1]], F32))
        semaphore = stack.enter_context(nc.semaphore(f"constants_{group}_loaded"))
        nc.sync.dma_start(self.const[group][:, :], self.a[f"constants_{group}"]).then_inc(semaphore, 16)
        self.const_loaded = (semaphore, 16)

    def s(self, name, n=1, i=0):
        at = SMALL_AT[name] + i
        return self.small[:, at:at + n]

    def load(self, source, rows, cols):
        slot = self.raw.take()
        kc = rows // P
        self.sp.wait(slot.free)
        slot.view = slot.tile[:, 0:kc * cols].rearrange("p (k n) -> p k n", k=kc)
        self.nc.sync.dma_start(slot.view, source.rearrange("(k p) n -> p k n", p=P)).then_inc(slot.semaphore, 16)
        slot.loads += 1
        slot.loaded = (slot.semaphore, 16 * slot.loads)
        return slot

    def prepare(self):
        if not self.planned:
            return
        key, source, rows, cols = self.planned.pop(0)
        nc, kc = self.nc, rows // P
        raw, slot = self.load(source, rows, cols), self.split.take()
        n = kc * cols
        hi, lo = slot.tile
        self.act.wait(raw.loaded, slot.free)
        mark = self.act.done(nc.scalar.copy(hi[:, 0:n], raw.tile[:, 0:n]))
        self.dve.wait(mark)
        raw.free = slot.ready = self.dve.done(nc.vector.tensor_tensor(
            lo[:, 0:n], raw.tile[:, 0:n], hi[:, 0:n].bitcast(F32), ALU.subtract))
        slot.hi, slot.lo = (t[:, 0:n].rearrange("p (k n) -> p k n", k=kc) for t in (hi, lo))
        slot.key = key
        self.prepared.append(slot)

    def weights(self, key):
        while len(self.prepared) <= AHEAD and self.planned:
            self.prepare()
        slot = self.prepared.pop(0)
        assert slot.key == key, (slot.key, key)
        self.pe.wait(slot.ready)
        return slot

    def product(self, out, pairs, start=True, stop=True, **more):
        for i, (lhsT, rhs) in enumerate(pairs):
            last = self.nc.tensor.matmul(out, lhsT, rhs, start=start and i == 0,
                                         stop=stop and i == len(pairs) - 1, **more)
        return last

    def split_product(self, out, pairs, start=True, stop=True, **more):
        n = len(pairs)
        for i, ((a_hi, a_lo), (b_hi, b_lo)) in enumerate(pairs):
            self.nc.tensor.matmul(out, a_hi, b_hi, start=start and i == 0, stop=False, **more)
            self.nc.tensor.matmul(out, a_hi, b_lo, start=False, stop=False, **more)
            last = self.nc.tensor.matmul(out, a_lo, b_hi, start=False, stop=stop and i == n - 1, **more)
        return last

    def split_values(self, dst, index, source, ready):
        self.act.wait(ready)
        mark = self.act.done(self.nc.scalar.copy(dst.hi[index], source))
        self.dve.wait(mark)
        return self.dve.done(self.nc.vector.tensor_tensor(
            dst.lo[index], source, dst.hi[index].bitcast(F32), ALU.subtract))

    def dense(self, keys, x, x_ready, evacuate, first=0):
        at = first
        for key in keys:
            slot = self.weights(key)
            kc, cols = slot.hi.shape[1], slot.hi.shape[2]
            blocks = cols // P
            for b in range(0, blocks, 2):
                bank = self.products.take()
                self.pe.wait(bank.free)
                n = min(2, blocks - b)
                for j in range(n):
                    at_cols = slice((b + j) * P, (b + j + 1) * P)
                    for k in range(kc):
                        self.pe.wait(x_ready[k] if isinstance(x_ready, list) else x_ready)
                        last = self.split_product(
                            bank.tile[:, j * T:(j + 1) * T],
                            [((slot.hi[:, k, at_cols], slot.lo[:, k, at_cols]), (x.hi[:, k, :], x.lo[:, k, :]))],
                            start=k == 0, stop=k == kc - 1)
                slot.free = mark = self.pe.done(last)
                bank.free = evacuate(bank.tile, at, n, mark)
                at += n
                yield
            self.count_unit()

    def token_major(self, keys, x, x_ready, evacuate):
        for u, key in enumerate(keys):
            slot = self.weights(key)
            kc = slot.hi.shape[1]
            bank = self.products.take()
            self.pe.wait(x_ready, bank.free)
            for b in range(TB):
                tok = slice(b * P, (b + 1) * P)
                last = self.split_product(
                    bank.tile[:, b * 256:(b + 1) * 256],
                    [((x.hi[:, k, tok], x.lo[:, k, tok]), (slot.hi[:, k, :], slot.lo[:, k, :])) for k in range(kc)])
            slot.free = mark = self.pe.done(last)
            bank.free = evacuate(bank.tile, u, mark)
            self.count_unit()
            yield

    def accumulate(self, slot, banks, x, pair, pair_ready, first, last):
        self.pe.wait(pair_ready)
        for c in range(DC):
            bank = banks[c // 2]
            if first:
                self.pe.wait(bank.free)
            cols = slice(c * P, (c + 1) * P)
            m = self.split_product(
                bank.tile[:, (c % 2) * T:(c % 2 + 1) * T],
                [((slot.hi[:, k, cols], slot.lo[:, k, cols]), (x.hi[:, pair + k, :], x.lo[:, pair + k, :]))
                 for k in range(2)],
                start=first and c % 2 == 0, stop=last and c % 2 == 1, skip_group_check=True)
            if last and c % 2 == 1:
                bank.ready = self.pe.done(m)
        slot.free = bank.ready if last else self.pe.done(m)
        self.count_unit()

    def count_unit(self):
        if self.mods_pause:
            return
        self.since_mod += 1
        self.add_mod_bias()
        if self.since_mod >= self.mod_every:
            self.since_mod = 0
            self.mod_step()

    def add_mod_bias(self):
        if self.mod_summed:
            bank, at, bias = self.mod_summed.pop(0)
            self.dve.wait(bank.ready)
            bank.free = self.mod_last = self.dve.done(self.nc.vector.tensor_tensor(
                self.mods[:, at:at + 2], bank.tile[:, 0:2], bias, ALU.add))

    def mod_step(self):
        nc = self.nc
        self.add_mod_bias()
        if self.mod_scaled:
            total, at, bias = self.mod_scaled.pop(0)
            bank = self.mod_banks.take()
            self.pe.wait(total.ready, bank.free)
            for i in range(2):
                last = nc.tensor.matmul(bank.tile[:, i:i + 1], total.tile[:, i * P:(i + 1) * P],
                                        self.k("ones", 0), start=True, stop=True)
            total.free = bank.ready = self.pe.done(last)
            self.mod_summed.append((bank, at, bias))
        if not self.mod_todo:
            return
        name, l, j = self.mod_todo.pop(0)
        source = self.a[name][l] if l < DEPTH else self.a[name]
        slot = self.load(source[:, j * 256:(j + 1) * 256], D, 256)
        total = self.mod_sum.take()
        self.dve.wait(slot.loaded, self.cond_ready, total.free)
        mark = self.dve.done(nc.vector.tensor_scalar(
            total.tile[:, :], slot.view[:, 0, :], self.cond[:, 0:1], None, ALU.mult))
        for k in range(1, DC):
            self.dve.wait(mark)
            mark = self.dve.done(nc.vector.scalar_tensor_tensor(
                total.tile[:, :], slot.view[:, k, :], self.cond[:, k:k + 1], total.tile[:, :],
                ALU.mult, ALU.add))
        slot.free = total.ready = mark
        bias = self.s(f"ada_b{l}", 2, 2 * j) if l < DEPTH else self.s("final_ada_b", 2, 2 * j)
        self.mod_scaled.append((total, l * 72 + 2 * j, bias))

    def finish_mods(self, left):
        while len(self.mod_todo) + len(self.mod_scaled) + len(self.mod_summed) > left:
            self.mod_step()

    def inverse_rms(self, squares, groups, per_group, count, eps, ready, ring=None):
        nc, pe, dve, act = self.nc, self.pe, self.dve, self.act
        n = groups * TB
        st = self.stats.take()
        mean, inv, tmp = st.tile[:, 0, 0:n], st.tile[:, 1, 0:n], st.tile[:, 2, 0:n]
        dve.wait(st.free)
        ring = ring or (self.turned if groups == 1 else self.scores)
        for g in range(0, groups, 2):
            sums = ring.take()
            pe.wait(sums.free)
            some = min(2, groups - g)
            for k in range(per_group):
                pe.wait(ready[k] if isinstance(ready, list) else ready)
                rhs = squares[:, k, :] if groups == 1 else squares[:, g:g + 2, :].rearrange("p j t -> p (j t)")
                last = nc.tensor.matmul(sums.tile[:, 0:some * T], self.k("ones"), rhs,
                                        start=k == 0, stop=k == per_group - 1)
            dve.wait(pe.done(last))
            for i in range(some * TB):
                col = g * TB + i
                dve.wait(self.diagonal_free)
                sums.free = self.diagonal_free = dve.done(nc.vector.tensor_tensor_reduce(
                    self.diagonal[:, :], sums.tile[:, i * P:(i + 1) * P], self.k("ident"), 1.0 / count, eps,
                    ALU.mult, ALU.add, mean[:, col:col + 1]))
        act.wait(self.diagonal_free)
        mark = act.done(nc.scalar.activation(tmp, mean, ACT.Sqrt))
        dve.wait(mark)
        dve.wait(dve.done(nc.vector.reciprocal(inv, tmp)))
        dve.wait(dve.done(nc.vector.tensor_tensor(tmp, mean, inv, ALU.mult)))
        dve.wait(dve.done(nc.vector.tensor_tensor(tmp, tmp, inv, ALU.mult)))
        dve.wait(dve.done(nc.vector.tensor_scalar(tmp, tmp, -0.5, 1.5, ALU.mult, ALU.add)))
        mark = dve.done(nc.vector.tensor_tensor(inv, inv, tmp, ALU.mult))
        pe.wait(mark)
        return self.broadcast(st, inv, groups)

    def broadcast(self, st, columns_, groups):
        banks = []
        for g in range(groups):
            if g % 2 == 0:
                bank = self.scores.take()
                self.pe.wait(bank.free)
                banks.append(bank)
            for b in range(TB):
                i = g * TB + b
                last = self.nc.tensor.matmul(
                    bank.tile[:, (g % 2) * T + b * P:(g % 2) * T + (b + 1) * P],
                    columns_[:, i:i + 1].to_broadcast([P, P]), self.k("ident"), start=True, stop=True)
            bank.ready = self.pe.done(last)
        st.free = bank.ready
        return banks

    def square(self, out, in_, ready):
        self.pool.wait(ready)
        self.pool.settle()
        return self.pool.done(self.nc.gpsimd.tensor_tensor(out, in_, in_, ALU.mult))

    def pipeline(self, units, filler):
        active, units = [], list(units)
        while active or units:
            if units:
                active.append(units.pop(0))
            active = [u for u in active if next(u, "ended") != "ended"]
            filler.step()

    def softmax(self, raw, raw_ready, buf, bias_op):
        nc, dve, act = self.nc, self.dve, self.act
        st = buf.stat
        dve.wait(raw_ready, buf.free)
        mark = dve.done(bias_op(buf.tile))
        raw.free = mark
        dve.wait(mark)
        parts = ((0, P), (P, TRI))
        for i, (lo, hi) in enumerate(parts):
            mark = dve.done(nc.vector.tensor_reduce(st[:, i:i + 1], buf.tile[:, lo:hi], AX.X, ALU.max,
                                                    negate=True))
        act.wait(mark)
        for i, (lo, hi) in enumerate(parts):
            mark = act.done(nc.scalar.activation(buf.tile[:, lo:hi], buf.tile[:, lo:hi], ACT.Exp,
                                                 bias=st[:, i:i + 1], accum_out=st[:, 2 + i:3 + i]))
        dve.wait(mark)
        buf.inverted = dve.done(nc.vector.reciprocal(st[:, 4:6], st[:, 2:4]))
        dve.wait(buf.inverted)
        return parts

    def transpose_map(self, probs, ready):
        nc = self.nc
        bank = self.turned.take()
        self.pe.wait(ready, bank.free)
        for i in range(3):
            last = nc.tensor.transpose(bank.tile[:, i * P:(i + 1) * P],
                                       probs.tile[:, i * P:(i + 1) * P], self.k("ident"))
        probs.free = mark = self.pe.done(last)
        pt = self.maps_t.take()
        self.act.wait(mark, pt.free)
        bank.free = pt.ready = self.act.done(nc.scalar.copy(pt.tile[:, :], bank.tile[:, 0:TRI]))
        return pt

    def weigh_values(self, out, v, cols, pt):
        nc = self.nc
        self.pe.wait(pt.ready)
        nc.tensor.matmul(out, v[:, 0, cols], pt.tile[:, 0:T], start=True, stop=False)
        pt.free = mark = self.pe.done(nc.tensor.matmul(
            out[:, P:T], v[:, 1, cols], pt.tile[:, T:TRI], start=False, stop=True))
        return mark

    def rows_of(self, name, l):
        return self.a[name][l]

    def copy_to(self, dst, name, scale=1.0):
        def evacuate(tile, b, n, mark):
            self.act.wait(mark, self.reuse.get(name))
            if n == 2:
                got = self.act.done(self.nc.scalar.activation(
                    dst[:, b:b + 2, :], tile[:, :].rearrange("p (j t) -> p j t", j=2), ACT.Copy, scale=scale))
            else:
                got = self.act.done(self.nc.scalar.activation(dst[:, b, :], tile[:, 0:T], ACT.Copy, scale=scale))
            self.ready[name] = got
            return got
        return evacuate

    def function_to(self, dst, name, func, bias=None):
        def evacuate(tile, b, n, mark):
            self.act.wait(mark, self.reuse.get(name))
            if bias is None:
                got = self.act.done(self.nc.scalar.activation(
                    dst[:, b:b + 2, :], tile[:, :].rearrange("p (j t) -> p j t", j=2), func))
            else:
                for j in range(n):
                    got = self.act.done(self.nc.scalar.activation(
                        dst[:, b + j, :], tile[:, j * T:(j + 1) * T], func, bias=bias(b + j)))
            self.ready[name] = got
            return got
        return evacuate

    def tokens_to(self, dst, name):
        def evacuate(tile, u, mark):
            self.act.wait(mark, self.reuse.get(name))
            self.ready[name] = self.act.done(self.nc.scalar.copy(
                dst[:, :, u * 256:(u + 1) * 256], tile[:, :].rearrange("p (b n) -> p b n", b=TB)))
            return self.ready[name]
        return evacuate

    def first_stack(self, stack):
        nc = self.nc
        sb = lambda name, shape: stack.enter_context(nc.sbuf_tensor(name, shape, F32))
        pair = lambda name, shape: Split(*(stack.enter_context(nc.sbuf_tensor(f"{name}_{part}", shape, F32R))
                                           for part in ("hi", "lo")))
        self.ready, self.reuse = {}, {}
        self.mod_every = 3
        b = self.b = {}
        b["x"] = pair("x", [P, DC, T])
        b["merged"] = sb("a_qk_then_merged", [P, DC, T])
        b["a_q"], b["a_k"] = b["merged"][:, 0:4, :], b["merged"][:, 4:8, :]
        c_qk = sb("latents_then_c_qk", [P, DC, T])
        b["cq"], b["ckv"] = c_qk[:, 0:3, :], c_qk[:, 3:5, :]
        b["c_q"], b["c_k"] = c_qk[:, 0:4, :], c_qk[:, 4:8, :]
        b["a_z"], b["c_z"] = sb("a_z_then_b_z", [P, 4, T]), sb("c_z", [P, 4, T])
        b["a_v"], b["c_v"] = sb("a_v_then_b_v", [P, TB, W]), sb("c_v", [P, TB, W])
        b["b_z"], b["b_v"] = b["a_z"], b["a_v"]
        b["b_q"], b["b_k"] = sb("b_q", [P, HEADS, T]), sb("b_k", [P, HEADS, T])
        b["gate"] = Turn([sb(f"gate{i}", [P, 2 * T]) for i in range(2)])
        b["kr"] = sb("kr", [P, T])
        b["tmp"] = sb("tmp", [P, 2 * T])
        b["pT"] = b["c_q"][:, 0:PLE // P, :]
        b["p"] = pair("p", [P, PLE // P, T])
        y = b["y"] = pair("y", [P, DC + 1, T])
        b["cqn"] = Split(y.hi[:, 4:7, :], y.lo[:, 4:7, :])
        b["ckvn"] = Split(y.hi[:, 7:9, :], y.lo[:, 7:9, :])
        self.maps = Turn([sb(f"map{i}", [P, TRI]) for i in range(4)])
        for i, m in enumerate(self.maps.buffers):
            m.stat = sb(f"map_stat{i}", [P, 8])
        self.maps_t = Turn([sb(f"map_t{i}", [P, TRI]) for i in range(2)])
        b["lam"] = sb("lam", [P, 8])
        b["lam_prod"] = sb("lam_prod", [P, 2, DIFF_QK])
        self.p_sem = stack.enter_context(nc.semaphore("p_loaded"))
        x_dram, x_ready = self.a["x"].rearrange("(c p) t -> p c t", p=P), []
        nc.sync.dma_start(self.h[:, 0:4, :], x_dram[:, 0:4, :]).then_inc(self.x_loaded, 16)
        self.sp.wait((self.x_loaded, 16))
        nc.sync.dma_start(self.h[:, 4:8, :], x_dram[:, 4:8, :]).then_inc(self.x_loaded, 16)
        for c in range(DC):
            x_ready.append(self.split_values(b["x"], (slice(None), c), self.h[:, c, :],
                                             (self.x_loaded, 16 if c < 4 else 32)))
        self.prepare()
        nc.sync.dma_start(self.small[:, :], self.a["small"]).then_inc(self.loaded, 16)
        nc.sync.dma_start(self.const["both"][:, :], self.a["constants_both"]).then_inc(self.loaded, 16)
        self.load_constants(stack, "first")
        self.prepare()
        for e in (self.pe, self.dve, self.act, self.pool):
            e.wait((self.loaded, 32), self.const_loaded)
        self.cond_ready = self.act.done(nc.scalar.activation(self.cond[:, :], self.s("c", 8), ACT.Silu))
        self.h_ready = x_ready
        for l in range(DEPTH):
            self.first_layer(l)
        self.finish_mods(44)

    def first_layer(self, l):
        nc, b, pe, dve, act, pool = self.nc, self.b, self.pe, self.dve, self.act, self.pool
        ready, x, h, x_ready = self.ready, self.b["x"], self.h, self.h_ready

        lam_init = 0.8 - 0.6 * math.exp(-0.3 * l)
        lam, prod = b["lam"], b["lam_prod"]
        lf = self.s(f"lambda{l}", 256).rearrange("p (a b d) -> p a b d", a=2, b=2)
        dve.wait(dve.done(nc.vector.tensor_tensor(prod[:, :, :], lf[:, :, 0, :], lf[:, :, 1, :], ALU.mult)))
        mark = dve.done(nc.vector.tensor_reduce(lam[:, 0:2], prod[:, :, :], AX.X, ALU.add))
        act.wait(mark)
        mark = act.done(nc.scalar.activation(lam[:, 2:4], lam[:, 0:2], ACT.Exp))
        dve.wait(mark)
        dve.wait(dve.done(nc.vector.scalar_tensor_tensor(lam[:, 4:5], lam[:, 3:4], -lam_init, lam[:, 2:3],
                                                         ALU.add, ALU.subtract)))
        mark = dve.done(nc.vector.tensor_scalar(lam[:, 5:6], self.s(f"subln{l}"), 1.0 - lam_init, None, ALU.mult))
        dve.wait(mark)
        neg_lam, subln = lam[:, 4:5], lam[:, 5:6]

        def run(g):
            for _ in g:
                pass
        run(self.dense(keys(f"b_cq{l}", 2), x, x_ready, self.copy_to(b["cq"], "cq")))
        run(self.dense(keys(f"b_ckvr{l}", 1), x, None, self.copy_to(b["ckv"], "ckv")))
        slot = self.weights((f"b_ckvr{l}", 1))
        bank = self.products.take()
        pe.wait(bank.free)
        for j, (lo, hi) in enumerate(((0, P), (64, 160))):
            last = self.split_product(
                bank.tile[0:hi - lo, j * T:(j + 1) * T],
                [((slot.hi[:, k, lo:hi], slot.lo[:, k, lo:hi]), (x.hi[:, k, :], x.lo[:, k, :])) for k in range(DC)])
        slot.free = mark = pe.done(last)
        act.wait(mark)
        act.done(nc.scalar.copy(b["ckv"][:, 1, :], bank.tile[:, 0:T]))
        bank.free = ready["ckv"] = ready["kr"] = act.done(nc.scalar.copy(b["kr"][64:96, :], bank.tile[64:96, T:2 * T]))
        self.count_unit()

        run(self.dense(keys(f"a_q{l}", 2), x, None, self.copy_to(b["a_q"], "a_q", HD ** -0.5)))
        run(self.dense(keys(f"a_k{l}", 2), x, None, self.copy_to(b["a_k"], "a_k")))
        sq_q = self.square(b["b_q"][:, 0:3, :], b["cq"], [ready["cq"], self.reuse.get("b_q")])
        sq_kv = self.square(b["b_k"][:, 0:2, :], b["ckv"], [ready["ckv"], self.reuse.get("b_k")])
        run(self.token_major(keys(f"a_v{l}", 2), x, None, self.tokens_to(b["a_v"], "a_v")))

        def latent_norm(buf, pair, chunks, gain, squares, sq_mark):
            (bank,) = self.inverse_rms(squares, 1, chunks, chunks * P, 1e-6, sq_mark)
            dve.wait(bank.ready)
            for c in range(chunks):
                mark = dve.done(nc.vector.scalar_tensor_tensor(
                    buf[:, c, :], buf[:, c, :], self.s(f"{gain}{l}", 1, c), bank.tile[:, 0:T], ALU.mult, ALU.mult))
            bank.free = mark
            return self.split_values(pair, (slice(None), slice(None)), buf, mark)
        self.act.wait(self.reuse.get("y"))
        ready["cqn"] = latent_norm(b["cq"], b["cqn"], 3, "gq", b["b_q"], sq_q)
        ready["ckvn"] = latent_norm(b["ckv"], b["ckvn"], 2, "gkv", b["b_k"], sq_kv)

        def rope32(raw, heads, mark):
            bank = self.products.take()
            pe.wait(mark, bank.free)
            rows = slice(64, 96)
            n = heads * T
            mark = pe.done(nc.tensor.matmul(bank.tile[rows, 0:n], self.k("swap16")[rows, :], raw,
                                            start=True, stop=True))
            dve.wait(mark, self.reuse.get("tmp"))
            tmp = b["tmp"][rows, 0:n]
            flat = raw.rearrange("p h t -> p (h t)") if heads == 2 else raw
            bank.free = m = dve.done(nc.vector.tensor_tensor(tmp, bank.tile[rows, 0:n], self.k("sin32")[rows, 0:n], ALU.mult))
            m2 = dve.done(nc.vector.tensor_tensor(flat, flat, self.k("cos32")[rows, 0:n], ALU.mult))
            dve.wait(m2)
            self.reuse["tmp"] = dve.done(nc.vector.tensor_tensor(flat, flat, tmp, ALU.add))
            return self.reuse["tmp"]

        def mla_q():
            cq = b["cqn"]
            for u in range(2):
                slot = self.weights((f"uq{l}", u))
                pe.wait(ready["cqn"])
                for h0 in range(0, 4, 2):
                    bank = self.products.take()
                    pe.wait(bank.free)
                    for j in range(2):
                        cols = slice((h0 + j) * 96, (h0 + j + 1) * 96)
                        last = self.split_product(
                            bank.tile[0:96, j * T:(j + 1) * T],
                            [((slot.hi[:, k, cols], slot.lo[:, k, cols]), (cq.hi[:, k, :], cq.lo[:, k, :]))
                             for k in range(3)])
                    slot.free = mark = pe.done(last)
                    act.wait(mark)
                    hh = 4 * u + h0
                    bank.free = mark = act.done(nc.scalar.copy(
                        b["b_q"][0:96, hh:hh + 2, :], bank.tile[0:96, :].rearrange("p (j t) -> p j t", j=2)))
                    ready["b_q"] = rope32(b["b_q"][64:96, hh:hh + 2, :], 2, mark)
                    yield
                self.count_unit()

        def mla_kv():
            mark = rope32(b["kr"][64:96, :], 1, ready["kr"])
            slot = self.weights((f"ukv{l}", 0))
            hi, lo = (t.rearrange("p k (h c) -> p k h c", h=HEADS) for t in (slot.hi, slot.lo))
            ckv = b["ckvn"]
            pool.wait(mark)
            for h in range(HEADS):
                pool.settle()
                ready["b_k_rope"] = pool.done(nc.gpsimd.tensor_copy(b["b_k"][64:96, h, :], b["kr"][64:96, :]))
            pe.wait(ready["ckvn"])
            for h in range(0, HEADS, 2):
                bank = self.products.take()
                pe.wait(bank.free)
                for j in range(2):
                    cols = slice((h + j) * P, (h + j + 1) * P)
                    last = self.split_product(
                        bank.tile[:, j * T:(j + 1) * T],
                        [((slot.hi[:, k, cols], slot.lo[:, k, cols]), (ckv.hi[:, k, :], ckv.lo[:, k, :]))
                         for k in range(2)])
                mark = pe.done(last)
                act.wait(mark)
                bank.free = ready["b_k"] = act.done(nc.scalar.copy(
                    b["b_k"][0:64, h:h + 2, :], bank.tile[0:64, :].rearrange("p (j t) -> p j t", j=2)))
                if h % 4 == 2:
                    yield
            for t in range(TB):
                bank = self.products.take()
                pe.wait(bank.free)
                tok = slice(t * P, (t + 1) * P)
                last = self.split_product(
                    bank.tile[:, :].rearrange("p (h c) -> p h c", h=HEADS),
                    [((ckv.hi[:, k, tok], ckv.lo[:, k, tok]), (hi[:, k, :, NOPE:P], lo[:, k, :, NOPE:P]))
                     for k in range(2)])
                slot.free = mark = pe.done(last)
                act.wait(mark, self.reuse.get("b_v"))
                bank.free = ready["b_v"] = act.done(nc.scalar.copy(b["b_v"][:, t, :], bank.tile[:, :]))
            self.count_unit()
            yield

        merged, y = b["merged"], b["y"]

        def merge(i, branch, y_at, y_ready):
            state = {}

            def gate(tile, at, n, mark):
                buf = b["gate"].take()
                act.wait(mark, buf.free)
                for j in range(n):
                    got = act.done(nc.scalar.activation(
                        buf.tile[:, j * T:(j + 1) * T], tile[:, j * T:(j + 1) * T], ACT.Sigmoid,
                        bias=self.s(f"b_merge{l}", 1, i * DC + at + j)))
                state["gate"], state["ready"] = buf, got
                return got

            def weigh(tile, at, n, mark):
                buf = state["gate"]
                m = merged[:, at:at + 2, :].rearrange("p j t -> p (j t)")
                dve.wait(mark, state["ready"])
                if i == 0:
                    buf.free = ready["merged"] = dve.done(nc.vector.tensor_tensor(m, tile[:, :], buf.tile[:, :], ALU.mult))
                    return buf.free
                dve.wait(ready["merged"])
                got = dve.done(nc.vector.tensor_tensor(buf.tile[:, :], tile[:, :], buf.tile[:, :], ALU.mult))
                dve.wait(got)
                buf.free = ready["merged"] = dve.done(nc.vector.tensor_tensor(m, m, buf.tile[:, :], ALU.add))
                return got

            branch_x = Split(y.hi[:, y_at:y_at + 4, :], y.lo[:, y_at:y_at + 4, :])
            for j in range(DC // MERGE_BLOCKS):
                while y_ready not in ready:
                    yield
                yield from self.dense([(f"gate_{branch}{l}", j)], x, None, gate, first=MERGE_BLOCKS * j)
                yield from self.dense([(f"branch_{branch}{l}", j)], branch_x, ready[y_ready], weigh, first=MERGE_BLOCKS * j)
            self.reuse[y_ready] = slot_mark(self)

        def slot_mark(self):
            return (pe.semaphore, pe.count)

        def fill():
            k2 = lambda n: keys(f"{n}{l}", 2)
            yield from self.dense(k2("a_z"), x, None, self.function_to(b["a_z"], "a_z", ACT.Silu))
            self.reuse["c_q"] = self.reuse["c_k"] = [ready["cqn"], ready["ckvn"]]
            yield from self.dense(k2("c_q"), x, None, self.copy_to(b["c_q"], "c_q", DIFF_QK ** -0.5))
            yield from self.dense(k2("c_k"), x, None, self.copy_to(b["c_k"], "c_k"))
            yield from self.token_major(k2("c_v"), x, None, self.tokens_to(b["c_v"], "c_v"))
            yield from self.dense(k2("c_z"), x, None, self.function_to(b["c_z"], "c_z", ACT.Silu))
            yield "differential attention can start"
            yield from merge(0, "a", 0, "ya")
            yield from mla_q()
            yield from mla_kv()
            yield from self.dense(k2("b_z"), x, None, self.function_to(b["b_z"], "b_z", ACT.Silu))
            yield "MLA can start"
            yield from merge(2, "c", 4, "ycn")
        filler = Filler(fill())

        state = {}

        def moba(h):
            rows, c = slice(64 * (h % 2), 64 * (h % 2) + 64), h // 2
            raw, probs = self.scores.take(), self.maps.take()
            pe.wait(ready["a_q"], ready["a_k"], raw.free)
            q, k_ = b["a_q"], b["a_k"]
            nc.tensor.matmul(raw.tile[:, 0:P], q[rows, c, 0:P], k_[rows, c, 0:P], start=True, stop=True)
            mark = pe.done(nc.tensor.matmul(raw.tile[:, P:TRI], q[rows, c, P:T], k_[rows, c, :], start=True, stop=True))
            parts = self.softmax(raw, mark, probs, lambda o: nc.vector.scalar_tensor_tensor(
                o[:, :], self.k("dist"), -float(MOBA_SLOPES[h]), raw.tile[:, 0:TRI], ALU.mult, ALU.add))
            mark = self.normalise(probs, parts)
            yield
            yield
            pt = self.transpose_map(probs, mark)
            yield
            if h % 2 == 0:
                state["bank"] = self.values.take()
                pe.wait(state["bank"].free)
            bank = state["bank"]
            mark = self.weigh_values(bank.tile[rows, 0:T], b["a_v"], slice(h * HD, (h + 1) * HD), pt)
            if h % 2 == 1:
                dve.wait(mark, ready["a_z"])
                bank.free = m = dve.done(nc.vector.tensor_tensor(
                    b["a_z"][:, c, :], bank.tile[:, 0:T], b["a_z"][:, c, :], ALU.mult))
                act.wait(self.reuse.get("y"))
                ya = self.split_values(y, (slice(None), c), b["a_z"][:, c, :], m)
                if h == HEADS - 1:
                    ready["ya"] = ya
        self.pipeline([moba(h) for h in range(HEADS)], filler)
        self.reuse["b_v"] = self.reuse["b_z"] = self.reuse["ya_done"] = ready["ya"]

        filler.until("differential attention can start")
        yc = b["c_q"]
        yc_sq = b["c_k"]

        def diff(h):
            p_maps = []
            for m in range(2):
                rows = slice(64 * m, 64 * m + 64)
                raw, probs = self.scores.take(), self.maps.take()
                pe.wait(ready["c_q"], ready["c_k"], raw.free)
                q, k_ = b["c_q"], b["c_k"]
                nc.tensor.matmul(raw.tile[:, 0:P], q[rows, h, 0:P], k_[rows, h, 0:P], start=True, stop=True)
                mark = pe.done(nc.tensor.matmul(raw.tile[:, P:TRI], q[rows, h, P:T], k_[rows, h, :], start=True, stop=True))
                parts = self.softmax(raw, mark, probs, lambda o: nc.vector.scalar_tensor_tensor(
                    o[:, :], self.k("dist"), -float(DIFF_SLOPES[h]), raw.tile[:, 0:TRI], ALU.mult, ALU.add))
                p_maps.append(probs)
                if m == 0:
                    normalised = self.normalise(probs, parts)
            st = p_maps[1].stat
            dve.wait(dve.done(nc.vector.tensor_scalar(st[:, 6:8], st[:, 4:6], neg_lam, None, ALU.mult)))
            first, second = p_maps
            dve.wait(normalised)
            for i, (lo, hi) in enumerate(parts):
                mark = dve.done(nc.vector.scalar_tensor_tensor(
                    first.tile[:, lo:hi], second.tile[:, lo:hi], st[:, 6 + i:7 + i], first.tile[:, lo:hi],
                    ALU.mult, ALU.add))
            second.free = mark
            yield
            pt = self.transpose_map(first, mark)
            yield
            bank = self.values.take()
            pe.wait(bank.free)
            mark = self.weigh_values(bank.tile[:, 0:T], b["c_v"], slice(h * P, (h + 1) * P), pt)
            act.wait(mark)
            bank.free = ready["yc"] = mark = act.done(nc.scalar.copy(yc[:, h, :], bank.tile[:, 0:T]))
            ready["yc_sq"] = self.square(yc_sq[:, h, :], yc[:, h, :], mark)
        self.pipeline([diff(h) for h in range(DIFF_HEADS)], filler)

        filler.until("MLA can start")

        def mla(h):
            raw, probs = self.scores.take(), self.maps.take()
            pe.wait(ready["b_q"], ready["b_k"], ready["b_k_rope"], raw.free)
            q, k_ = b["b_q"], b["b_k"]
            nc.tensor.matmul(raw.tile[:, 0:P], q[0:96, h, 0:P], k_[0:96, h, 0:P], start=True, stop=True)
            mark = pe.done(nc.tensor.matmul(raw.tile[:, P:TRI], q[0:96, h, P:T], k_[0:96, h, :], start=True, stop=True))
            parts = self.softmax(raw, mark, probs, lambda o: nc.vector.scalar_tensor_tensor(
                o[:, :], raw.tile[:, 0:TRI], (NOPE + ROPE) ** -0.5, self.k("causal"), ALU.mult, ALU.add))
            mark = self.normalise(probs, parts)
            yield
            yield
            pt = self.transpose_map(probs, mark)
            yield
            rows, c = slice(64 * (h % 2), 64 * (h % 2) + 64), h // 2
            if h % 2 == 0:
                state["bank"] = self.values.take()
                pe.wait(state["bank"].free)
            bank = state["bank"]
            mark = self.weigh_values(bank.tile[rows, 0:T], b["b_v"], slice(h * HD, (h + 1) * HD), pt)
            if h % 2 == 1:
                dve.wait(mark, ready["b_z"])
                bank.free = m = dve.done(nc.vector.tensor_tensor(
                    b["b_z"][:, c, :], bank.tile[:, 0:T], b["b_z"][:, c, :], ALU.mult))
                act.wait(self.reuse["ya"])
                yb = self.split_values(y, (slice(None), c), b["b_z"][:, c, :], m)
                if h == HEADS - 1:
                    ready["yb"] = yb
        act.wait(ready["b_q"], ready["b_v"])
        banks = self.inverse_rms(yc_sq, 4, 1, P, 1e-5, ready["yc_sq"])
        for g in range(0, 4, 2):
            bank = banks[g // 2]
            both = yc[:, g:g + 2, :].rearrange("p j t -> p (j t)")
            z = b["c_z"][:, g:g + 2, :].rearrange("p j t -> p (j t)")
            dve.wait(bank.ready, ready["yc"], ready["c_z"])
            bank.free = mark = dve.done(nc.vector.tensor_tensor(both, both, bank.tile[:, :], ALU.mult))
            dve.wait(mark)
            mark = dve.done(nc.vector.scalar_tensor_tensor(z, both, subln, z, ALU.mult, ALU.mult))
            ycn = self.split_values(y, (slice(None), slice(4 + g, 6 + g)), b["c_z"][:, g:g + 2, :], mark)
        ready["ycn"] = ycn
        self.pipeline([mla(h) for h in range(HEADS)], filler)
        while filler.step():
            pass
        self.sp.wait(ready["ycn"])
        nc.sync.dma_start(b["pT"], self.a["p"][l].rearrange("(c p) t -> p c t", p=P)).then_inc(self.p_sem, 16)
        p_loaded = (self.p_sem, 16 * (l + 1))
        run(merge(1, "b", 0, "yb"))
        self.reuse["a_z"] = self.reuse["c_z"] = self.reuse["a_v"] = self.reuse["c_v"] = ready["yb"]

        act.wait(self.reuse["yb"], self.reuse["ycn"])
        merged_ready = []
        for c in range(DC):
            merged_ready.append(self.split_values(y, (slice(None), c), merged[:, c, :], ready["merged"]))
        pp = b["b_k"]
        p_ready = self.split_values(b["p"], (slice(None), slice(None)), b["pT"], p_loaded)
        self.reuse["cq"] = p_ready
        run(self.dense(keys(f"ple{l}", 1), b["p"], p_ready, self.copy_to(pp, "pp")))

        r_ready = []

        def residual(tile, at, n, mark):
            r = h[:, at:at + 2, :].rearrange("p j t -> p (j t)")
            dve.wait(mark)
            got = dve.done(nc.vector.scalar_tensor_tensor(r, r, ALPHA, tile[:, :], ALU.mult, ALU.add))
            for j in range(2):
                r_ready.append(self.split_values(x, (slice(None), at + j), h[:, at + j, :], got))
            return got
        run(self.dense(keys(f"w_out{l}", 4), y, merged_ready, residual))
        self.reuse["y"] = (pe.semaphore, pe.count)
        r2, sg, r2_ready = b["b_q"], b["merged"], []

        def ple(tile, c, n, mark):
            act.wait(mark, merged_ready[-1])
            s_ = sg[:, c:c + 2, :].rearrange("p j t -> p (j t)")
            q_ = pp[:, c:c + 2, :].rearrange("p j t -> p (j t)")
            r_ = h[:, c:c + 2, :].rearrange("p j t -> p (j t)")
            o_ = r2[:, c:c + 2, :].rearrange("p j t -> p (j t)")
            got = act.done(nc.scalar.activation(s_, tile[:, :], ACT.Sigmoid))
            dve.wait(got, ready["pp"])
            dve.wait(dve.done(nc.vector.tensor_tensor(s_, s_, q_, ALU.mult)))
            r2_ready.extend([dve.done(nc.vector.tensor_tensor(o_, s_, r_, ALU.add))] * 2)
            return got
        run(self.dense(keys(f"ple_gate{l}", 4), x, r_ready, ple))

        bank = self.turned.take()
        pe.wait(bank.free)
        for k in range(DC):
            pe.wait(r2_ready[k])
            last = nc.tensor.matmul(bank.tile[:, 0:T], self.k("ones"), r2[:, k, :], start=k == 0, stop=k == DC - 1)
        dve.wait(pe.done(last))
        sq, sq_ready = b["merged"], []
        for c in range(DC):
            bank.free = mark = dve.done(nc.vector.scalar_tensor_tensor(
                r2[:, c, :], bank.tile[:, 0:T], -1.0 / D, r2[:, c, :], ALU.mult, ALU.add))
            act.wait(mark)
            sq_ready.append(act.done(nc.scalar.activation(sq[:, c, :], r2[:, c, :], ACT.Square)))
        (bank,) = self.inverse_rms(sq, 1, DC, D, 1e-5, sq_ready)
        self.h_ready = []
        dve.wait(bank.ready)
        for c in range(DC):
            mark = dve.done(nc.vector.scalar_tensor_tensor(
                r2[:, c, :], r2[:, c, :], self.s(f"ln_g{l}", 1, c), bank.tile[:, 0:T], ALU.mult, ALU.mult))
            bank.free = mark
            act.wait(mark)
            got = act.done(nc.scalar.activation(
                h[:, c, :], r2[:, c, :], ACT.Identity, bias=self.s(f"ln_b{l}", 1, c)))
            if l < DEPTH - 1:
                got = self.split_values(x, (slice(None), c), h[:, c, :], got)
            self.h_ready.append(got)
        self.reuse["b_q"] = self.reuse["b_k"] = self.reuse["cq"] = self.reuse["ckv"] = self.h_ready[-1]
        self.reuse["a_q"] = self.reuse["a_k"] = self.h_ready[-1]

    def normalise(self, probs, parts):
        self.act.wait(probs.inverted)
        for i, (lo, hi) in enumerate(parts):
            mark = self.act.done(self.nc.scalar.activation(
                probs.tile[:, lo:hi], probs.tile[:, lo:hi], ACT.Copy, scale=probs.stat[:, 4 + i:5 + i]))
        return mark

    def second_stack(self, stack, out):
        nc = self.nc
        sb = lambda name, shape: stack.enter_context(nc.sbuf_tensor(name, shape, F32))
        self.ready, self.reuse = {}, {}
        self.mod_every = 2
        b = self.b = {}
        pair = lambda name, shape: Split(*(stack.enter_context(nc.sbuf_tensor(f"{name}_{part}", shape, F32R))
                                           for part in ("hi", "lo")))
        b["u"] = pair("u", [P, DC, T])
        b["y"] = pair("y2", [P, HIDDEN_BLOCKS, T])
        hidden = [sb(f"hidden{i}", [P, 2 * T]) for i in range(2)]
        b["hidden"] = Turn(hidden)
        b["norm"] = Turn([h_[:, j * T:(j + 1) * T] for h_ in hidden for j in range(2)])
        b["tmp"] = hidden[0]
        for n in ("r_q", "r_k", "r_g", "m_z"):
            b[n] = sb(n, [P, 4, T])
        b["y_r"] = b["r_q"]
        for n in ("r_v", "s_v"):
            b[n] = sb(n, [P, TB, 512])
        b["squares"] = sb("squares", [P, DC, T])
        b["s_q"], b["s_k"] = b["squares"][:, 0:4, :], b["squares"][:, 4:8, :]
        xbc_in = sb("xbc_in", [P, XBC // P * (T + TAPS - 1)])
        b["xbc_in"] = xbc_in[:, :].rearrange("p (c t) -> p c t", c=XBC // P)
        b["xbc"] = sb("xbc", [P, XBC // P, T])
        b["m_v"] = xbc_in[:, 0:1024].rearrange("p (b n) -> p b n", b=TB)
        b["y_m"] = xbc_in[:, 1024:2048].rearrange("p (c t) -> p c t", c=4)
        b["dt"] = sb("dt", [P, 6, 2 * MH])
        b["cum"] = sb("cum", [P, 4, MH])
        b["neg_a"] = sb("neg_a", [P, MH])
        b["cb"] = sb("keep_then_cb", [P, MG, TRI])
        b["coef"] = sb("coef", [P, 4, DC])
        self.sp.wait(self.h_ready)
        self.load_constants(stack, "second")
        for e in (self.pe, self.dve, self.act, self.pool):
            e.wait(self.const_loaded)
        self.maps = Turn([sb(f"work{i}", [P, TRI]) for i in range(3)])
        self.keep = Turn([b["cb"][:, i, :] for i in range(2)])
        self.maps_t = Turn([sb(f"weights_t{i}", [P, TRI]) for i in range(4)])
        self.dve.wait(self.h_ready)
        self.pool.wait(self.h_ready)
        self.act.wait(self.h_ready)
        self.sp.wait(self.h_ready)
        for l in range(DEPTH):
            self.second_layer(l)
        self.finish_mods(0)
        marks = self.modulated_norm("final_norm", DEPTH * 72, DEPTH * 72 + 8, None)
        written = stack.enter_context(nc.semaphore("written"))
        for c in range(0, DC, 2):
            self.sp.wait(marks[c + 1])
            nc.sync.dma_start(out.rearrange("(c p) t -> p c t", p=P)[:, c:c + 2, :],
                              self.b["xbc"][:, c:c + 2, :]).then_inc(written, 16)
        nc.sync.wait_ge(written, 16 * (DC // 2))

    def modulated_norm(self, gain, shift_at, scale_at, dst):
        nc, b, dve, act = self.nc, self.b, self.dve, self.act
        h, coef, sq = self.h, b["coef"], []
        for c in range(DC):
            act.wait(self.h_ready[c], self.reuse.get("squares"))
            sq.append(act.done(nc.scalar.activation(b["squares"][:, c, :], h[:, c, :], ACT.Square)))
        dve.wait(self.mod_last, self.reuse.get("coef"))
        dve.wait(dve.done(nc.vector.scalar_tensor_tensor(
            coef[:, 0, :], self.mods[:, scale_at:scale_at + DC], 1.0, self.s(gain, DC), ALU.add, ALU.mult)))
        (bank,) = self.inverse_rms(b["squares"], 1, DC, D, 1e-6, sq, ring=self.values)
        self.reuse["squares"] = bank.ready
        marks = []
        dve.wait(bank.ready)
        act.wait(self.reuse.get("u"))
        for c in range(DC):
            shift = self.mods[:, shift_at + c:shift_at + c + 1]
            buf = b["norm"].take()
            dve.wait(buf.free)
            bank.free = mark = dve.done(nc.vector.scalar_tensor_tensor(
                buf.tile, h[:, c, :], coef[:, 0, c:c + 1], bank.tile[:, 0:T], ALU.mult, ALU.mult))
            act.wait(mark)
            if dst is None:
                marks.append(act.done(nc.scalar.activation(b["xbc"][:, c, :], buf.tile, ACT.Identity, bias=shift)))
                buf.free = marks[-1]
                continue
            got = act.done(nc.scalar.activation(dst.hi[:, c, :], buf.tile, ACT.Identity, bias=shift))
            dve.wait(got)
            buf.free = dve.done(nc.vector.scalar_tensor_tensor(
                dst.lo[:, c, :], buf.tile, shift, dst.hi[:, c, :].bitcast(F32), ALU.add, ALU.subtract))
            marks.append(buf.free)
        return marks

    def run(self, g):
        for _ in g:
            pass

    def feed_forward(self, l, n, gain, at):
        nc, b, pe, dve, act = self.nc, self.b, self.pe, self.dve, self.act
        u, ff = b["u"], b["y"]
        marks = self.modulated_norm(gain, at, at + DC, u)
        dve.wait(dve.done(nc.vector.tensor_scalar(b["coef"][:, 1, :], self.mods[:, at + 2 * DC:at + 3 * DC],
                                                  0.5, 0.5, ALU.mult, ALU.add)))
        banks = [self.scores.take(), self.scores.take(), self.turned.take(), self.turned.take()]
        pairs = FC // 2
        places = HIDDEN_BLOCKS // 2
        hidden_ready, place_free = {}, [self.reuse.get("y")] * places
        state = {}

        def gate(tile, blk, m, mark):
            buf = b["hidden"].take()
            act.wait(mark, buf.free)
            state["buf"] = buf
            state["gate"] = act.done(nc.scalar.activation(buf.tile[:, :], tile[:, :], ACT.Silu))
            return state["gate"]

        def up(i):
            def evacuate(tile, blk, m, mark):
                buf = state["buf"]
                dve.wait(mark, state["gate"])
                got = dve.done(nc.vector.tensor_tensor(buf.tile[:, :], tile[:, :], buf.tile[:, :], ALU.mult))
                act.wait(place_free[i % places])
                at_ = 2 * (i % places)
                buf.free = hidden_ready[i] = self.split_values(
                    ff, (slice(None), slice(at_, at_ + 2)), buf.tile[:, :].rearrange("p (j t) -> p j t", j=2), got)
                return got
            return evacuate
        for i in range(pairs + 1):
            if i < pairs:
                self.run(self.dense([(f"wg{n}{l}", i)], u, marks, gate))
                self.run(self.dense([(f"wu{n}{l}", i)], u, None, up(i)))
            if i > 0:
                slot = self.weights((f"wd{n}{l}", i - 1))
                self.accumulate(slot, banks, ff, 2 * ((i - 1) % places), hidden_ready[i - 1], i == 1, i == pairs)
                place_free[(i - 1) % places] = slot.free
        self.reuse["y"] = self.reuse["u"] = slot.free
        self.add_to_h(banks)

    def add_to_h(self, banks):
        h, dve = self.h, self.dve
        self.h_ready = []
        for c in range(DC):
            bank = banks[c // 2]
            dve.wait(bank.ready)
            bank.free = got = dve.done(self.nc.vector.scalar_tensor_tensor(
                h[:, c, :], bank.tile[:, (c % 2) * T:(c % 2 + 1) * T], self.b["coef"][:, 1, c:c + 1], h[:, c, :],
                ALU.mult, ALU.add))
            self.h_ready.append(got)

    def second_layer(self, l):
        self.finish_mods(44 if l == 0 else 8)
        at = 72 * l
        self.feed_forward(l, 1, f"norm_ffn1{l}", at)
        self.mixers(l, at + 3 * DC)
        self.feed_forward(l, 2, f"norm_ffn2{l}", at + 6 * DC)

    def mixers(self, l, at):
        nc, b, pe, dve, act, pool = self.nc, self.b, self.pe, self.dve, self.act, self.pool
        ready, u, h, y, y_m, y_r = self.ready, b["u"], self.h, b["y"], b["y_m"], b["y_r"]
        marks = self.modulated_norm(f"norm_mix{l}", at, at + DC, u)
        dve.wait(dve.done(nc.vector.tensor_scalar(b["coef"][:, 1, :], self.mods[:, at + 2 * DC:at + 3 * DC],
                                                  1.0, None, ALU.add)))
        k2 = lambda n: keys(f"{n}{l}", 2)

        dve.wait(self.reuse.get("xbc_in"))
        self.pad_ready = dve.done(nc.vector.memset(b["xbc_in"][:, :, 0:TAPS - 1], 0.0))
        def conv_in(base):
            def evacuate(tile, blk, n, mark):
                act.wait(mark, self.pad_ready)
                got = act.done(nc.scalar.copy(b["xbc_in"][:, base + blk:base + blk + 2, TAPS - 1:],
                                              tile[:, :].rearrange("p (j t) -> p j t", j=2)))
                dve.wait(got)
                for c in (base + blk, base + blk + 1):
                    src, dst = b["xbc_in"], b["xbc"]
                    tap = lambda i: self.s(f"conv_w{l}", 1, 8 * i + c)
                    m = dve.done(nc.vector.tensor_scalar(dst[:, c, :], src[:, c, 0:T], tap(0), None, ALU.mult))
                    for i in range(1, TAPS):
                        dve.wait(m)
                        m = dve.done(nc.vector.scalar_tensor_tensor(
                            dst[:, c, :], src[:, c, i:i + T], tap(i), dst[:, c, :], ALU.mult, ALU.add))
                    act.wait(m)
                    ready["xbc"] = act.done(nc.scalar.activation(dst[:, c, :], dst[:, c, :], ACT.Silu,
                                                                 bias=self.s(f"conv_b{l}", 1, c)))
                return got
            return evacuate
        self.run(self.dense(k2("m_x"), u, marks, conv_in(0)))
        self.run(self.dense(k2("m_bc"), u, None, conv_in(4)))

        slot = self.weights((f"m_dt{l}", 0))
        bank = self.products.take()
        pe.wait(bank.free)
        for t in range(TB):
            tok = slice(t * P, (t + 1) * P)
            last = self.split_product(
                bank.tile[:, t * MH:(t + 1) * MH],
                [((u.hi[:, k, tok], u.lo[:, k, tok]), (slot.hi[:, k, :], slot.lo[:, k, :])) for k in range(DC)])
        slot.free = mark = pe.done(last)
        self.count_unit()
        z, az, ez, lz, dt, da = (b["dt"][:, i, :] for i in range(6))
        dve.wait(mark)
        for t in range(TB):
            bank.free = m = dve.done(nc.vector.tensor_tensor(
                z[:, t * MH:(t + 1) * MH], bank.tile[:, t * MH:(t + 1) * MH], self.s(f"dt_bias{l}", MH), ALU.add))
        act.wait(m)
        act.wait(act.done(nc.scalar.activation(az, z, ACT.Abs)))
        act.wait(act.done(nc.scalar.activation(ez, az, ACT.Exp, scale=-1.0)))
        act.done(nc.scalar.activation(b["neg_a"][:, :], self.s(f"a_log{l}", MH), ACT.Exp))
        m = act.done(nc.scalar.activation(lz, ez, ACT.Ln, bias=1.0))
        dve.wait(m)
        dve.wait(dve.done(nc.vector.scalar_tensor_tensor(dt, z, 0.0, lz, ALU.max, ALU.add)))
        for t in range(TB):
            cols = slice(t * MH, (t + 1) * MH)
            da_ready = dve.done(nc.vector.scalar_tensor_tensor(da[:, cols], dt[:, cols], -1.0, b["neg_a"][:, :],
                                                               ALU.mult, ALU.mult))

        def rotate(name):
            for c in range(0, 4, 2):
                both = b[name][:, c:c + 2, :].rearrange("p j t -> p (j t)")
                bank = self.products.take()
                pe.wait(ready[name], bank.free)
                m = pe.done(nc.tensor.matmul(bank.tile[:, :], self.k("swap64"), both, start=True, stop=True))
                dve.wait(m, self.reuse.get("tmp"))
                bank.free = dve.done(nc.vector.tensor_tensor(b["tmp"][:, :], bank.tile[:, :], self.k("sin128"), ALU.mult))
                dve.wait(dve.done(nc.vector.tensor_tensor(both, both, self.k("cos128"), ALU.mult)))
                self.reuse["tmp"] = ready[name + "_rot"] = dve.done(nc.vector.tensor_tensor(both, both, b["tmp"][:, :], ALU.add))

        def fill():
            yield from self.dense(k2("s_q"), u, None, self.copy_to(b["s_q"], "s_q", SBD ** -0.5))
            yield from self.dense(k2("s_k"), u, None, self.copy_to(b["s_k"], "s_k"))
            yield "stick-breaking can start"
            yield from self.token_major(k2("s_v"), u, None, self.tokens_to(b["s_v"], "s_v"))
            yield from self.dense(k2("m_z"), u, None, self.function_to(b["m_z"], "m_z", ACT.Silu))
            yield from self.dense(k2("r_q"), u, None, self.copy_to(b["r_q"], "r_q"))
            yield from self.dense(k2("r_k"), u, None, self.copy_to(b["r_k"], "r_k"))
            rotate("r_q")
            yield from self.token_major(k2("r_v"), u, None, self.tokens_to(b["r_v"], "r_v"))
            rotate("r_k")
            yield from self.dense(k2("r_g"), u, None, self.function_to(b["r_g"], "r_g", ACT.Silu))
            yield "retention can start"
        filler = Filler(fill())
        filler.until("stick-breaking can start")

        def stick(i):
            q, k_ = b["s_q"], b["s_k"]
            bank, work, keep = self.scores.take(), self.maps.take(), self.keep.take()
            pe.wait(ready["s_q"], ready["s_k"], bank.free)
            nc.tensor.matmul(bank.tile[:, 0:T], k_[:, i, 0:P], q[:, i, :], start=True, stop=False, skip_group_check=True)
            mark = pe.done(nc.tensor.matmul(bank.tile[:, T:TRI], k_[:, i, P:T], q[:, i, P:T], start=False, stop=False,
                                            skip_group_check=True))
            raw = bank.tile[:, 0:TRI]
            act.wait(mark, work.free, keep.free)
            act.wait(act.done(nc.scalar.activation(work.tile[:, :], raw, ACT.Abs)))
            act.wait(act.done(nc.scalar.activation(work.tile[:, :], work.tile[:, :], ACT.Exp, scale=-1.0)))
            m = act.done(nc.scalar.activation(work.tile[:, :], work.tile[:, :], ACT.Ln, bias=1.0))
            dve.wait(m)
            m = dve.done(nc.vector.scalar_tensor_tensor(work.tile[:, :], raw, 0.0, work.tile[:, :], ALU.max, ALU.add))
            dve.wait(m)
            m = dve.done(nc.vector.tensor_tensor(keep.tile, work.tile[:, :], self.k("before"), ALU.mult))
            yield
            pe.wait(m)
            nc.tensor.matmul(bank.tile[:, 0:T], self.k("neg_ge"), keep.tile[:, 0:T], start=False, stop=False, skip_group_check=True)
            nc.tensor.matmul(bank.tile[:, P:T], self.k("neg_ones"), keep.tile[:, T:TRI], start=False, stop=False, skip_group_check=True)
            keep.free = m = pe.done(nc.tensor.matmul(bank.tile[:, T:TRI], self.k("neg_ge"), keep.tile[:, T:TRI],
                                                     start=False, stop=True, skip_group_check=True))
            wt = self.maps_t.take()
            dve.wait(m, wt.free)
            bank.free = m = dve.done(nc.vector.tensor_tensor(work.tile[:, :], raw, self.k("before_neg"), ALU.add))
            act.wait(m)
            work.free = wt.ready = act.done(nc.scalar.activation(wt.tile[:, :], work.tile[:, :], ACT.Exp))
            yield
            vbank = self.values.take()
            pe.wait(vbank.free, ready["s_v"])
            m = self.weigh_values(vbank.tile[:, 0:T], b["s_v"], slice(i * P, (i + 1) * P), wt)
            act.wait(self.reuse["y"])
            vbank.free = ready["y_s"] = self.split_values(y, (slice(None), i), vbank.tile[:, 0:T], m)
        self.pipeline([stick(i) for i in range(SBH)], filler)
        stick_done = ready["y_s"]

        bank = self.scores.take()
        pe.wait(da_ready, bank.free)
        for t in range(TB):
            nc.tensor.matmul(bank.tile[:, t * MH:(t + 1) * MH], self.k("le"), da[:, t * MH:(t + 1) * MH], start=True, stop=True)
        m = pe.done(nc.tensor.matmul(bank.tile[:, 2 * MH:3 * MH], self.k("gt"), da[:, 0:MH], start=True, stop=True))
        dve.wait(m, self.reuse.get("cum"))
        bank.free = cum_ready = dve.done(nc.vector.tensor_copy(
            b["cum"][:, 0:3, :].rearrange("p i h -> p (i h)"), bank.tile[:, 0:3 * MH]))
        for t in range(TB):
            bank = self.turned.take()
            pe.wait(ready["xbc"], bank.free)
            for c in range(4):
                last = nc.tensor.transpose(bank.tile[:, c * P:(c + 1) * P], b["xbc"][:, c, t * P:(t + 1) * P], self.k("ident"))
            m = pe.done(last)
            act.wait(m)
            bank.free = ready["m_v"] = act.done(nc.scalar.copy(b["m_v"][:, t, :], bank.tile[:, :]))
        for g in range(MG):
            bank = self.scores.take()
            pe.wait(bank.free)
            B_, C_ = b["xbc"][:, 4 + g, :], b["xbc"][:, 6 + g, :]
            nc.tensor.matmul(bank.tile[:, 0:T], B_[:, 0:P], C_, start=True, stop=True)
            m = pe.done(nc.tensor.matmul(bank.tile[:, T:TRI], B_[:, P:T], C_[:, P:T], start=True, stop=True))
            act.wait(m, stick_done)
            bank.free = cb_ready = act.done(nc.scalar.copy(b["cb"][:, g, :], bank.tile[:, 0:TRI]))
        state = {}

        def mamba_map(i):
            bank, work = self.scores.take(), self.maps.take()
            pe.wait(bank.free)
            for t in range(TB):
                last = nc.tensor.matmul(bank.tile[:, t * P:(t + 1) * P],
                                        da[:, t * MH + i:t * MH + i + 1].to_broadcast([P, P]), self.k("le"),
                                        start=True, stop=True)
            m = pe.done(last)
            cum = lambda j: b["cum"][:, j, i:i + 1]
            dve.wait(m, cum_ready, work.free)
            w_ = work.tile
            nc.vector.scalar_tensor_tensor(w_[:, 0:P], bank.tile[:, 0:P], cum(0), self.k("upto_min"), ALU.subtract, ALU.min)
            nc.vector.tensor_scalar(w_[:, P:T], bank.tile[:, P:T], cum(2), None, ALU.add)
            bank.free = m = dve.done(nc.vector.scalar_tensor_tensor(
                w_[:, T:TRI], bank.tile[:, P:T], cum(1), self.k("upto_min"), ALU.subtract, ALU.min))
            act.wait(m)
            m = act.done(nc.scalar.activation(w_[:, :], w_[:, :], ACT.Exp))
            wt = self.maps_t.take()
            dve.wait(m, cb_ready, wt.free)
            g = i // (MH // MG)
            nc.vector.scalar_tensor_tensor(wt.tile[:, 0:T], w_[:, 0:T], dt[:, i:i + 1], b["cb"][:, g, 0:T], ALU.mult, ALU.mult)
            wt.ready = work.free = dve.done(nc.vector.scalar_tensor_tensor(
                wt.tile[:, T:TRI], w_[:, T:TRI], dt[:, MH + i:MH + i + 1], b["cb"][:, g, T:TRI], ALU.mult, ALU.mult))
            return wt

        def mamba_values(i, wt):
            rows, c = slice(64 * (i % 2), 64 * (i % 2) + 64), i // 2
            if i % 2 == 0:
                state["bank"] = self.values.take()
                pe.wait(state["bank"].free)
            vbank = state["bank"]
            pe.wait(ready["m_v"])
            m = self.weigh_values(vbank.tile[rows, 0:T], b["m_v"], slice(i * MP, (i + 1) * MP), wt)
            if i % 2 == 1:
                dve.wait(m, ready["m_z"])
                vbank.free = m = dve.done(nc.vector.scalar_tensor_tensor(
                    y_m[:, c, :], b["xbc"][:, c, :], self.s(f"d_skip{l}", 1, c), vbank.tile[:, 0:T], ALU.mult, ALU.add))
                dve.wait(m)
                m = dve.done(nc.vector.tensor_tensor(y_m[:, c, :], y_m[:, c, :], b["m_z"][:, c, :], ALU.mult))
                ready["y_m_sq"] = self.square(b["squares"][:, c, :], y_m[:, c, :], [m, ready["y_s"]])
                ready["y_m"] = m
        def mamba(i):
            maps = [mamba_map(2 * i + j) for j in range(2)]
            yield
            for j, wt in enumerate(maps):
                mamba_values(2 * i + j, wt)
        self.pipeline([mamba(i) for i in range(MH // 2)], filler)
        filler.until("retention can start")
        u_read = (pe.semaphore, pe.count)
        self.reuse["cum"] = self.reuse["m_z"] = ready["y_m"]

        (bank,) = self.inverse_rms(b["squares"], 1, 4, 512, 1e-6, ready["y_m_sq"])
        dve.wait(bank.ready)
        for c in range(4):
            m = dve.done(nc.vector.scalar_tensor_tensor(
                y_m[:, c, :], y_m[:, c, :], self.s(f"ssm_norm{l}", 1, c), bank.tile[:, 0:T], ALU.mult, ALU.mult))
        bank.free = m
        act.wait(u_read)
        ready["y_m"] = self.split_values(u, (slice(None), slice(4, 8)), y_m, m)

        self.add_mod_bias()
        banks = [self.products.take(), self.products.take(), self.turned.take(), self.mod_banks.take()]
        self.mods_pause = True
        place = {4: (y, 0, "y_s"), 6: (y, 2, "y_s"), 8: (u, 4, "y_m"), 10: (u, 6, "y_m"),
                 0: (u, 0, "y_r"), 2: (u, 2, "y_r")}

        def mix_out(pairs):
            for c in pairs:
                slot = self.weights((f"mix_out{l}", c))
                x, at_, name = place[c]
                self.accumulate(slot, banks, x, at_, ready[name], c == OUT_ORDER[0], c == OUT_ORDER[-1])
                self.reuse["y"] = self.reuse["u"] = self.reuse["xbc_in"] = slot.free
                yield
        filler = Filler(mix_out(OUT_ORDER[:4]))

        def retain(i):
            q, k_ = b["r_q"], b["r_k"]
            bank, wt = self.scores.take(), self.maps_t.take()
            pe.wait(ready["r_q_rot"], ready["r_k_rot"], bank.free)
            nc.tensor.matmul(bank.tile[:, 0:T], k_[:, i, 0:P], q[:, i, :], start=True, stop=True)
            m = pe.done(nc.tensor.matmul(bank.tile[:, T:TRI], k_[:, i, P:T], q[:, i, P:T], start=True, stop=True))
            dve.wait(m, wt.free)
            bank.free = wt.ready = dve.done(nc.vector.tensor_tensor(
                wt.tile[:, :], bank.tile[:, 0:TRI], self.k("decay", i * TRI, TRI), ALU.mult))
            yield
            vbank = self.values.take()
            pe.wait(vbank.free, ready["r_v"])
            m = self.weigh_values(vbank.tile[:, 0:T], b["r_v"], slice(i * P, (i + 1) * P), wt)
            act.wait(m)
            vbank.free = m = act.done(nc.scalar.copy(y_r[:, i, :], vbank.tile[:, 0:T]))
            ready["y_r"] = m
            ready["y_r_sq"] = self.square(b["squares"][:, 4 + i, :], y_r[:, i, :], m)
        self.pipeline([retain(i) for i in range(RH)], filler)
        while filler.step():
            pass
        scales = self.inverse_rms(b["squares"][:, 4:8, :], 4, 1, RD, 1e-6, ready["y_r_sq"])
        for i in range(RH):
            bank = scales[i // 2]
            dve.wait(bank.ready, ready["y_r"], ready["r_g"])
            bank.free = m = dve.done(nc.vector.scalar_tensor_tensor(
                y_r[:, i, :], y_r[:, i, :], self.s(f"ret_gn{l}", 1, i), bank.tile[:, (i % 2) * T:(i % 2 + 1) * T],
                ALU.mult, ALU.mult))
            dve.wait(m)
            m = dve.done(nc.vector.tensor_tensor(y_r[:, i, :], y_r[:, i, :], b["r_g"][:, i, :], ALU.mult))
            ready["y_r"] = self.split_values(u, (slice(None), i), y_r[:, i, :], m)
        self.reuse["squares"] = bank.ready
        for n in ("r_q", "r_k", "r_v", "r_g", "s_q", "s_k", "s_v"):
            self.reuse[n] = ready["y_r"]

        self.run(mix_out(OUT_ORDER[4:]))
        self.mods_pause = False
        self.add_to_h(banks)


def constants():
    f = np.float32
    c = {}
    i = np.arange(P)
    c["ident"] = np.eye(P, dtype=f)
    c["ones"] = np.ones((P, P), f)
    c["swap64"] = (i[:, None] == (i[None, :] + 64) % P).astype(f)
    s16 = np.zeros((P, 32), f)
    j = np.arange(32)
    s16[64 + (j + 16) % 32, j] = 1.0
    c["swap16"] = s16

    def tri(fn):
        k = np.arange(T)
        return np.concatenate([fn(i[:, None], k[None, :P]), fn(P + i[:, None], k[None, :])], 1).astype(f)

    def tri_t(fn):
        t = np.arange(T)
        return np.concatenate([fn(i[:, None], t[None, :]), fn(P + i[:, None], t[None, P:])], 1).astype(f)
    c["dist"] = tri(lambda q, k: np.where(k <= q, q - k, 1e33))
    c["causal"] = tri(lambda q, k: np.where(k <= q, 0.0, NEG))

    def rotary(half, base_row, rows, freqs):
        pos = np.arange(T, dtype=f)
        ang = (pos[:, None] * freqs[None, :]).astype(f)
        cos, sin = np.cos(ang).T, np.sin(ang).T
        cc, ss = np.zeros((P, T), f), np.zeros((P, T), f)
        cc[base_row:base_row + rows] = np.concatenate([cos, cos])
        ss[base_row:base_row + rows] = np.concatenate([-sin, sin])
        return np.concatenate([cc, cc], 1), np.concatenate([ss, ss], 1)
    fr = (f(10000.0) ** (-np.arange(0, ROPE, 2, dtype=f) / f(ROPE))).astype(f)
    c["cos32"], c["sin32"] = rotary(16, 64, 32, fr)
    fr = (f(10000.0) ** (-np.arange(64, dtype=f) / f(64))).astype(f)
    c["cos128"], c["sin128"] = rotary(64, 0, 128, fr)
    decay = []
    for h in range(RH):
        lg = math.log1p(-(2.0 ** (-5.0 - h)))
        decay.append(tri_t(lambda s, t: np.where(s // 64 <= t // 64, np.exp(lg * np.abs(t - s)), 0.0) * RD ** -0.5))
    c["decay"] = np.concatenate(decay, 1)
    c["before"] = tri_t(lambda s, t: s < t)
    c["before_neg"] = tri_t(lambda s, t: np.where(s < t, 0.0, NEG))
    c["upto_min"] = np.where(i[:, None] <= i[None, :], 0.0, NEG).astype(f)
    c["le"] = (i[:, None] <= i[None, :]).astype(f)
    c["gt"] = (i[:, None] > i[None, :]).astype(f)
    c["neg_ge"] = -(i[:, None] >= i[None, :]).astype(f)
    c["neg_ones"] = -np.ones((P, P), f)
    return {f"constants_{group}": np.ascontiguousarray(np.concatenate([c[n] for n, _ in sizes], 1))
            for group, sizes in CONST_SIZES.items()}


def small_parameters(a):
    col = lambda v: np.ascontiguousarray(v).reshape(-1, P).T
    every = lambda v: np.broadcast_to(np.asarray(v).reshape(1, -1), (P, np.asarray(v).size))
    parts = []
    for l in range(DEPTH):
        parts += [col(a["mla_q_norm_g"][l]), col(a["mla_kv_norm_g"][l]), col(a["diff_subln_g"][l]),
                  col(a["b_merge"][l]), col(a["ln_g"][l]), col(a["ln_b"][l]), col(a["ada_b_2"][l]),
                  col(a["norm_ffn1_2"][l]), col(a["norm_mix_2"][l]), col(a["norm_ffn2_2"][l]),
                  col(a["conv_w_2"][l].reshape(-1)), col(a["conv_b_2"][l]), col(a["ret_gn_2"][l]),
                  col(a["ssm_norm_2"][l]), col(np.repeat(a["d_skip_2"][l], MP)), every(a["dt_bias_2"][l]),
                  every(a["a_log_2"][l]), every(a["diff_lambda"][l])]
    parts += [col(a["c_2"]), col(a["final_ada_b_2"]), col(a["final_norm_2"])]
    return np.ascontiguousarray(np.concatenate(parts, 1))


DIRECT = {"w_in": "w_in", "mla_w_uq": "mla_w_uq", "mla_w_ukv": "mla_w_ukv", "w_branch_a": "w_branch_a",
          "w_branch_b": "w_branch_b", "w_branch_c": "w_branch_c", "w_merge": "w_merge", "w_out": "w_out",
          "w_ple_gate": "w_ple_gate", "w_ple": "w_ple", "ada_w": "ada_w_2", "final_ada_w": "final_ada_w_2",
          "ffn1_wg_2": "ffn1_wg_2", "ffn1_wu_2": "ffn1_wu_2", "ffn1_wd_2": "ffn1_wd_2", "w_in_2": "w_in_2",
          "w_out_2": "w_out_2", "ffn2_wg_2": "ffn2_wg_2", "ffn2_wu_2": "ffn2_wu_2", "ffn2_wd_2": "ffn2_wd_2"}


def kernel(**inputs):
    import concourse.bacc as bacc
    from concourse.bass_utils import run_bass_kernel_spmd

    given = {n: np.asarray(v) for n, v in inputs.items()}
    arrays = {n: np.ascontiguousarray(given[src]) for n, src in DIRECT.items()}
    arrays["x"] = np.ascontiguousarray(given["x"][0].T)
    arrays["p"] = np.ascontiguousarray(given["p"][:, 0].transpose(0, 2, 1))
    arrays["small"] = small_parameters(given)
    arrays.update(constants())
    nc = bacc.Bacc("TRN2", target_bir_lowering=False, num_devices=1)
    handles = {n: nc.dram_tensor(f"in_{n}", v.shape, mybir.dt.from_np(v.dtype), kind="ExternalInput").ap()
               for n, v in arrays.items()}
    out = nc.dram_tensor("out", (D, T), F32, kind="ExternalOutput").ap()
    build(nc, handles, out)
    r = run_bass_kernel_spmd(nc, [{f"in_{n}": v for n, v in arrays.items()}], core_ids=[0])
    return np.ascontiguousarray(r.results[0]["out"].T)[None]
```

```python
from contextlib import ExitStack
import math

import numpy as np
import concourse.bass as bass
from concourse import mybir

F32 = mybir.dt.float32
F32R = mybir.dt.float32r
ALU = mybir.AluOpType
ACT = mybir.ActivationFunctionType
AX = mybir.AxisListType

P = 128
T = 256
TB = T // P
D = 1024
DC = D // P
DEPTH = 2
TRI = 3 * P
MAP_PARTS = ((0, P), (P, TRI))

HEADS, HD = 8, 64
Q_LORA, KV_LORA, NOPE, ROPE = 384, 256, 64, 32
DIFF_HEADS, DIFF_QK = 4, 64
PLE = 256
W = HEADS * HD
IN1 = dict(a_q=(0, 512), a_k=(512, 512), a_v=(1024, 512), a_z=(1536, 512), b_cq=(2048, 384),
           b_ckvr=(2432, 288), b_z=(2720, 512), c_q=(3232, 512), c_k=(3744, 512),
           c_v=(4256, 512), c_z=(4768, 512))
ALPHA = (2 * DEPTH) ** 0.25
NSLOPE = HEADS + DIFF_HEADS
SLOPES = 2.0 ** (-8.0 * (np.arange(NSLOPE) + 1) / NSLOPE)
DIFF_IDX = np.arange(DIFF_HEADS) * (NSLOPE // DIFF_HEADS)
DIFF_SLOPES = SLOPES[DIFF_IDX].astype(np.float32)
MOBA_SLOPES = SLOPES[np.setdiff1d(np.arange(NSLOPE), DIFF_IDX)].astype(np.float32)

RH, RD = 4, 128
SBH, SBD = 4, 128
MH, MP, MN, MG = 8, 64, 128, 2
TAPS = 4
FF = 2816
FC = FF // P
IN2 = dict(r_q=(0, 512), r_k=(512, 512), r_v=(1024, 512), r_g=(1536, 512), s_q=(2048, 512),
           s_k=(2560, 512), s_v=(3072, 512), m_z=(3584, 512), m_x=(4096, 512),
           m_bc=(4608, 512), m_dt=(5120, 8))
XBC = 1024
OUT_ORDER = (4, 6, 8, 10, 0, 2)
HIDDEN_BLOCKS = 6

NEG = -1e30
SLOT = 2048
RAW_SLOTS = 4
SPLIT_SLOTS = 3
AHEAD = 2
MERGE_BLOCKS = 2


def columns(sizes):
    at, out = 0, {}
    for name, n in sizes:
        out[name] = at
        at += n
    return out, at


CONST_SIZES = {
    "both": [("ident", P), ("ones", P)],
    "first": [("swap16", 32), ("dist", TRI), ("causal", TRI), ("cos32", T), ("sin32", T)],
    "second": [("swap64", P), ("cos128", T), ("sin128", T), ("decay", RH * TRI), ("before", TRI),
               ("before_neg", TRI), ("upto_min", P), ("le", P), ("gt", P), ("neg_ge", P), ("neg_ones", P)]}
CONST_AT = {n: (group, at) for group, sizes in CONST_SIZES.items() for n, at in columns(sizes)[0].items()}
CONST_WIDTH = {n: w for sizes in CONST_SIZES.values() for n, w in sizes}

PER_LAYER = [("gq", 3), ("gkv", 2), ("subln", 1), ("b_merge", 24), ("ln_g", 8), ("ln_b", 8),
             ("ada_b", 72), ("norm_ffn1", 8), ("norm_mix", 8), ("norm_ffn2", 8), ("conv_w", 32),
             ("conv_b", 8), ("ret_gn", 4), ("ssm_norm", 4), ("d_skip", 4), ("dt_bias", 8),
             ("a_log", 8), ("lambda", 256)]
SMALL_SIZES = [(f"{n}{l}", s) for l in range(DEPTH) for n, s in PER_LAYER]
SMALL_SIZES += [("c", 8), ("final_ada_b", 16), ("final_norm", 8)]
SMALL_AT, SMALL_N = columns(SMALL_SIZES)


def plan(a):
    def panels(name, w, rows, start, total, width):
        for i, c in enumerate(range(0, total, width)):
            n = min(width, total - c)
            yield (name, i), w[:, start + c:start + c + n], rows, n

    def w_in(table, w, l, names):
        for n in names:
            yield from panels(f"{n}{l}", w[l], D, *table[n], 256)

    def merge(l, i, branch):
        width = MERGE_BLOCKS * P
        gates = panels(f"gate_{branch}{l}", a["w_merge"][l], D, i * D, D, width)
        products = panels(f"branch_{branch}{l}", a[f"w_branch_{branch}"][l], W, 0, D, width)
        for pair in zip(gates, products):
            yield from pair

    for l in range(DEPTH):
        yield from panels(f"b_cq{l}", a["w_in"][l], D, *IN1["b_cq"], P)
        start = IN1["b_ckvr"][0]
        yield (f"b_ckvr{l}", 0), a["w_in"][l][:, start:start + P], D, P
        yield (f"b_ckvr{l}", 1), a["w_in"][l][:, start + P:start + 288], D, 160
        yield from w_in(IN1, a["w_in"], l, ["a_q", "a_k", "a_v", "a_z", "c_q", "c_k", "c_v", "c_z"])
        yield from panels(f"uq{l}", a["mla_w_uq"][l], Q_LORA, 0, 768, 384)
        yield from merge(l, 0, "a")
        yield from panels(f"ukv{l}", a["mla_w_ukv"][l], KV_LORA, 0, 1024, 1024)
        yield from w_in(IN1, a["w_in"], l, ["b_z"])
        yield from merge(l, 2, "c")
        yield from panels(f"gate_b{l}", a["w_merge"][l], D, D, D, MERGE_BLOCKS * P)
        yield from panels(f"branch_b{l}", a["w_branch_b"][l], W, 0, D, MERGE_BLOCKS * P)
        ple = list(panels(f"ple{l}", a["w_ple"][l], PLE, 0, D, D // 2))
        yield ple[0]
        yield from panels(f"w_out{l}", a["w_out"][l], D, 0, D, 256)
        yield ple[1]
        yield from panels(f"ple_gate{l}", a["w_ple_gate"][l], D, 0, D, 256)
    for l in range(DEPTH):
        for ffn in (1, 2):
            wg, wu, wd = (a[f"ffn{ffn}_{w}_2"][l] for w in ("wg", "wu", "wd"))
            pairs = FC // 2
            for i in range(pairs + 1):
                if i < pairs:
                    yield (f"wg{ffn}{l}", i), wg[:, 256 * i:256 * (i + 1)], D, 256
                    yield (f"wu{ffn}{l}", i), wu[:, 256 * i:256 * (i + 1)], D, 256
                if i > 0:
                    yield (f"wd{ffn}{l}", i - 1), wd[256 * (i - 1):256 * i, :], 256, D
            if ffn == 1:
                yield from w_in(IN2, a["w_in_2"], l, ["m_x", "m_bc", "m_dt", "s_q", "s_k", "s_v", "m_z",
                                                      "r_q", "r_k", "r_v", "r_g"])
                for c in OUT_ORDER:
                    yield (f"mix_out{l}", c), a["w_out_2"][l][c * P:(c + 2) * P, :], 256, D


def keys(name, n):
    return [(name, i) for i in range(n)]


class Split:

    def __init__(self, hi, lo):
        self.hi, self.lo = hi, lo


class Engine:

    def __init__(self, queue, semaphore):
        self.queue, self.semaphore, self.count, self.waited = queue, semaphore, 0, {}

    def done(self, instruction):
        instruction.then_inc(self.semaphore, 1)
        self.count += 1
        return (self.semaphore, self.count)

    def settle(self):
        if self.count:
            self.wait((self.semaphore, self.count))

    def wait(self, *marks):
        for mark in marks:
            if mark is None:
                continue
            if isinstance(mark, list):
                self.wait(*mark)
                continue
            semaphore, value = mark
            if self.waited.get(semaphore.name, 0) < value:
                self.queue.wait_ge(semaphore, value)
                self.waited[semaphore.name] = value


class Buffer:

    def __init__(self, tile):
        self.tile, self.free = tile, None


class Filler:

    def __init__(self, steps):
        self.steps, self.passed = steps, set()

    def step(self):
        for point in self.steps:
            if point is None:
                return True
            self.passed.add(point)
        return False

    def until(self, point):
        while point not in self.passed:
            if not self.step():
                assert point in self.passed


class Turn:

    def __init__(self, tiles):
        self.buffers, self.at = [Buffer(t) for t in tiles], 0

    def take(self):
        self.at += 1
        return self.buffers[(self.at - 1) % len(self.buffers)]


def build(nc, a, out):
    with ExitStack() as whole:
        Program(nc, a, out, whole)


class Program:
    def __init__(self, nc, a, out, whole):
        self.nc, self.a = nc, a
        sb = lambda name, shape: whole.enter_context(nc.sbuf_tensor(name, shape, F32))
        sem = lambda name: whole.enter_context(nc.semaphore(name))
        self.pe = Engine(nc.tensor, sem("pe_marks"))
        self.dve = Engine(nc.vector, sem("dve_marks"))
        self.act = Engine(nc.scalar, sem("act_marks"))
        self.pool = Engine(nc.gpsimd, sem("pool_marks"))
        self.sp = Engine(nc.sync, sem("sp_marks"))
        banks = [whole.enter_context(nc.psum_tensor(f"bank{i}", [P, 512], F32)) for i in range(8)]
        self.products = Turn(banks[0:2])
        self.mod_banks = Turn(banks[2:3])
        self.scores = Turn(banks[3:5])
        self.turned = Turn(banks[5:7])
        self.values = Turn(banks[7:8])
        self.raw = Turn([sb(f"weights{i}", [P, SLOT]) for i in range(RAW_SLOTS)])
        for i, s in enumerate(self.raw.buffers):
            s.semaphore, s.loads = sem(f"weights{i}_loaded"), 0
        sb_r = lambda name, shape: whole.enter_context(nc.sbuf_tensor(name, shape, F32R))
        self.split = Turn([(sb_r(f"weights_hi{i}", [P, SLOT]), sb_r(f"weights_lo{i}", [P, SLOT]))
                           for i in range(SPLIT_SLOTS)])

        self.const = {"both": sb("constants", [P, columns(CONST_SIZES["both"])[1]])}
        self.small = sb("small_parameters", [P, SMALL_N])
        self.h = sb("h", [P, DC, T])
        self.loaded = sem("parameters_loaded")

        self.stats = Turn([sb(f"statistics{i}", [P, 3, 8]) for i in range(2)])

        self.mods = sb("modulations", [P, DEPTH * 72 + 16])
        self.mod_sum = Turn([sb(f"mod_sum{i}", [P, 256]) for i in range(2)])
        self.cond = sb("cond", [P, DC])
        self.mod_work, self.mods_known, self.mod_summed = self.modulations(), 0, None
        self.mods_pause = False
        self.diagonal_free = None
        self.planned, self.prepared = list(plan(a)), []

        with ExitStack() as stack:
            self.first_stack(stack)
        with ExitStack() as stack:
            self.second_stack(stack, out)

    def k(self, name, i=None, n=None):
        group, at = CONST_AT[name]
        at += i or 0
        size = n if n is not None else (1 if i is not None else CONST_WIDTH[name])
        return self.const[group][:, at:at + size]

    def load_constants(self, stack, group):
        nc = self.nc
        self.const[group] = stack.enter_context(
            nc.sbuf_tensor(f"constants_{group}", [P, columns(CONST_SIZES[group])[1]], F32))
        semaphore = stack.enter_context(nc.semaphore(f"constants_{group}_loaded"))
        nc.sync.dma_start(self.const[group][:, :], self.a[f"constants_{group}"]).then_inc(semaphore, 16)
        self.const_loaded = (semaphore, 16)

    def per_head(self, v, heads):
        return v.rearrange("p (h t) -> p h t", h=heads)

    def s(self, name, n=1, i=0):
        at = SMALL_AT[name] + i
        return self.small[:, at:at + n]

    def load(self, source, rows, cols):
        slot = self.raw.take()
        kc = rows // P
        self.sp.wait(slot.free)
        slot.view = slot.tile[:, 0:kc * cols].rearrange("p (k n) -> p k n", k=kc)
        self.nc.sync.dma_start(slot.view, source.rearrange("(k p) n -> p k n", p=P)).then_inc(slot.semaphore, 16)
        slot.loads += 1
        slot.loaded = (slot.semaphore, 16 * slot.loads)
        return slot

    def prepare(self):
        if not self.planned:
            return
        key, source, rows, cols = self.planned.pop(0)
        nc, kc = self.nc, rows // P
        raw, slot = self.load(source, rows, cols), self.split.take()
        n = kc * cols
        hi, lo = slot.tile
        self.act.wait(raw.loaded, slot.free)
        mark = self.act.done(nc.scalar.copy(hi[:, 0:n], raw.tile[:, 0:n]))
        self.dve.wait(mark)
        raw.free = slot.ready = self.dve.done(nc.vector.tensor_tensor(
            lo[:, 0:n], raw.tile[:, 0:n], hi[:, 0:n].bitcast(F32), ALU.subtract))
        slot.hi, slot.lo = (t[:, 0:n].rearrange("p (k n) -> p k n", k=kc) for t in (hi, lo))
        slot.key = key
        self.prepared.append(slot)

    def weights(self, key):
        while len(self.prepared) <= AHEAD and self.planned:
            self.prepare()
        slot = self.prepared.pop(0)
        assert slot.key == key, (slot.key, key)
        self.pe.wait(slot.ready)
        return slot

    def split_product(self, out, pairs, start=True, stop=True, **more):
        n = len(pairs)
        for i, ((a_hi, a_lo), (b_hi, b_lo)) in enumerate(pairs):
            self.nc.tensor.matmul(out, a_hi, b_hi, start=start and i == 0, stop=False, **more)
            self.nc.tensor.matmul(out, a_hi, b_lo, start=False, stop=False, **more)
            last = self.nc.tensor.matmul(out, a_lo, b_hi, start=False, stop=stop and i == n - 1, **more)
        return last

    def split_values(self, dst, index, source, ready):
        self.act.wait(ready)
        mark = self.act.done(self.nc.scalar.copy(dst.hi[index], source))
        self.dve.wait(mark)
        return self.dve.done(self.nc.vector.tensor_tensor(
            dst.lo[index], source, dst.hi[index].bitcast(F32), ALU.subtract))

    def dense(self, keys, x, x_ready, evacuate, first=0, x_from=0):
        at = first
        for key in keys:
            slot = self.weights(key)
            kc, cols = slot.hi.shape[1], slot.hi.shape[2]
            blocks = cols // P
            for b in range(0, blocks, 2):
                bank = self.products.take()
                self.pe.wait(bank.free)
                n = min(2, blocks - b)
                for j in range(n):
                    at_cols = slice((b + j) * P, (b + j + 1) * P)
                    for k in range(kc):
                        self.pe.wait(x_ready[k] if isinstance(x_ready, list) else x_ready)
                        xk = (k + x_from) % kc
                        last = self.split_product(
                            bank.tile[:, j * T:(j + 1) * T],
                            [((slot.hi[:, k, at_cols], slot.lo[:, k, at_cols]), (x.hi[:, xk, :], x.lo[:, xk, :]))],
                            start=k == 0, stop=k == kc - 1)
                slot.free = mark = self.pe.done(last)
                bank.free = evacuate(bank.tile, at, n, mark)
                at += n
                yield
            self.count_unit()

    def token_major(self, keys, x, x_ready, evacuate):
        for u, key in enumerate(keys):
            slot = self.weights(key)
            kc = slot.hi.shape[1]
            bank = self.products.take()
            self.pe.wait(x_ready, bank.free)
            for b in range(TB):
                tok = slice(b * P, (b + 1) * P)
                last = self.split_product(
                    bank.tile[:, b * 256:(b + 1) * 256],
                    [((x.hi[:, k, tok], x.lo[:, k, tok]), (slot.hi[:, k, :], slot.lo[:, k, :])) for k in range(kc)])
            slot.free = mark = self.pe.done(last)
            bank.free = evacuate(bank.tile, u, mark)
            self.count_unit()
            yield

    def accumulate(self, slot, banks, x, pair, pair_ready, first, last):
        self.pe.wait(pair_ready)
        for c in range(DC):
            if c == DC // 2:
                yield
            bank = banks[c // 2]
            if first:
                self.pe.wait(bank.free)
            cols = slice(c * P, (c + 1) * P)
            m = self.split_product(
                bank.tile[:, (c % 2) * T:(c % 2 + 1) * T],
                [((slot.hi[:, k, cols], slot.lo[:, k, cols]), (x.hi[:, pair + k, :], x.lo[:, pair + k, :]))
                 for k in range(2)],
                start=first and c % 2 == 0, stop=last and c % 2 == 1, skip_group_check=True)
            if last and c % 2 == 1:
                bank.ready = self.pe.done(m)
        slot.free = bank.ready if last else self.pe.done(m)
        self.count_unit()

    def count_unit(self):
        if not self.mods_pause:
            next(self.mod_work, None)

    def modulations(self):
        nc, pending = self.nc, []

        def sum_partitions():
            if not pending:
                return
            total, at, bias = pending.pop()
            bank = self.mod_banks.take()
            self.pe.wait(total.ready, bank.free)
            for i in range(2):
                last = nc.tensor.matmul(bank.tile[:, i:i + 1], total.tile[:, i * P:(i + 1) * P],
                                        self.k("ones", 0), start=True, stop=True)
            total.free = bank.ready = self.pe.done(last)
            self.mod_summed = (bank, at, bias)
        todo = [("ada_w", l, j) for l in range(DEPTH) for j in range(36)]
        todo += [("final_ada_w", DEPTH, j) for j in range(8)]
        for name, l, j in todo:
            sum_partitions()
            source = self.a[name][l] if l < DEPTH else self.a[name]
            slot = self.load(source[:, j * 256:(j + 1) * 256], D, 256)
            slot.free = "being read"
            total = self.mod_sum.take()
            self.dve.wait(slot.loaded, self.cond_ready, total.free)
            mark = self.dve.done(nc.vector.tensor_scalar(
                total.tile[:, :], slot.view[:, 0, :], self.cond[:, 0:1], None, ALU.mult))
            for k in range(1, DC):
                if k == DC // 2:
                    yield
                    self.add_mod_bias()
                self.dve.wait(mark)
                mark = self.dve.done(nc.vector.scalar_tensor_tensor(
                    total.tile[:, :], slot.view[:, k, :], self.cond[:, k:k + 1], total.tile[:, :],
                    ALU.mult, ALU.add))
            slot.free = total.ready = mark
            bias = self.s(f"ada_b{l}", 2, 2 * j) if l < DEPTH else self.s("final_ada_b", 2, 2 * j)
            pending.append((total, l * 72 + 2 * j, bias))
            yield
            yield
        sum_partitions()
        yield
        self.add_mod_bias()
        yield

    def add_mod_bias(self):
        if self.mod_summed:
            bank, at, bias = self.mod_summed
            self.mod_summed = None
            self.dve.wait(bank.ready)
            bank.free = self.mod_last = self.dve.done(self.nc.vector.tensor_tensor(
                self.mods[:, at:at + 2], bank.tile[:, 0:2], bias, ALU.add))
            self.mods_known = at + 2

    def mods_until(self, columns):
        while self.mods_known < columns:
            next(self.mod_work)

    def pause_mods(self):
        while any(slot.free == "being read" for slot in self.raw.buffers):
            next(self.mod_work)
        self.add_mod_bias()
        self.mods_pause = True

    def inverse_rms(self, squares, groups, per_group, count, eps, ready, ring=None):
        nc, pe, dve, act = self.nc, self.pe, self.dve, self.act
        n = groups * TB
        st = self.stats.take()
        mean, inv, tmp = st.tile[:, 0, 0:n], st.tile[:, 1, 0:n], st.tile[:, 2, 0:n]
        dve.wait(st.free)
        ring = ring or (self.turned if groups == 1 else self.scores)
        for g in range(0, groups, 2):
            sums = ring.take()
            pe.wait(sums.free)
            some = min(2, groups - g)
            for k in range(per_group):
                pe.wait(ready[k] if isinstance(ready, list) else ready)
                rhs = squares[:, k, :] if groups == 1 else squares[:, g:g + 2, :].rearrange("p j t -> p (j t)")
                last = nc.tensor.matmul(sums.tile[:, 0:some * T], self.k("ones"), rhs,
                                        start=k == 0, stop=k == per_group - 1)
            dve.wait(pe.done(last))
            for i in range(some * TB):
                col = g * TB + i
                dve.wait(self.diagonal_free)
                sums.free = self.diagonal_free = dve.done(nc.vector.tensor_tensor_reduce(
                    self.diagonal[:, :], sums.tile[:, i * P:(i + 1) * P], self.k("ident"), 1.0 / count, eps,
                    ALU.mult, ALU.add, mean[:, col:col + 1]))
        act.wait(self.diagonal_free)
        mark = act.done(nc.scalar.activation(tmp, mean, ACT.Sqrt))
        dve.wait(mark)
        dve.wait(dve.done(nc.vector.reciprocal(inv, tmp)))
        dve.wait(dve.done(nc.vector.tensor_tensor(tmp, mean, inv, ALU.mult)))
        dve.wait(dve.done(nc.vector.tensor_tensor(tmp, tmp, inv, ALU.mult)))
        dve.wait(dve.done(nc.vector.tensor_scalar(tmp, tmp, -0.5, 1.5, ALU.mult, ALU.add)))
        mark = dve.done(nc.vector.tensor_tensor(inv, inv, tmp, ALU.mult))
        yield
        pe.wait(mark)
        yield self.broadcast(st, inv, groups)

    def at_once(self, norm):
        next(norm)
        return next(norm)

    def broadcast(self, st, columns_, groups):
        banks = []
        for g in range(groups):
            if g % 2 == 0:
                bank = self.scores.take()
                self.pe.wait(bank.free)
                banks.append(bank)
            for b in range(TB):
                i = g * TB + b
                last = self.nc.tensor.matmul(
                    bank.tile[:, (g % 2) * T + b * P:(g % 2) * T + (b + 1) * P],
                    columns_[:, i:i + 1].to_broadcast([P, P]), self.k("ident"), start=True, stop=True)
            bank.ready = self.pe.done(last)
        st.free = bank.ready
        return banks

    def square(self, out, in_, ready):
        self.pool.wait(ready)
        self.pool.settle()
        return self.pool.done(self.nc.gpsimd.tensor_tensor(out, in_, in_, ALU.mult))

    def pipeline(self, units, filler):
        active, units = [], list(units)
        while active or units:
            if units:
                active.append(units.pop(0))
            active = [u for u in active if next(u, "ended") != "ended"]
            filler.step()

    def biased_scores(self, raw, raw_ready, buf, bias_op):
        nc, dve = self.nc, self.dve
        dve.wait(raw_ready, buf.free)
        raw.free = mark = dve.done(bias_op(buf.tile))
        dve.wait(mark)
        for i, (lo, hi) in enumerate(MAP_PARTS):
            buf.maxima = dve.done(nc.vector.tensor_reduce(buf.stat[:, i:i + 1], buf.tile[:, lo:hi], AX.X, ALU.max,
                                                          negate=True))

    def exponentials(self, buf):
        nc, dve, act, st = self.nc, self.dve, self.act, buf.stat
        act.wait(buf.maxima)
        for i, (lo, hi) in enumerate(MAP_PARTS):
            mark = act.done(nc.scalar.activation(buf.tile[:, lo:hi], buf.tile[:, lo:hi], ACT.Exp,
                                                 bias=st[:, i:i + 1], accum_out=st[:, 2 + i:3 + i]))
        dve.wait(mark)
        buf.inverted = dve.done(nc.vector.reciprocal(st[:, 4:6], st[:, 2:4]))
        dve.wait(buf.inverted)

    def transpose_map(self, probs, ready):
        nc = self.nc
        bank = self.turned.take()
        self.pe.wait(ready, bank.free)
        for i in range(3):
            last = nc.tensor.transpose(bank.tile[:, i * P:(i + 1) * P],
                                       probs.tile[:, i * P:(i + 1) * P], self.k("ident"))
        probs.free = mark = self.pe.done(last)
        pt = self.maps_t.take()
        self.act.wait(mark, pt.free)
        bank.free = pt.ready = self.act.done(nc.scalar.copy(pt.tile[:, :], bank.tile[:, 0:TRI]))
        return pt

    def weigh_values(self, out, v, cols, pt):
        nc = self.nc
        self.pe.wait(pt.ready)
        nc.tensor.matmul(out, v[:, 0, cols], pt.tile[:, 0:T], start=True, stop=False)
        pt.free = mark = self.pe.done(nc.tensor.matmul(
            out[:, P:T], v[:, 1, cols], pt.tile[:, T:TRI], start=False, stop=True))
        return mark

    def copy_to(self, dst, name, scale=1.0):
        def evacuate(tile, b, n, mark):
            self.act.wait(mark, self.reuse.get(name))
            if n == 2:
                got = self.act.done(self.nc.scalar.activation(
                    dst[:, b:b + 2, :], tile[:, :].rearrange("p (j t) -> p j t", j=2), ACT.Copy, scale=scale))
            else:
                got = self.act.done(self.nc.scalar.activation(dst[:, b, :], tile[:, 0:T], ACT.Copy, scale=scale))
            self.ready[name] = got
            return got
        return evacuate

    def silu_to(self, dst, name):
        def evacuate(tile, b, n, mark):
            self.act.wait(mark, self.reuse.get(name))
            z = dst[:, b:b + 2, :].rearrange("p j t -> p (j t)")
            self.dve.wait(self.act.done(self.nc.scalar.activation(z, tile[:, :], ACT.Tanh, scale=0.5)))
            self.ready[name] = self.dve.done(self.nc.vector.scalar_tensor_tensor(
                z, z, 1.0, tile[:, :], ALU.add, ALU.mult))
            return self.ready[name]
        return evacuate

    def tokens_to(self, dst, name):
        def evacuate(tile, u, mark):
            self.act.wait(mark, self.reuse.get(name))
            self.ready[name] = self.act.done(self.nc.scalar.copy(
                dst[:, :, u * 256:(u + 1) * 256], tile[:, :].rearrange("p (b n) -> p b n", b=TB)))
            return self.ready[name]
        return evacuate

    def first_stack(self, stack):
        nc = self.nc
        sb = lambda name, shape: stack.enter_context(nc.sbuf_tensor(name, shape, F32))
        pair = lambda name, shape: Split(*(stack.enter_context(nc.sbuf_tensor(f"{name}_{part}", shape, F32R))
                                           for part in ("hi", "lo")))
        self.ready, self.reuse = {}, {}
        b = self.b = {}
        b["x"] = pair("x", [P, DC, T])
        b["merged"] = sb("a_qk_then_merged", [P, DC, T])
        b["a_q"], b["a_k"] = b["merged"][:, 0:4, :], b["merged"][:, 4:8, :]
        c_qk = sb("latents_then_c_qk", [P, DC, T])
        b["cq"], b["ckv"] = c_qk[:, 0:3, :], c_qk[:, 3:5, :]
        b["c_q"], b["c_k"] = c_qk[:, 0:4, :], c_qk[:, 4:8, :]
        b["a_z"], b["c_z"] = sb("a_z_then_b_z", [P, 4, T]), sb("c_z", [P, 4, T])
        b["a_v"], b["c_v"] = sb("a_v_then_b_v", [P, TB, W]), sb("c_v", [P, TB, W])
        b["b_z"], b["b_v"] = b["a_z"], b["a_v"]
        b["b_q"], b["b_k"] = sb("b_q", [P, HEADS, T]), sb("b_k", [P, HEADS, T])
        b["gate"] = Turn([sb(f"gate{i}", [P, 2 * T]) for i in range(2)])
        b["late_gate"] = Turn([b["c_z"][:, j:j + 2, :].rearrange("p j t -> p (j t)") for j in (0, 2)])
        b["kr"] = sb("kr", [P, T])
        b["tmp"] = sb("tmp", [P, 2 * T])
        b["pT"] = b["c_q"][:, 0:PLE // P, :]
        b["p"] = pair("p", [P, PLE // P, T])
        y = b["y"] = pair("y", [P, DC + 1, T])
        b["cqn"] = Split(y.hi[:, 4:7, :], y.lo[:, 4:7, :])
        b["ckvn"] = Split(y.hi[:, 7:9, :], y.lo[:, 7:9, :])
        self.maps = Turn([sb(f"map{i}", [P, TRI]) for i in range(6)])
        for i, m in enumerate(self.maps.buffers):
            m.stat = sb(f"map_stat{i}", [P, 8])
        self.maps_t = Turn([sb(f"map_t{i}", [P, TRI]) for i in range(2)])
        self.diagonal = sb("diagonal", [P, P])
        b["lam"] = sb("lam", [P, 8])
        b["lam_prod"] = b["tmp"][:, 0:2 * DIFF_QK].rearrange("p (a d) -> p a d", a=2)
        self.p_sem = stack.enter_context(nc.semaphore("p_loaded"))
        x_dram, x_ready = self.a["x"].rearrange("(c p) t -> p c t", p=P), []
        for half in range(2):
            at = half * DC // 2
            loaded = stack.enter_context(nc.semaphore(f"x{half}_loaded"))
            nc.sync.dma_start(self.h[:, at:at + DC // 2, :], x_dram[:, at:at + DC // 2, :]).then_inc(loaded, 16)
            for c in range(at, at + DC // 2):
                x_ready.append(self.split_values(b["x"], (slice(None), c), self.h[:, c, :], (loaded, 16)))
            self.prepare()
        nc.sync.dma_start(self.small[:, :], self.a["small"]).then_inc(self.loaded, 16)
        nc.sync.dma_start(self.const["both"][:, :], self.a["constants_both"]).then_inc(self.loaded, 16)
        self.load_constants(stack, "first")
        self.h_ready = x_ready
        for l in range(DEPTH):
            self.first_layer(l)

    def constants_arrived(self):
        for e in (self.pe, self.dve, self.act, self.pool):
            e.wait((self.loaded, 32), self.const_loaded)
        self.cond_ready = self.act.done(self.nc.scalar.activation(self.cond[:, :], self.s("c", 8), ACT.Silu))
        for l in range(DEPTH):
            biases = self.s(f"b_merge{l}", 24)
            mark = self.dve.done(self.nc.vector.tensor_scalar(biases, biases, 0.5, None, ALU.mult))
        self.act.wait(mark)
        self.mods_pause = False

    def first_layer(self, l):
        nc, b, pe, dve, act, pool = self.nc, self.b, self.pe, self.dve, self.act, self.pool
        self.ready = {}
        ready, x, h, x_ready = self.ready, self.b["x"], self.h, self.h_ready

        def run(g):
            for _ in g:
                pass
        if l == 0:
            self.mods_pause = True
        run(self.dense(keys(f"b_cq{l}", 3), x, x_ready, self.copy_to(b["cq"], "cq")))
        if l == 0:
            self.constants_arrived()
        lam_init = 0.8 - 0.6 * math.exp(-0.3 * l)
        lam, prod = b["lam"], b["lam_prod"]
        lf = self.s(f"lambda{l}", 256).rearrange("p (a b d) -> p a b d", a=2, b=2)
        dve.wait(dve.done(nc.vector.tensor_tensor(prod[:, :, :], lf[:, :, 0, :], lf[:, :, 1, :], ALU.mult)))
        mark = dve.done(nc.vector.tensor_reduce(lam[:, 0:2], prod[:, :, :], AX.X, ALU.add))
        act.wait(mark)
        mark = act.done(nc.scalar.activation(lam[:, 2:4], lam[:, 0:2], ACT.Exp))
        dve.wait(mark)
        dve.wait(dve.done(nc.vector.scalar_tensor_tensor(lam[:, 4:5], lam[:, 3:4], -lam_init, lam[:, 2:3],
                                                         ALU.add, ALU.subtract)))
        mark = dve.done(nc.vector.tensor_scalar(lam[:, 5:6], self.s(f"subln{l}"), 0.5 * (1.0 - lam_init), None, ALU.mult))
        dve.wait(mark)
        neg_lam, subln = lam[:, 4:5], lam[:, 5:6]

        run(self.dense(keys(f"b_ckvr{l}", 1), x, None, self.copy_to(b["ckv"], "ckv")))
        slot = self.weights((f"b_ckvr{l}", 1))
        bank = self.products.take()
        pe.wait(bank.free)
        for j, (lo, hi) in enumerate(((0, P), (64, 160))):
            last = self.split_product(
                bank.tile[0:hi - lo, j * T:(j + 1) * T],
                [((slot.hi[:, k, lo:hi], slot.lo[:, k, lo:hi]), (x.hi[:, k, :], x.lo[:, k, :])) for k in range(DC)])
        slot.free = mark = pe.done(last)
        act.wait(mark)
        act.done(nc.scalar.copy(b["ckv"][:, 1, :], bank.tile[:, 0:T]))
        bank.free = ready["ckv"] = ready["kr"] = act.done(nc.scalar.copy(b["kr"][64:96, :], bank.tile[64:96, T:2 * T]))
        self.count_unit()

        sq_q = self.square(b["b_q"][:, 0:3, :], b["cq"], [ready["cq"], self.reuse.get("b_q")])
        sq_kv = self.square(b["b_k"][:, 0:2, :], b["ckv"], [ready["ckv"], self.reuse.get("b_k")])
        run(self.dense(keys(f"a_q{l}", 2), x, None, self.copy_to(b["a_q"], "a_q", HD ** -0.5)))
        run(self.dense(keys(f"a_k{l}", 2), x, None, self.copy_to(b["a_k"], "a_k")))
        norms = [self.inverse_rms(b["b_q"], 1, 3, Q_LORA, 1e-6, sq_q),
                 self.inverse_rms(b["b_k"], 1, 2, KV_LORA, 1e-6, sq_kv)]
        for n in norms:
            next(n)
        a_v = self.token_major(keys(f"a_v{l}", 2), x, None, self.tokens_to(b["a_v"], "a_v"))
        next(a_v)
        act.wait(self.reuse.get("y"))
        for norm, name, chunks in zip(norms, ("cq", "ckv"), (3, 2)):
            (bank,), buf = next(norm), b[name]
            dve.wait(bank.ready)
            for c in range(chunks):
                mark = dve.done(nc.vector.scalar_tensor_tensor(
                    buf[:, c, :], buf[:, c, :], self.s(f"g{name[1:]}{l}", 1, c), bank.tile[:, 0:T],
                    ALU.mult, ALU.mult))
            bank.free = mark
            ready[name + "n"] = self.split_values(b[name + "n"], (slice(None), slice(None)), buf, mark)
        run(a_v)

        def rope32(raw, heads, mark):
            bank = self.turned.take()
            pe.wait(mark, bank.free)
            rows = slice(64, 96)
            n = heads * T
            mark = pe.done(nc.tensor.matmul(bank.tile[rows, 0:n], self.k("swap16")[rows, :], raw,
                                            start=True, stop=True))
            dve.wait(mark, self.reuse.get("tmp"))
            table = lambda name: self.per_head(self.k(name)[rows, :], 1).to_broadcast([32, heads, T])
            tmp = self.per_head(b["tmp"][rows, 0:n], heads)
            bank.free = dve.done(nc.vector.tensor_tensor(tmp, self.per_head(bank.tile[rows, 0:n], heads),
                                                         table("sin32"), ALU.mult))
            dve.wait(dve.done(nc.vector.tensor_tensor(raw, raw, table("cos32"), ALU.mult)))
            self.reuse["tmp"] = dve.done(nc.vector.tensor_tensor(raw, raw, tmp, ALU.add))
            return self.reuse["tmp"]

        unrotated = []

        def rotate_q(mark=None, heads_at=None):
            for m, at in unrotated:
                ready["b_q"] = rope32(b["b_q"][64:96, at:at + 2, :], 2, m)
            unrotated[:] = [(mark, heads_at)] if mark else []

        def mla_q():
            cq = b["cqn"]
            for u in range(2):
                slot = self.weights((f"uq{l}", u))
                pe.wait(ready["cqn"])
                for h0 in range(0, 4, 2):
                    bank = self.products.take()
                    pe.wait(bank.free)
                    for j in range(2):
                        cols = slice((h0 + j) * 96, (h0 + j + 1) * 96)
                        last = self.split_product(
                            bank.tile[0:96, j * T:(j + 1) * T],
                            [((slot.hi[:, k, cols], slot.lo[:, k, cols]), (cq.hi[:, k, :], cq.lo[:, k, :]))
                             for k in range(3)])
                    slot.free = mark = pe.done(last)
                    act.wait(mark)
                    hh = 4 * u + h0
                    bank.free = mark = act.done(nc.scalar.copy(
                        b["b_q"][0:96, hh:hh + 2, :], bank.tile[0:96, :].rearrange("p (j t) -> p j t", j=2)))
                    rotate_q(mark, hh)
                    yield
                self.count_unit()

        def mla_kv():
            rotate_q()
            while "ya" not in ready:
                yield
            self.reuse["b_v"] = self.reuse["b_z"] = ready["ya"]
            ready["merge_a_done"] = self.reuse["ya"]
            mark = rope32(self.per_head(b["kr"][64:96, :], 1), 1, ready["kr"])
            slot = self.weights((f"ukv{l}", 0))
            hi, lo = (t.rearrange("p k (h c) -> p k h c", h=HEADS) for t in (slot.hi, slot.lo))
            ckv = b["ckvn"]
            pool.wait(mark)
            for h in range(HEADS):
                pool.settle()
                ready["b_k_rope"] = pool.done(nc.gpsimd.tensor_copy(b["b_k"][64:96, h, :], b["kr"][64:96, :]))
            pe.wait(ready["ckvn"])
            for h in range(0, HEADS, 2):
                bank = self.products.take()
                pe.wait(bank.free)
                for j in range(2):
                    cols = slice((h + j) * P, (h + j + 1) * P)
                    last = self.split_product(
                        bank.tile[:, j * T:(j + 1) * T],
                        [((slot.hi[:, k, cols], slot.lo[:, k, cols]), (ckv.hi[:, k, :], ckv.lo[:, k, :]))
                         for k in range(2)])
                mark = pe.done(last)
                act.wait(mark)
                bank.free = ready["b_k"] = act.done(nc.scalar.copy(
                    b["b_k"][0:64, h:h + 2, :], bank.tile[0:64, :].rearrange("p (j t) -> p j t", j=2)))
                if h % 4 == 2:
                    yield
            for t in range(TB):
                bank = self.products.take()
                pe.wait(bank.free)
                tok = slice(t * P, (t + 1) * P)
                last = self.split_product(
                    bank.tile[:, :].rearrange("p (h c) -> p h c", h=HEADS),
                    [((ckv.hi[:, k, tok], ckv.lo[:, k, tok]), (hi[:, k, :, NOPE:P], lo[:, k, :, NOPE:P]))
                     for k in range(2)])
                slot.free = mark = pe.done(last)
                act.wait(mark, self.reuse.get("b_v"))
                bank.free = ready["b_v"] = act.done(nc.scalar.copy(b["b_v"][:, t, :], bank.tile[:, :]))
            self.reuse["latents"] = slot.free
            self.count_unit()
            yield

        merged, y = b["merged"], b["y"]
        gates = []

        def gate(i):
            def evacuate(tile, at, n, mark):
                buf = b["gate"].take() if len(gates) < 2 else b["late_gate"].take()
                act.wait(ready["ycn"] if len(gates) >= 2 else None)
                act.wait(mark, buf.free)
                for j in range(n):
                    buf.ready = act.done(nc.scalar.activation(
                        buf.tile[:, j * T:(j + 1) * T], tile[:, j * T:(j + 1) * T], ACT.Tanh, scale=0.5,
                        bias=self.s(f"b_merge{l}", 1, i * DC + at + j)))
                gates.append(buf)
                return buf.ready
            return evacuate

        def weigh(i):
            def evacuate(tile, at, n, mark):
                buf = gates.pop(0)
                m = merged[:, at:at + 2, :].rearrange("p j t -> p (j t)")
                dve.wait(mark, buf.ready)
                if i == 0:
                    buf.free = ready["merged"] = dve.done(nc.vector.scalar_tensor_tensor(
                        m, buf.tile[:, :], 1.0, tile[:, :], ALU.add, ALU.mult))
                    return buf.free
                dve.wait(ready["merged"])
                got = dve.done(nc.vector.scalar_tensor_tensor(
                    buf.tile[:, :], buf.tile[:, :], 1.0, tile[:, :], ALU.add, ALU.mult))
                dve.wait(got)
                buf.free = ready["merged"] = dve.done(nc.vector.tensor_tensor(m, m, buf.tile[:, :], ALU.add))
                if i == 1 and at < DC // 2:
                    split_merged(at)
                return got
            return evacuate

        merged_ready = []

        def split_merged(at):
            act.wait(self.reuse["ycn"] if at < DC // 2 else self.reuse["yb"], ready["merged"])
            for c in (at, at + 1):
                to = (c + DC // 2) % DC
                dve.wait(act.done(nc.scalar.activation(y.hi[:, to, :], merged[:, c, :], ACT.Copy, scale=0.5)))
                merged_ready.append(dve.done(nc.vector.scalar_tensor_tensor(
                    y.lo[:, to, :], merged[:, c, :], 0.5, y.hi[:, to, :].bitcast(F32), ALU.mult, ALU.subtract)))

        def merge(i, branch, y_at, y_ready):
            branch_x = Split(y.hi[:, y_at:y_at + 4, :], y.lo[:, y_at:y_at + 4, :])
            while y_ready not in ready:
                yield
            for j in range(DC // MERGE_BLOCKS):
                yield from self.dense([(f"gate_{branch}{l}", j)], x, None, gate(i), first=MERGE_BLOCKS * j)
                yield from self.dense([(f"branch_{branch}{l}", j)], branch_x, ready[y_ready], weigh(i),
                                      first=MERGE_BLOCKS * j)
            self.reuse[y_ready] = (pe.semaphore, pe.count)

        def fill():
            k2 = lambda n: keys(f"{n}{l}", 2)
            yield from self.dense(k2("a_z"), x, None, self.silu_to(b["a_z"], "a_z"))
            self.reuse["c_q"] = self.reuse["c_k"] = [ready["cqn"], ready["ckvn"]]
            yield from self.dense(k2("c_q"), x, None, self.copy_to(b["c_q"], "c_q", DIFF_QK ** -0.5))
            yield from self.dense(k2("c_k"), x, None, self.copy_to(b["c_k"], "c_k"))
            yield from self.token_major(k2("c_v"), x, None, self.tokens_to(b["c_v"], "c_v"))
            yield "differential attention can start"
            yield from self.dense(k2("c_z"), x, None, self.silu_to(b["c_z"], "c_z"))
            yield from mla_q()
            yield from merge(0, "a", 0, "ya")
            yield from mla_kv()
            yield "MLA can start"
            yield from self.dense(k2("b_z"), x, None, self.silu_to(b["b_z"], "b_z"))
            yield from merge(2, "c", 4, "ycn")
            yield from self.dense(keys(f"gate_b{l}", DC // MERGE_BLOCKS), x, None, gate(1))
        filler = Filler(fill())

        def causal_scores(raw, q, k_):
            nc.tensor.matmul(raw.tile[:, 0:P], q[..., 0:P], k_[..., 0:P], start=True, stop=True)
            return pe.done(nc.tensor.matmul(raw.tile[:, P:TRI], q[..., P:T], k_, start=True, stop=True))

        def two_heads(h, values, z, y_name, probs, mark):
            rows, c = slice(64 * (h % 2), 64 * (h % 2) + 64), h // 2
            yield
            yield
            pt = self.transpose_map(probs, mark)
            yield
            if h % 2 == 0:
                state["bank"] = self.values.take()
                pe.wait(state["bank"].free)
            bank = state["bank"]
            mark = self.weigh_values(bank.tile[rows, 0:T], b[values], slice(h * HD, (h + 1) * HD), pt)
            if h % 2 == 0:
                return
            dve.wait(mark, ready[z])
            bank.free = mark = dve.done(nc.vector.scalar_tensor_tensor(
                b[z][:, c, :], bank.tile[:, 0:T], 0.5, b[z][:, c, :], ALU.mult, ALU.mult))
            yield
            act.wait(self.reuse.get("y"), ready.get("merge_a_done"))
            mark = self.split_values(y, (slice(None), c), b[z][:, c, :], mark)
            if h == HEADS - 1:
                ready[y_name] = mark
        state = {}

        def moba(h):
            rows, c = slice(64 * (h % 2), 64 * (h % 2) + 64), h // 2
            raw, probs = self.scores.take(), self.maps.take()
            pe.wait(ready["a_q"], ready["a_k"], raw.free)
            mark = causal_scores(raw, b["a_q"][rows, c, :], b["a_k"][rows, c, :])
            self.biased_scores(raw, mark, probs, lambda o: nc.vector.scalar_tensor_tensor(
                o[:, :], self.k("dist"), -float(MOBA_SLOPES[h]), raw.tile[:, 0:TRI], ALU.mult, ALU.add))
            self.exponentials(probs)
            mark = self.normalise(probs)
            yield from two_heads(h, "a_v", "a_z", "ya", probs, mark)

        yc, yc_sq = b["c_q"], b["c_k"]

        def diff(h):
            filler.until("differential attention can start")
            p_maps = []
            for m in range(2):
                rows = slice(64 * m, 64 * m + 64)
                raw, probs = self.scores.take(), self.maps.take()
                pe.wait(ready["c_q"], ready["c_k"], raw.free)
                mark = causal_scores(raw, b["c_q"][rows, h, :], b["c_k"][rows, h, :])
                self.biased_scores(raw, mark, probs, lambda o: nc.vector.scalar_tensor_tensor(
                    o[:, :], self.k("dist"), -float(DIFF_SLOPES[h]), raw.tile[:, 0:TRI], ALU.mult, ALU.add))
                p_maps.append(probs)
            first, second = p_maps
            self.exponentials(first)
            self.exponentials(second)
            normalised = self.normalise(first)
            st = second.stat
            dve.wait(dve.done(nc.vector.tensor_scalar(st[:, 6:8], st[:, 4:6], neg_lam, None, ALU.mult)))
            dve.wait(normalised)
            for i, (lo, hi) in enumerate(MAP_PARTS):
                mark = dve.done(nc.vector.scalar_tensor_tensor(
                    first.tile[:, lo:hi], second.tile[:, lo:hi], st[:, 6 + i:7 + i], first.tile[:, lo:hi],
                    ALU.mult, ALU.add))
            second.free = mark
            yield
            pt = self.transpose_map(first, mark)
            yield
            bank = self.turned.take()
            pe.wait(bank.free)
            mark = self.weigh_values(bank.tile[:, 0:T], b["c_v"], slice(h * P, (h + 1) * P), pt)
            act.wait(mark)
            bank.free = ready["yc"] = mark = act.done(nc.scalar.copy(yc[:, h, :], bank.tile[:, 0:T]))
            ready["yc_sq"] = self.square(yc_sq[:, h, :], yc[:, h, :], mark)

        def diff_norm():
            yield
            yield
            norm = self.inverse_rms(yc_sq, 4, 1, P, 1e-5, ready["yc_sq"])
            next(norm)
            yield
            banks = next(norm)
            for g in range(0, 4, 2):
                bank = banks[g // 2]
                both = yc[:, g:g + 2, :].rearrange("p j t -> p (j t)")
                z = b["c_z"][:, g:g + 2, :].rearrange("p j t -> p (j t)")
                dve.wait(bank.ready, ready["yc"], ready["c_z"])
                bank.free = mark = dve.done(nc.vector.tensor_tensor(both, both, bank.tile[:, :], ALU.mult))
                dve.wait(mark)
                mark = dve.done(nc.vector.scalar_tensor_tensor(z, both, subln, z, ALU.mult, ALU.mult))
                act.wait(self.reuse["latents"])
                ycn = self.split_values(y, (slice(None), slice(4 + g, 6 + g)), b["c_z"][:, g:g + 2, :], mark)
            ready["ycn"] = ycn

        def mla(h):
            filler.until("MLA can start")
            if h == HEADS - 1:
                self.sp.wait(ready["ycn"])
                nc.sync.dma_start(b["pT"], self.a["p"][l].rearrange("(c p) t -> p c t", p=P)).then_inc(self.p_sem, 16)
            raw, probs = self.scores.take(), self.maps.take()
            pe.wait(ready["b_q"], ready["b_k"], ready["b_k_rope"], raw.free)
            mark = causal_scores(raw, b["b_q"][0:96, h, :], b["b_k"][0:96, h, :])
            self.biased_scores(raw, mark, probs, lambda o: nc.vector.scalar_tensor_tensor(
                o[:, :], raw.tile[:, 0:TRI], (NOPE + ROPE) ** -0.5, self.k("causal"), ALU.mult, ALU.add))
            self.exponentials(probs)
            mark = self.normalise(probs)
            yield from two_heads(h, "b_v", "b_z", "yb", probs, mark)

        self.pipeline([moba(h) for h in range(HEADS)] + [diff(h) for h in range(DIFF_HEADS)] + [diff_norm()]
                      + [mla(h) for h in range(HEADS)], filler)
        while filler.step():
            pass
        branch_b = Split(y.hi[:, 0:4, :], y.lo[:, 0:4, :])
        self.pause_mods()
        for i, _ in enumerate(self.dense(keys(f"branch_b{l}", DC // MERGE_BLOCKS), branch_b, ready["yb"], weigh(1))):
            if i == 1:
                p_ready = self.split_values(b["p"], (slice(None), slice(None)), b["pT"], (self.p_sem, 16 * (l + 1)))
                self.reuse["cq"] = p_ready
        self.reuse["yb"] = (pe.semaphore, pe.count)
        self.reuse["a_z"] = self.reuse["a_v"] = ready["yb"]
        self.reuse["c_z"] = self.reuse["c_v"] = [ready["ycn"], ready["merged"]]

        pp = b["b_k"]
        for at in (4, 6):
            split_merged(at)
        run(self.dense([(f"ple{l}", 0)], b["p"], p_ready, self.copy_to(pp, "pp")))
        self.mods_pause = False

        r_ready = []

        def residual(tile, at, n, mark):
            r = h[:, at:at + 2, :].rearrange("p j t -> p (j t)")
            dve.wait(mark)
            got = dve.done(nc.vector.scalar_tensor_tensor(r, r, ALPHA, tile[:, :], ALU.mult, ALU.add))
            for j in range(2):
                r_ready.append(self.split_values(x, (slice(None), at + j), h[:, at + j, :], got))
            return got
        run(self.dense(keys(f"w_out{l}", 4), y, merged_ready, residual, x_from=DC // 2))
        run(self.dense([(f"ple{l}", 1)], b["p"], None, self.copy_to(pp, "pp"), first=DC // 2))
        self.reuse["y"] = (pe.semaphore, pe.count)
        r2, sg, r2_ready = b["b_q"], b["merged"], []

        def ple(tile, c, n, mark):
            act.wait(mark, merged_ready[-1])
            s_ = sg[:, c:c + 2, :].rearrange("p j t -> p (j t)")
            q_ = pp[:, c:c + 2, :].rearrange("p j t -> p (j t)")
            r_ = h[:, c:c + 2, :].rearrange("p j t -> p (j t)")
            o_ = r2[:, c:c + 2, :].rearrange("p j t -> p (j t)")
            got = act.done(nc.scalar.activation(s_, tile[:, :], ACT.Tanh, scale=0.5))
            dve.wait(got, ready["pp"])
            dve.wait(dve.done(nc.vector.scalar_tensor_tensor(s_, s_, 1.0, q_, ALU.add, ALU.mult)))
            r2_ready.extend([dve.done(nc.vector.scalar_tensor_tensor(o_, s_, 0.5, r_, ALU.mult, ALU.add))] * 2)
            return got
        run(self.dense(keys(f"ple_gate{l}", 4), x, r_ready, ple))

        bank = self.turned.take()
        pe.wait(bank.free)
        for k in range(DC):
            pe.wait(r2_ready[k])
            last = nc.tensor.matmul(bank.tile[:, 0:T], self.k("ones"), r2[:, k, :], start=k == 0, stop=k == DC - 1)
        dve.wait(pe.done(last))
        sq, sq_ready = b["merged"], []
        for c in range(DC):
            bank.free = mark = dve.done(nc.vector.scalar_tensor_tensor(
                r2[:, c, :], bank.tile[:, 0:T], -1.0 / D, r2[:, c, :], ALU.mult, ALU.add))
            act.wait(mark)
            sq_ready.append(act.done(nc.scalar.activation(sq[:, c, :], r2[:, c, :], ACT.Square)))
        (bank,) = self.at_once(self.inverse_rms(sq, 1, DC, D, 1e-5, sq_ready))
        self.h_ready = []
        dve.wait(bank.ready)
        shifted = []
        for c in range(DC + 1):
            if c < DC:
                bank.free = mark = dve.done(nc.vector.scalar_tensor_tensor(
                    r2[:, c, :], r2[:, c, :], self.s(f"ln_g{l}", 1, c), bank.tile[:, 0:T], ALU.mult, ALU.mult))
                act.wait(mark)
                shifted.append(act.done(nc.scalar.activation(
                    h[:, c, :], r2[:, c, :], ACT.Identity, bias=self.s(f"ln_b{l}", 1, c))))
                if l < DEPTH - 1:
                    act.wait(shifted[c])
                    shifted[c] = act.done(nc.scalar.copy(x.hi[:, c, :], h[:, c, :]))
                else:
                    self.h_ready.append(shifted[c])
            if c > 0 and l < DEPTH - 1:
                dve.wait(shifted[c - 1])
                self.h_ready.append(dve.done(nc.vector.tensor_tensor(
                    x.lo[:, c - 1, :], h[:, c - 1, :], x.hi[:, c - 1, :].bitcast(F32), ALU.subtract)))
        self.reuse["b_q"] = self.reuse["b_k"] = self.reuse["cq"] = self.reuse["ckv"] = self.h_ready[-1]
        self.reuse["a_q"] = self.reuse["a_k"] = self.h_ready[-1]

    def normalise(self, probs):
        self.act.wait(probs.inverted)
        for i, (lo, hi) in enumerate(MAP_PARTS):
            mark = self.act.done(self.nc.scalar.activation(
                probs.tile[:, lo:hi], probs.tile[:, lo:hi], ACT.Copy, scale=probs.stat[:, 4 + i:5 + i]))
        return mark

    def second_stack(self, stack, out):
        nc = self.nc
        sb = lambda name, shape: stack.enter_context(nc.sbuf_tensor(name, shape, F32))
        self.ready, self.reuse = {}, {}
        b = self.b = {}
        pair = lambda name, shape: Split(*(stack.enter_context(nc.sbuf_tensor(f"{name}_{part}", shape, F32R))
                                           for part in ("hi", "lo")))
        b["u"] = pair("u", [P, DC, T])
        b["y"] = pair("y2", [P, HIDDEN_BLOCKS, T])
        hidden = [sb(f"hidden{i}", [P, 2 * T]) for i in range(2)]
        b["hidden"] = Turn(hidden)
        b["norm"] = Turn([h_[:, j * T:(j + 1) * T] for h_ in hidden for j in range(2)])
        b["tmp"] = hidden[0]
        for n in ("r_q", "r_k", "r_g", "m_z"):
            b[n] = sb(n, [P, 4, T])
        b["y_r"] = b["r_q"]
        for n in ("r_v", "s_v"):
            b[n] = sb(n, [P, TB, 512])
        b["squares"] = sb("squares", [P, DC, T])
        b["s_q"], b["s_k"] = b["squares"][:, 0:4, :], b["squares"][:, 4:8, :]
        xbc_in = sb("xbc_in", [P, XBC // P * (T + TAPS - 1)])
        b["xbc_in"] = xbc_in[:, :].rearrange("p (c t) -> p c t", c=XBC // P)
        b["xbc"] = sb("xbc", [P, XBC // P, T])
        b["m_v"] = xbc_in[:, 0:1024].rearrange("p (b n) -> p b n", b=TB)
        b["y_m"] = xbc_in[:, 1024:2048].rearrange("p (c t) -> p c t", c=4)
        b["stick_space"] = xbc_in[:, 0:3 * TRI].rearrange("p (i n) -> p i n", i=3)
        b["dt"] = sb("dt", [P, 6, 2 * MH])
        b["cum"] = sb("cum", [P, 4, MH])
        b["neg_a"] = sb("neg_a", [P, MH])
        b["cb"] = sb("keep_then_cb", [P, MG, TRI])
        b["coef"] = sb("coef", [P, 2, DC])
        self.sp.wait(self.h_ready)
        self.load_constants(stack, "second")
        self.maps = Turn([sb(f"work{i}", [P, TRI]) for i in range(3)])
        self.diagonal = self.maps.buffers[0].tile[:, 0:P]
        self.maps_t = Turn([sb(f"weights_t{i}", [P, TRI]) for i in range(4)])
        self.dve.wait(self.h_ready)
        self.pool.wait(self.h_ready)
        self.act.wait(self.h_ready)
        self.sp.wait(self.h_ready)
        for l in range(DEPTH):
            self.second_layer(l)
        marks = self.modulated_norm("final_norm", DEPTH * 72, DEPTH * 72 + 8, None)
        written = stack.enter_context(nc.semaphore("written"))
        for c in range(0, DC, 2):
            self.sp.wait(marks[c + 1])
            nc.sync.dma_start(out.rearrange("(c p) t -> p c t", p=P)[:, c:c + 2, :],
                              self.b["xbc"][:, c:c + 2, :]).then_inc(written, 16)
        nc.sync.wait_ge(written, 16 * (DC // 2))

    def modulated_norm(self, gain, shift_at, scale_at, dst):
        nc, b, dve, act = self.nc, self.b, self.dve, self.act
        h, coef, sq = self.h, b["coef"], []
        for c in range(DC):
            act.wait(self.h_ready[c], self.reuse.get("squares"))
            sq.append(act.done(nc.scalar.activation(b["squares"][:, c, :], h[:, c, :], ACT.Square)))
        self.mods_until(max(shift_at, scale_at) + DC)
        dve.wait(self.mod_last)
        dve.wait(dve.done(nc.vector.scalar_tensor_tensor(
            coef[:, 0, :], self.mods[:, scale_at:scale_at + DC], 1.0, self.s(gain, DC), ALU.add, ALU.mult)))
        (bank,) = self.at_once(self.inverse_rms(b["squares"], 1, DC, D, 1e-6, sq, ring=self.values))
        self.reuse["squares"] = bank.ready
        marks = []
        dve.wait(bank.ready)
        act.wait(self.reuse.get("u"))
        shifts = [self.mods[:, shift_at + c:shift_at + c + 1] for c in range(DC)]
        bufs, shifted = [], []
        for c in range(DC + 1):
            if c < DC:
                buf = b["norm"].take()
                bufs.append(buf)
                dve.wait(buf.free)
                bank.free = mark = dve.done(nc.vector.scalar_tensor_tensor(
                    buf.tile, h[:, c, :], coef[:, 0, c:c + 1], bank.tile[:, 0:T], ALU.mult, ALU.mult))
                act.wait(mark)
                to = b["xbc"] if dst is None else dst.hi
                shifted.append(act.done(nc.scalar.activation(to[:, c, :], buf.tile, ACT.Identity, bias=shifts[c])))
                if dst is None:
                    buf.free = shifted[c]
            if c > 0 and dst is not None:
                dve.wait(shifted[c - 1])
                bufs[c - 1].free = dve.done(nc.vector.scalar_tensor_tensor(
                    dst.lo[:, c - 1, :], bufs[c - 1].tile, shifts[c - 1], dst.hi[:, c - 1, :].bitcast(F32),
                    ALU.add, ALU.subtract))
                marks.append(bufs[c - 1].free)
        marks = marks or shifted
        return marks

    def run(self, g):
        for _ in g:
            pass

    def feed_forward(self, l, n, gain, at):
        nc, b, dve, act = self.nc, self.b, self.dve, self.act
        u, ff = b["u"], b["y"]
        marks = self.modulated_norm(gain, at, at + DC, u)
        self.gate_coefficients(at + 2 * DC, 0.5)
        banks = [self.scores.take(), self.scores.take(), self.turned.take(), self.turned.take()]
        pairs = FC // 2
        places = HIDDEN_BLOCKS // 2
        hidden_ready, place_free = {}, [self.reuse.get("y")] * places
        state = {}

        def gate(tile, blk, m, mark):
            buf = b["hidden"].take()
            act.wait(mark, buf.free)
            state["buf"] = buf
            state["gate"] = act.done(nc.scalar.activation(buf.tile[:, :], tile[:, :], ACT.Silu))
            return state["gate"]

        def up(i):
            def evacuate(tile, blk, m, mark):
                buf = state["buf"]
                dve.wait(mark, state["gate"])
                got = dve.done(nc.vector.tensor_tensor(buf.tile[:, :], tile[:, :], buf.tile[:, :], ALU.mult))
                act.wait(place_free[i % places])
                at_ = 2 * (i % places)
                buf.free = hidden_ready[i] = self.split_values(
                    ff, (slice(None), slice(at_, at_ + 2)), buf.tile[:, :].rearrange("p (j t) -> p j t", j=2), got)
                return got
            return evacuate
        for i in range(pairs + 1):
            if i < pairs:
                self.run(self.dense([(f"wg{n}{l}", i)], u, marks, gate))
                self.run(self.dense([(f"wu{n}{l}", i)], u, None, up(i)))
            if i > 0:
                slot = self.weights((f"wd{n}{l}", i - 1))
                self.run(self.accumulate(slot, banks, ff, 2 * ((i - 1) % places), hidden_ready[i - 1],
                                         i == 1, i == pairs))
                place_free[(i - 1) % places] = slot.free
        self.reuse["y"] = self.reuse["u"] = slot.free
        self.add_to_h(banks)

    def gate_coefficients(self, gate_at, factor):
        self.mods_until(gate_at + DC)
        self.dve.wait(self.mod_last)
        self.dve.wait(self.dve.done(self.nc.vector.tensor_scalar(
            self.b["coef"][:, 1, :], self.mods[:, gate_at:gate_at + DC], factor, factor, ALU.mult, ALU.add)))

    def add_to_h(self, banks):
        h, dve = self.h, self.dve
        self.h_ready = []
        for c in range(DC):
            bank = banks[c // 2]
            dve.wait(bank.ready)
            bank.free = got = dve.done(self.nc.vector.scalar_tensor_tensor(
                h[:, c, :], bank.tile[:, (c % 2) * T:(c % 2 + 1) * T], self.b["coef"][:, 1, c:c + 1], h[:, c, :],
                ALU.mult, ALU.add))
            self.h_ready.append(got)

    def second_layer(self, l):
        at = 72 * l
        self.feed_forward(l, 1, f"norm_ffn1{l}", at)
        self.mixers(l, at + 3 * DC)
        self.feed_forward(l, 2, f"norm_ffn2{l}", at + 6 * DC)

    def mixers(self, l, at):
        nc, b, pe, dve, act = self.nc, self.b, self.pe, self.dve, self.act
        ready, u, y, y_m, y_r = self.ready, b["u"], b["y"], b["y_m"], b["y_r"]
        marks = self.modulated_norm(f"norm_mix{l}", at, at + DC, u)
        self.gate_coefficients(at + 2 * DC, 1.0)
        k2 = lambda n: keys(f"{n}{l}", 2)

        for e in (pe, dve):
            e.wait(self.const_loaded)

        dve.wait(self.reuse.get("xbc_in"))
        self.pad_ready = dve.done(nc.vector.memset(b["xbc_in"][:, :, 0:TAPS - 1], 0.0))
        def conv_in(base):
            def evacuate(tile, blk, n, mark):
                act.wait(mark, self.pad_ready)
                got = act.done(nc.scalar.copy(b["xbc_in"][:, base + blk:base + blk + 2, TAPS - 1:],
                                              tile[:, :].rearrange("p (j t) -> p j t", j=2)))
                dve.wait(got)
                for c in (base + blk, base + blk + 1):
                    src, dst = b["xbc_in"], b["xbc"]
                    tap = lambda i: self.s(f"conv_w{l}", 1, 8 * i + c)
                    m = dve.done(nc.vector.tensor_scalar(dst[:, c, :], src[:, c, 0:T], tap(0), None, ALU.mult))
                    for i in range(1, TAPS):
                        dve.wait(m)
                        m = dve.done(nc.vector.scalar_tensor_tensor(
                            dst[:, c, :], src[:, c, i:i + T], tap(i), dst[:, c, :], ALU.mult, ALU.add))
                    act.wait(m)
                    ready["xbc"] = act.done(nc.scalar.activation(dst[:, c, :], dst[:, c, :], ACT.Silu,
                                                                 bias=self.s(f"conv_b{l}", 1, c)))
                return got
            return evacuate
        self.run(self.dense(k2("m_x"), u, marks, conv_in(0)))
        self.run(self.dense(k2("m_bc"), u, None, conv_in(4)))

        slot = self.weights((f"m_dt{l}", 0))
        bank = self.products.take()
        pe.wait(bank.free)
        for t in range(TB):
            tok = slice(t * P, (t + 1) * P)
            last = self.split_product(
                bank.tile[:, t * MH:(t + 1) * MH],
                [((u.hi[:, k, tok], u.lo[:, k, tok]), (slot.hi[:, k, :], slot.lo[:, k, :])) for k in range(DC)])
        slot.free = mark = pe.done(last)
        self.count_unit()
        z, az, ez, lz, dt, da = (b["dt"][:, i, :] for i in range(6))
        dve.wait(mark)
        for t in range(TB):
            bank.free = m = dve.done(nc.vector.tensor_tensor(
                z[:, t * MH:(t + 1) * MH], bank.tile[:, t * MH:(t + 1) * MH], self.s(f"dt_bias{l}", MH), ALU.add))
        act.wait(m)
        act.wait(act.done(nc.scalar.activation(az, z, ACT.Abs)))
        act.wait(act.done(nc.scalar.activation(ez, az, ACT.Exp, scale=-1.0)))
        act.done(nc.scalar.activation(b["neg_a"][:, :], self.s(f"a_log{l}", MH), ACT.Exp))
        m = act.done(nc.scalar.activation(lz, ez, ACT.Ln, bias=1.0))
        dve.wait(m)
        dve.wait(dve.done(nc.vector.scalar_tensor_tensor(dt, z, 0.0, lz, ALU.max, ALU.add)))
        for t in range(TB):
            cols = slice(t * MH, (t + 1) * MH)
            da_ready = dve.done(nc.vector.scalar_tensor_tensor(da[:, cols], dt[:, cols], -1.0, b["neg_a"][:, :],
                                                               ALU.mult, ALU.mult))

        def rotate(name, c):
            both = b[name][:, c:c + 2, :]
            table = lambda n: self.per_head(self.k(n), 1).to_broadcast([P, 2, T])
            bank = self.turned.take()
            pe.wait(ready[name], bank.free)
            m = pe.done(nc.tensor.matmul(bank.tile[:, :], self.k("swap64"), both, start=True, stop=True))
            dve.wait(m, self.reuse.get("tmp"))
            tmp = self.per_head(b["tmp"][:, :], 2)
            bank.free = dve.done(nc.vector.tensor_tensor(tmp, self.per_head(bank.tile[:, :], 2), table("sin128"),
                                                         ALU.mult))
            dve.wait(dve.done(nc.vector.tensor_tensor(both, both, table("cos128"), ALU.mult)))
            self.reuse["tmp"] = ready[name + "_rot"] = dve.done(nc.vector.tensor_tensor(both, both, tmp, ALU.add))

        def fill():
            yield from self.dense(k2("s_q"), u, None, self.copy_to(b["s_q"], "s_q", SBD ** -0.5))
            yield from self.dense(k2("s_k"), u, None, self.copy_to(b["s_k"], "s_k"))
            yield "stick-breaking can start"
            yield from self.token_major(k2("s_v"), u, None, self.tokens_to(b["s_v"], "s_v"))
            yield from self.dense(k2("m_z"), u, None, self.silu_to(b["m_z"], "m_z"))
            yield from self.dense(k2("r_q"), u, None, self.copy_to(b["r_q"], "r_q"))
            r_k = self.dense(k2("r_k"), u, None, self.copy_to(b["r_k"], "r_k"))
            r_v = self.token_major(k2("r_v"), u, None, self.tokens_to(b["r_v"], "r_v"))
            for product, rotated in ((r_k, "r_q"), (r_v, "r_k")):
                for i, _ in enumerate(product):
                    rotate(rotated, 2 * i)
                    yield
            yield from self.dense(k2("r_g"), u, None, self.silu_to(b["r_g"], "r_g"))
            yield "retention can start"
        filler = Filler(fill())
        filler.until("stick-breaking can start")

        conv_read = ready["xbc"]
        heads = range(SBH)
        raws = [self.scores.take(), self.scores.take(), self.turned.take(), self.turned.take()]
        works = [self.maps.take() for _ in range(3)] + [Buffer(b["stick_space"][:, 0, :])]
        keeps = [Buffer(b["cb"][:, i, :]) for i in range(2)] + [Buffer(b["stick_space"][:, 1 + i, :]) for i in range(2)]

        def stick_scores(i):
            q, k_, bank, work = b["s_q"], b["s_k"], raws[i], works[i]
            pe.wait(ready["s_q"], ready["s_k"], bank.free)
            nc.tensor.matmul(bank.tile[:, 0:T], k_[:, i, 0:P], q[:, i, :], start=True, stop=False, skip_group_check=True)
            mark = pe.done(nc.tensor.matmul(bank.tile[:, T:TRI], k_[:, i, P:T], q[:, i, P:T], start=False, stop=False,
                                            skip_group_check=True))
            act.wait(mark, work.free, conv_read)
            act.wait(act.done(nc.scalar.activation(work.tile[:, :], bank.tile[:, 0:TRI], ACT.Abs)))
            work.ready = act.done(nc.scalar.activation(work.tile[:, :], work.tile[:, :], ACT.Exp, scale=-1.0))

        def stick_logs(i):
            bank, work, keep = raws[i], works[i], keeps[i]
            act.wait(work.ready)
            dve.wait(act.done(nc.scalar.activation(work.tile[:, :], work.tile[:, :], ACT.Ln, bias=1.0)), conv_read)
            dve.wait(dve.done(nc.vector.scalar_tensor_tensor(
                work.tile[:, :], bank.tile[:, 0:TRI], 0.0, work.tile[:, :], ALU.max, ALU.add)))
            dve.wait(self.reuse.get("cb"))
            keep.ready = dve.done(nc.vector.tensor_tensor(keep.tile, work.tile[:, :], self.k("before"), ALU.mult))

        def stick_weights(i):
            bank, work, keep = raws[i], works[i], keeps[i]
            pe.wait(keep.ready)
            nc.tensor.matmul(bank.tile[:, 0:T], self.k("neg_ge"), keep.tile[:, 0:T], start=False, stop=False, skip_group_check=True)
            nc.tensor.matmul(bank.tile[:, P:T], self.k("neg_ones"), keep.tile[:, T:TRI], start=False, stop=False, skip_group_check=True)
            keep.free = m = pe.done(nc.tensor.matmul(bank.tile[:, T:TRI], self.k("neg_ge"), keep.tile[:, T:TRI],
                                                     start=False, stop=True, skip_group_check=True))
            wt = self.maps_t.take()
            dve.wait(m, wt.free)
            bank.free = m = dve.done(nc.vector.tensor_tensor(work.tile[:, :], bank.tile[:, 0:TRI], self.k("before_neg"), ALU.add))
            act.wait(m)
            work.free = wt.ready = act.done(nc.scalar.activation(wt.tile[:, :], work.tile[:, :], ACT.Exp))
            return wt

        def stick_values(i, wt):
            vbank = (self.values, self.turned, self.scores, self.turned)[i].take()
            pe.wait(vbank.free, ready["s_v"])
            m = self.weigh_values(vbank.tile[:, 0:T], b["s_v"], slice(i * P, (i + 1) * P), wt)
            act.wait(self.reuse["y"])
            vbank.free = ready["y_s"] = self.split_values(y, (slice(None), i), vbank.tile[:, 0:T], m)

        for i in heads:
            stick_scores(i)
            filler.step()
        for i in heads:
            stick_logs(i)
        filler.step()
        stick_maps = [stick_weights(i) for i in heads]
        filler.step()
        for i in heads:
            stick_values(i, stick_maps[i])
        stick_done = ready["y_s"]

        bank = self.scores.take()
        pe.wait(da_ready, bank.free)
        for t in range(TB):
            nc.tensor.matmul(bank.tile[:, t * MH:(t + 1) * MH], self.k("le"), da[:, t * MH:(t + 1) * MH], start=True, stop=True)
        m = pe.done(nc.tensor.matmul(bank.tile[:, 2 * MH:3 * MH], self.k("gt"), da[:, 0:MH], start=True, stop=True))
        dve.wait(m, self.reuse.get("cum"))
        bank.free = cum_ready = dve.done(nc.vector.tensor_copy(
            b["cum"][:, 0:3, :].rearrange("p i h -> p (i h)"), bank.tile[:, 0:3 * MH]))
        for t in range(TB):
            bank = self.turned.take()
            pe.wait(ready["xbc"], bank.free)
            for c in range(4):
                last = nc.tensor.transpose(bank.tile[:, c * P:(c + 1) * P], b["xbc"][:, c, t * P:(t + 1) * P], self.k("ident"))
            m = pe.done(last)
            act.wait(m, stick_done)
            bank.free = ready["m_v"] = act.done(nc.scalar.copy(b["m_v"][:, t, :], bank.tile[:, :]))
        for g in range(MG):
            bank = self.scores.take()
            pe.wait(bank.free)
            B_, C_ = b["xbc"][:, 4 + g, :], b["xbc"][:, 6 + g, :]
            nc.tensor.matmul(bank.tile[:, 0:T], B_[:, 0:P], C_, start=True, stop=True)
            m = pe.done(nc.tensor.matmul(bank.tile[:, T:TRI], B_[:, P:T], C_[:, P:T], start=True, stop=True))
            act.wait(m, stick_done)
            bank.free = cb_ready = act.done(nc.scalar.copy(b["cb"][:, g, :], bank.tile[:, 0:TRI]))
        state = {}

        def mamba_map(i):
            bank, work = self.scores.take(), self.maps.take()
            pe.wait(bank.free)
            for t in range(TB):
                last = nc.tensor.matmul(bank.tile[:, t * P:(t + 1) * P],
                                        da[:, t * MH + i:t * MH + i + 1].to_broadcast([P, P]), self.k("le"),
                                        start=True, stop=True)
            m = pe.done(last)
            cum = lambda j: b["cum"][:, j, i:i + 1]
            dve.wait(m, cum_ready, work.free)
            w_ = work.tile
            nc.vector.scalar_tensor_tensor(w_[:, 0:P], bank.tile[:, 0:P], cum(0), self.k("upto_min"), ALU.subtract, ALU.min)
            nc.vector.tensor_scalar(w_[:, P:T], bank.tile[:, P:T], cum(2), None, ALU.add)
            bank.free = m = dve.done(nc.vector.scalar_tensor_tensor(
                w_[:, T:TRI], bank.tile[:, P:T], cum(1), self.k("upto_min"), ALU.subtract, ALU.min))
            act.wait(m)
            m = act.done(nc.scalar.activation(w_[:, :], w_[:, :], ACT.Exp))
            wt = self.maps_t.take()
            dve.wait(m, cb_ready, wt.free)
            g = i // (MH // MG)
            nc.vector.scalar_tensor_tensor(wt.tile[:, 0:T], w_[:, 0:T], dt[:, i:i + 1], b["cb"][:, g, 0:T], ALU.mult, ALU.mult)
            wt.ready = work.free = dve.done(nc.vector.scalar_tensor_tensor(
                wt.tile[:, T:TRI], w_[:, T:TRI], dt[:, MH + i:MH + i + 1], b["cb"][:, g, T:TRI], ALU.mult, ALU.mult))
            return wt

        def mamba_values(i, wt):
            rows, c = slice(64 * (i % 2), 64 * (i % 2) + 64), i // 2
            if i % 2 == 0:
                state["bank"] = self.values.take()
                pe.wait(state["bank"].free)
            vbank = state["bank"]
            pe.wait(ready["m_v"])
            m = self.weigh_values(vbank.tile[rows, 0:T], b["m_v"], slice(i * MP, (i + 1) * MP), wt)
            if i % 2 == 1:
                dve.wait(m, ready["m_z"])
                vbank.free = m = dve.done(nc.vector.scalar_tensor_tensor(
                    y_m[:, c, :], b["xbc"][:, c, :], self.s(f"d_skip{l}", 1, c), vbank.tile[:, 0:T], ALU.mult, ALU.add))
                dve.wait(m)
                m = dve.done(nc.vector.scalar_tensor_tensor(y_m[:, c, :], y_m[:, c, :], 0.5, b["m_z"][:, c, :], ALU.mult, ALU.mult))
                ready["y_m_sq"] = self.square(b["squares"][:, c, :], y_m[:, c, :], [m, ready["y_s"]])
                ready["y_m"] = m
        def mamba(i):
            maps = [mamba_map(2 * i + j) for j in range(2)]
            yield
            for j, wt in enumerate(maps):
                mamba_values(2 * i + j, wt)
        self.pipeline([mamba(i) for i in range(MH // 2)], filler)
        m_norm = self.inverse_rms(b["squares"], 1, 4, 512, 1e-6, ready["y_m_sq"])
        next(m_norm)
        filler.until("retention can start")
        u_read = (pe.semaphore, pe.count)
        self.reuse["cum"] = self.reuse["m_z"] = self.reuse["cb"] = ready["y_m"]

        (bank,) = next(m_norm)
        dve.wait(bank.ready)
        for c in range(4):
            m = dve.done(nc.vector.scalar_tensor_tensor(
                y_m[:, c, :], y_m[:, c, :], self.s(f"ssm_norm{l}", 1, c), bank.tile[:, 0:T], ALU.mult, ALU.mult))
        bank.free = m
        act.wait(u_read)
        ready["y_m"] = self.split_values(u, (slice(None), slice(4, 8)), y_m, m)

        self.pause_mods()
        banks = [self.products.take(), self.products.take(), self.turned.take(), self.mod_banks.take()]
        place = {4: (y, 0, "y_s"), 6: (y, 2, "y_s"), 8: (u, 4, "y_m"), 10: (u, 6, "y_m"),
                 0: (u, 0, "y_r0"), 2: (u, 2, "y_r2")}

        def mix_out(pairs):
            for c in pairs:
                slot = self.weights((f"mix_out{l}", c))
                x, at_, name = place[c]
                yield from self.accumulate(slot, banks, x, at_, ready[name], c == OUT_ORDER[0],
                                           c == OUT_ORDER[-1])
                self.reuse["y"] = self.reuse["u"] = self.reuse["xbc_in"] = slot.free
                yield
        filler = Filler(mix_out(OUT_ORDER[:4]))

        def retain(i):
            q, k_ = b["r_q"], b["r_k"]
            bank, wt = self.scores.take(), self.maps_t.take()
            pe.wait(ready["r_q_rot"], ready["r_k_rot"], bank.free)
            nc.tensor.matmul(bank.tile[:, 0:T], k_[:, i, 0:P], q[:, i, :], start=True, stop=True)
            m = pe.done(nc.tensor.matmul(bank.tile[:, T:TRI], k_[:, i, P:T], q[:, i, P:T], start=True, stop=True))
            dve.wait(m, wt.free)
            bank.free = wt.ready = dve.done(nc.vector.tensor_tensor(
                wt.tile[:, :], bank.tile[:, 0:TRI], self.k("decay", i * TRI, TRI), ALU.mult))
            yield
            vbank = self.values.take()
            pe.wait(vbank.free, ready["r_v"])
            m = self.weigh_values(vbank.tile[:, 0:T], b["r_v"], slice(i * P, (i + 1) * P), wt)
            act.wait(m)
            vbank.free = m = act.done(nc.scalar.copy(y_r[:, i, :], vbank.tile[:, 0:T]))
            ready["y_r"] = m
            ready["y_r_sq"] = self.square(b["squares"][:, 4 + i, :], y_r[:, i, :], m)
        self.pipeline([retain(i) for i in range(RH)], filler)
        norm = self.inverse_rms(b["squares"][:, 4:8, :], 4, 1, RD, 1e-6, ready["y_r_sq"])
        filler.step()
        next(norm)
        filler.step()
        scales = next(norm)
        while filler.step():
            pass
        for i in range(RH):
            bank = scales[i // 2]
            dve.wait(bank.ready, ready["y_r"], ready["r_g"])
            bank.free = m = dve.done(nc.vector.scalar_tensor_tensor(
                y_r[:, i, :], y_r[:, i, :], self.s(f"ret_gn{l}", 1, i), bank.tile[:, (i % 2) * T:(i % 2 + 1) * T],
                ALU.mult, ALU.mult))
            dve.wait(m)
            m = dve.done(nc.vector.scalar_tensor_tensor(y_r[:, i, :], y_r[:, i, :], 0.5, b["r_g"][:, i, :], ALU.mult, ALU.mult))
            ready[f"y_r{i // 2 * 2}"] = ready["y_r"] = self.split_values(u, (slice(None), i), y_r[:, i, :], m)
        self.reuse["squares"] = bank.ready
        for n in ("r_q", "r_k", "r_v", "r_g", "s_q", "s_k", "s_v"):
            self.reuse[n] = ready["y_r"]

        self.run(mix_out(OUT_ORDER[4:]))
        self.add_to_h(banks)
        self.mods_pause = False


def constants():
    f = np.float32
    c = {}
    i = np.arange(P)
    c["ident"] = np.eye(P, dtype=f)
    c["ones"] = np.ones((P, P), f)
    c["swap64"] = (i[:, None] == (i[None, :] + 64) % P).astype(f)
    s16 = np.zeros((P, 32), f)
    j = np.arange(32)
    s16[64 + (j + 16) % 32, j] = 1.0
    c["swap16"] = s16

    def tri(fn):
        k = np.arange(T)
        return np.concatenate([fn(i[:, None], k[None, :P]), fn(P + i[:, None], k[None, :])], 1).astype(f)

    def tri_t(fn):
        t = np.arange(T)
        return np.concatenate([fn(i[:, None], t[None, :]), fn(P + i[:, None], t[None, P:])], 1).astype(f)
    c["dist"] = tri(lambda q, k: np.where(k <= q, q - k, 1e33))
    c["causal"] = tri(lambda q, k: np.where(k <= q, 0.0, NEG))

    def rotary(base_row, rows, freqs):
        pos = np.arange(T, dtype=f)
        ang = (pos[:, None] * freqs[None, :]).astype(f)
        cos, sin = np.cos(ang).T, np.sin(ang).T
        cc, ss = np.zeros((P, T), f), np.zeros((P, T), f)
        cc[base_row:base_row + rows] = np.concatenate([cos, cos])
        ss[base_row:base_row + rows] = np.concatenate([-sin, sin])
        return cc, ss
    fr = (f(10000.0) ** (-np.arange(0, ROPE, 2, dtype=f) / f(ROPE))).astype(f)
    c["cos32"], c["sin32"] = rotary(64, 32, fr)
    fr = (f(10000.0) ** (-np.arange(64, dtype=f) / f(64))).astype(f)
    c["cos128"], c["sin128"] = rotary(0, 128, fr)
    decay = []
    for h in range(RH):
        lg = math.log1p(-(2.0 ** (-5.0 - h)))
        decay.append(tri_t(lambda s, t: np.where(s // 64 <= t // 64, np.exp(lg * np.abs(t - s)), 0.0) * RD ** -0.5))
    c["decay"] = np.concatenate(decay, 1)
    c["before"] = tri_t(lambda s, t: s < t)
    c["before_neg"] = tri_t(lambda s, t: np.where(s < t, 0.0, NEG))
    c["upto_min"] = np.where(i[:, None] <= i[None, :], 0.0, NEG).astype(f)
    c["le"] = (i[:, None] <= i[None, :]).astype(f)
    c["gt"] = (i[:, None] > i[None, :]).astype(f)
    c["neg_ge"] = -(i[:, None] >= i[None, :]).astype(f)
    c["neg_ones"] = -np.ones((P, P), f)
    return {f"constants_{group}": np.ascontiguousarray(np.concatenate([c[n] for n, _ in sizes], 1))
            for group, sizes in CONST_SIZES.items()}


def small_parameters(a):
    col = lambda v: np.ascontiguousarray(v).reshape(-1, P).T
    every = lambda v: np.broadcast_to(np.asarray(v).reshape(1, -1), (P, np.asarray(v).size))
    parts = []
    for l in range(DEPTH):
        parts += [col(a["mla_q_norm_g"][l]), col(a["mla_kv_norm_g"][l]), col(a["diff_subln_g"][l]),
                  col(a["b_merge"][l]), col(a["ln_g"][l]), col(a["ln_b"][l]), col(a["ada_b_2"][l]),
                  col(a["norm_ffn1_2"][l]), col(a["norm_mix_2"][l]), col(a["norm_ffn2_2"][l]),
                  col(a["conv_w_2"][l].reshape(-1)), col(a["conv_b_2"][l]), col(a["ret_gn_2"][l]),
                  col(a["ssm_norm_2"][l]), col(np.repeat(a["d_skip_2"][l], MP)), every(a["dt_bias_2"][l]),
                  every(a["a_log_2"][l]), every(a["diff_lambda"][l])]
    parts += [col(a["c_2"]), col(a["final_ada_b_2"]), col(a["final_norm_2"])]
    return np.ascontiguousarray(np.concatenate(parts, 1))


DIRECT = {"w_in": "w_in", "mla_w_uq": "mla_w_uq", "mla_w_ukv": "mla_w_ukv", "w_branch_a": "w_branch_a",
          "w_branch_b": "w_branch_b", "w_branch_c": "w_branch_c", "w_merge": "w_merge", "w_out": "w_out",
          "w_ple_gate": "w_ple_gate", "w_ple": "w_ple", "ada_w": "ada_w_2", "final_ada_w": "final_ada_w_2",
          "ffn1_wg_2": "ffn1_wg_2", "ffn1_wu_2": "ffn1_wu_2", "ffn1_wd_2": "ffn1_wd_2", "w_in_2": "w_in_2",
          "w_out_2": "w_out_2", "ffn2_wg_2": "ffn2_wg_2", "ffn2_wu_2": "ffn2_wu_2", "ffn2_wd_2": "ffn2_wd_2"}


def kernel(**inputs):
    import concourse.bacc as bacc
    from concourse.bass_utils import run_bass_kernel_spmd

    given = {n: np.asarray(v) for n, v in inputs.items()}
    arrays = {n: np.ascontiguousarray(given[src]) for n, src in DIRECT.items()}
    arrays["x"] = np.ascontiguousarray(given["x"][0].T)
    arrays["p"] = np.ascontiguousarray(given["p"][:, 0].transpose(0, 2, 1))
    arrays["small"] = small_parameters(given)
    arrays.update(constants())
    nc = bacc.Bacc("TRN2", target_bir_lowering=False, num_devices=1)
    handles = {n: nc.dram_tensor(f"in_{n}", v.shape, mybir.dt.from_np(v.dtype), kind="ExternalInput").ap()
               for n, v in arrays.items()}
    out = nc.dram_tensor("out", (D, T), F32, kind="ExternalOutput").ap()
    build(nc, handles, out)
    r = run_bass_kernel_spmd(nc, [{f"in_{n}": v for n, v in arrays.items()}], core_ids=[0])
    return np.ascontiguousarray(r.results[0]["out"].T)[None]
```
